# Optimizing a Trainium2 kernel written in Bass

```python
import math
import jax, jax.numpy as jnp
from jax import lax
import numpy as np

D_MODEL = 2048
BATCH = 1
SEQ = 256
DEPTH = 1

CHUNK = 64
Q_BLOCK = 128
ATTN_WIDTH = D_MODEL // 2
SSM_WIDTH = D_MODEL - ATTN_WIDTH
N_HEADS = 8
HEAD_DIM = ATTN_WIDTH // (2 * N_HEADS)
V_DIM = 2 * HEAD_DIM
ROT_DIM = HEAD_DIM // 4
ROPE_THETA = 500000.0
SSM_GROUP = 16
N_SSM_GROUPS = SSM_WIDTH // SSM_GROUP
SSM_STATE = 64
D_FF = 256 * ((8 * D_MODEL // 3 + 255) // 256)
IN_COLS = 3 * ATTN_WIDTH + SSM_WIDTH
N_MOD = 9
EPS = 1e-6
NEG_INF = -1e30

kernel_name = "hymba_diffattn_s5_macaron_block"

def rms_norm(x, g):
    xf = x.astype(jnp.float32)
    y = xf * lax.rsqrt(jnp.mean(xf * xf, axis=-1, keepdims=True) + EPS)
    return (y * g.astype(jnp.float32)).astype(x.dtype)

def modulate(h, shift, scale):
    return h * (1 + scale[:, None, :]) + shift[:, None, :]

def swiglu(h, w1, w3, w2):
    return (jax.nn.silu(h @ w1) * (h @ w3)) @ w2

def rope_partial(x, cos, sin):
    half = ROT_DIM // 2
    x1, x2, xp = x[..., :half], x[..., half:ROT_DIM], x[..., ROT_DIM:]
    c = cos[:, :, None, None, :]
    s = sin[:, :, None, None, :]
    rot = jnp.concatenate([x1 * c - x2 * s, x1 * s + x2 * c], axis=-1).astype(x.dtype)
    return jnp.concatenate([rot, xp], axis=-1)

def diff_attention(q, k, v, chunk_id, lam, lam_init, subln_g):
    B, L = q.shape[0], q.shape[1]
    nb = L // Q_BLOCK
    qb = q.reshape(B, nb, Q_BLOCK, N_HEADS, 2, HEAD_DIM).transpose(1, 0, 2, 3, 4, 5)
    cb = chunk_id.reshape(B, nb, Q_BLOCK).transpose(1, 0, 2)
    scale = HEAD_DIM ** -0.5

    def one_block(args):
        q_blk, c_blk = args
        s = jnp.einsum('bqhcd,bkhcd->bhcqk', q_blk, k).astype(jnp.float32) * scale
        mask = chunk_id[:, None, :] <= c_blk[:, :, None]
        s = jnp.where(mask[:, None, None, :, :], s, NEG_INF)
        p = jax.nn.softmax(s, axis=-1)
        a = p[:, :, 0] - lam * p[:, :, 1]
        return jnp.einsum('bhqk,bkhe->bqhe', a.astype(v.dtype), v)

    o = lax.map(one_block, (qb, cb))
    o = o.transpose(1, 0, 2, 3, 4).reshape(B, L, N_HEADS, V_DIM)
    o = rms_norm(o, subln_g) * (1.0 - lam_init)
    return o.reshape(B, L, ATTN_WIDTH)

def s5_ssm(u, a_re, a_im, log_dt, b_re, b_im, c_re, c_im, d_skip):
    f32 = jnp.float32
    B, L = u.shape[0], u.shape[1]
    ug = u.astype(f32).reshape(B, L, N_SSM_GROUPS, SSM_GROUP)
    lam = lax.complex(jnp.minimum(a_re.astype(f32), -1e-4), a_im.astype(f32))
    dt = jnp.exp(log_dt.astype(f32))[:, None]
    lam_bar = jnp.exp(lam * dt)
    b = lax.complex(b_re.astype(f32), b_im.astype(f32))
    b_bar = ((lam_bar - 1.0) / lam)[..., None] * b
    bu = jnp.einsum('gpc,blgc->blgp', b_bar, ug.astype(jnp.complex64))
    a_elems = jnp.broadcast_to(lam_bar, bu.shape)

    def combine(e1, e2):
        a1, s1 = e1
        a2, s2 = e2
        return a2 * a1, a2 * s1 + s2

    _, states = lax.associative_scan(combine, (a_elems, bu), axis=1)
    y = (jnp.einsum('gcp,blgp->blgc', c_re.astype(f32), jnp.real(states))
         - jnp.einsum('gcp,blgp->blgc', c_im.astype(f32), jnp.imag(states)))
    y = y + d_skip.astype(f32) * ug
    return y.reshape(B, L, SSM_WIDTH).astype(u.dtype)

def setup_inputs(seed: int = 0) -> dict:
    key = jax.random.key(seed)
    ks = iter(jax.random.split(key, 40))
    f32 = jnp.float32

    def nrm(shape, scale):
        return jax.random.normal(next(ks), shape, f32) * scale

    def gain(shape):
        return 1.0 + 0.02 * jax.random.normal(next(ks), shape, f32)

    x = nrm((BATCH, SEQ, D_MODEL), 1.0)
    c = nrm((BATCH, D_MODEL), 1.0)
    offset = jax.random.randint(next(ks), (BATCH, 1), 0, 64, dtype=jnp.int32) * CHUNK
    positions = (offset + jnp.arange(SEQ, dtype=jnp.int32)[None, :]).astype(jnp.int32)

    w_ada = nrm((DEPTH, D_MODEL, N_MOD * D_MODEL), D_MODEL ** -0.5)
    b_ada = nrm((DEPTH, N_MOD * D_MODEL), 0.02)

    ffn1_norm = gain((DEPTH, D_MODEL))
    ffn1_w1 = nrm((DEPTH, D_MODEL, D_FF), D_MODEL ** -0.5)
    ffn1_w3 = nrm((DEPTH, D_MODEL, D_FF), D_MODEL ** -0.5)
    ffn1_w2 = nrm((DEPTH, D_FF, D_MODEL), D_FF ** -0.5)

    mix_norm = gain((DEPTH, D_MODEL))
    w_in = nrm((DEPTH, D_MODEL, IN_COLS), D_MODEL ** -0.5)
    q_norm = gain((DEPTH, HEAD_DIM))
    k_norm = gain((DEPTH, HEAD_DIM))
    lambda_q1 = nrm((DEPTH, HEAD_DIM), 0.1)
    lambda_k1 = nrm((DEPTH, HEAD_DIM), 0.1)
    lambda_q2 = nrm((DEPTH, HEAD_DIM), 0.1)
    lambda_k2 = nrm((DEPTH, HEAD_DIM), 0.1)
    attn_subln = gain((DEPTH, V_DIM))

    n_idx = jnp.arange(SSM_STATE, dtype=f32)
    ssm_a_re = -0.5 + nrm((DEPTH, N_SSM_GROUPS, SSM_STATE), 0.01)
    ssm_a_im = math.pi * n_idx + nrm((DEPTH, N_SSM_GROUPS, SSM_STATE), 0.01)
    ssm_log_dt = jax.random.uniform(next(ks), (DEPTH, N_SSM_GROUPS), f32,
                                    math.log(1e-3), math.log(1e-1))
    ssm_b_re = nrm((DEPTH, N_SSM_GROUPS, SSM_STATE, SSM_GROUP), (2 * SSM_GROUP) ** -0.5)
    ssm_b_im = nrm((DEPTH, N_SSM_GROUPS, SSM_STATE, SSM_GROUP), (2 * SSM_GROUP) ** -0.5)
    ssm_c_re = nrm((DEPTH, N_SSM_GROUPS, SSM_GROUP, SSM_STATE), (2 * SSM_STATE) ** -0.5)
    ssm_c_im = nrm((DEPTH, N_SSM_GROUPS, SSM_GROUP, SSM_STATE), (2 * SSM_STATE) ** -0.5)
    ssm_d = nrm((DEPTH, N_SSM_GROUPS, SSM_GROUP), 1.0)
    w_glu = nrm((DEPTH, SSM_WIDTH, SSM_WIDTH), SSM_WIDTH ** -0.5)
    b_glu = nrm((DEPTH, SSM_WIDTH), 0.02)
    ssm_out_norm = gain((DEPTH, SSM_WIDTH))
    w_out = nrm((DEPTH, D_MODEL, D_MODEL), D_MODEL ** -0.5)

    ffn2_norm = gain((DEPTH, D_MODEL))
    ffn2_w1 = nrm((DEPTH, D_MODEL, D_FF), D_MODEL ** -0.5)
    ffn2_w3 = nrm((DEPTH, D_MODEL, D_FF), D_MODEL ** -0.5)
    ffn2_w2 = nrm((DEPTH, D_FF, D_MODEL), D_FF ** -0.5)

    return {"x": x, "c": c, "positions": positions, "w_ada": w_ada, "b_ada": b_ada,
            "ffn1_norm": ffn1_norm, "ffn1_w1": ffn1_w1, "ffn1_w3": ffn1_w3, "ffn1_w2": ffn1_w2,
            "mix_norm": mix_norm, "w_in": w_in, "q_norm": q_norm, "k_norm": k_norm,
            "lambda_q1": lambda_q1, "lambda_k1": lambda_k1, "lambda_q2": lambda_q2,
            "lambda_k2": lambda_k2, "attn_subln": attn_subln,
            "ssm_a_re": ssm_a_re, "ssm_a_im": ssm_a_im, "ssm_log_dt": ssm_log_dt,
            "ssm_b_re": ssm_b_re, "ssm_b_im": ssm_b_im, "ssm_c_re": ssm_c_re,
            "ssm_c_im": ssm_c_im, "ssm_d": ssm_d, "w_glu": w_glu, "b_glu": b_glu,
            "ssm_out_norm": ssm_out_norm, "w_out": w_out,
            "ffn2_norm": ffn2_norm, "ffn2_w1": ffn2_w1, "ffn2_w3": ffn2_w3, "ffn2_w2": ffn2_w2}

def reference(x, c, positions, w_ada, b_ada, ffn1_norm, ffn1_w1, ffn1_w3, ffn1_w2,
              mix_norm, w_in, q_norm, k_norm, lambda_q1, lambda_k1, lambda_q2, lambda_k2,
              attn_subln, ssm_a_re, ssm_a_im, ssm_log_dt, ssm_b_re, ssm_b_im, ssm_c_re,
              ssm_c_im, ssm_d, w_glu, b_glu, ssm_out_norm, w_out,
              ffn2_norm, ffn2_w1, ffn2_w3, ffn2_w2):
    f32 = jnp.float32
    B, L, _ = x.shape
    chunk_id = positions // CHUNK
    inv_freq = ROPE_THETA ** (-jnp.arange(0, ROT_DIM, 2, dtype=f32) / ROT_DIM)
    ang = positions.astype(f32)[..., None] * inv_freq
    cos, sin = jnp.cos(ang), jnp.sin(ang)
    cond = jax.nn.silu(c)

    for l in range(DEPTH):
        lam_init = 0.8 - 0.6 * math.exp(-0.3 * l)
        mod = cond @ w_ada[l] + b_ada[l]
        sh1, sc1, g1, sh2, sc2, g2, sh3, sc3, g3 = jnp.split(mod, N_MOD, axis=-1)

        h = modulate(rms_norm(x, ffn1_norm[l]), sh1, sc1)
        x = x + 0.5 * g1[:, None, :] * swiglu(h, ffn1_w1[l], ffn1_w3[l], ffn1_w2[l])

        h = modulate(rms_norm(x, mix_norm[l]), sh2, sc2)
        proj = h @ w_in[l]
        q = proj[..., :ATTN_WIDTH].reshape(B, L, N_HEADS, 2, HEAD_DIM)
        k = proj[..., ATTN_WIDTH:2 * ATTN_WIDTH].reshape(B, L, N_HEADS, 2, HEAD_DIM)
        v = proj[..., 2 * ATTN_WIDTH:3 * ATTN_WIDTH].reshape(B, L, N_HEADS, V_DIM)
        u = proj[..., 3 * ATTN_WIDTH:]

        q = rope_partial(rms_norm(q, q_norm[l]), cos, sin)
        k = rope_partial(rms_norm(k, k_norm[l]), cos, sin)
        lam = (jnp.exp(jnp.sum(lambda_q1[l].astype(f32) * lambda_k1[l].astype(f32)))
               - jnp.exp(jnp.sum(lambda_q2[l].astype(f32) * lambda_k2[l].astype(f32)))
               + lam_init)
        attn_out = diff_attention(q, k, v, chunk_id, lam, lam_init, attn_subln[l])

        y = s5_ssm(u, ssm_a_re[l], ssm_a_im[l], ssm_log_dt[l], ssm_b_re[l], ssm_b_im[l],
                   ssm_c_re[l], ssm_c_im[l], ssm_d[l])
        y = jax.nn.gelu(y)
        y = y * jax.nn.sigmoid(y @ w_glu[l] + b_glu[l])
        y = rms_norm(y, ssm_out_norm[l])

        mixed = jnp.concatenate([attn_out, y], axis=-1) @ w_out[l]
        x = x + g2[:, None, :] * mixed

        h = modulate(rms_norm(x, ffn2_norm[l]), sh3, sc3)
        x = x + 0.5 * g3[:, None, :] * swiglu(h, ffn2_w1[l], ffn2_w3[l], ffn2_w2[l])
    return x


_drawn_inputs = setup_inputs


def setup_inputs(seed=0):
    import zlib

    import numpy as np

    out = dict(_drawn_inputs(seed))
    spreads = {}
    factors = {'ffn1_norm': 6.837,
     'mix_norm': 7.491,
     'q_norm': 8.0,
     'k_norm': 8.0,
     'lambda_q1': 8.0,
     'lambda_k1': 200.0,
     'lambda_q2': 8.0,
     'lambda_k2': 8.0,
     'attn_subln': 200.0,
     'ssm_a_re': 200.0,
     'ssm_b_re': 3.207,
     'ssm_b_im': 2.962,
     'ssm_c_re': 2.93,
     'ssm_c_im': 2.781,
     'b_glu': 64.0,
     'ssm_out_norm': 200.0,
     'ffn2_norm': 33.777}
    for name, (base, spread) in spreads.items():
        noise = np.random.default_rng([zlib.crc32(name.encode()), seed]).standard_normal(out[name].shape)
        drawn = base * np.exp(spread * noise) if base else spread * noise
        out[name] = __import__('jax').numpy.asarray(drawn.astype(out[name].dtype))
    for name, factor in factors.items():
        out[name] = (out[name] * factor).astype(out[name].dtype)
    return out
```

```python
from contextlib import ExitStack

import numpy as np

import concourse.bass as bass
from concourse import mybir

F32 = mybir.dt.float32
F32R = mybir.dt.float32r
I32 = mybir.dt.int32
ACT = mybir.ActivationFunctionType
ALU = mybir.AluOpType
AX = mybir.AxisListType

P = 128
D = 2048
T = 256
TT = T // P
KD = D // P
NB = 512
F = 5632
THIRDS = (4, 4, 3)
AW = 1024
SW = 1024
HEADS = 8
HD = 64
GROUPS = 64
GC = 16
ST = 64
NT = GROUPS * ST // P
EPS = 1e-6
LAM_INIT = 0.8 - 0.6
NEG = -1e30
MAGIC = 1.5 * 2.0 ** 23
MAGIC16 = 1.5 * 2.0 ** 7
TWO_PI = 2.0 * np.pi
C1 = 6.28125
C2 = float(np.float32(np.floor((TWO_PI - C1) * 2 ** 21) / 2 ** 21))
C3 = float(np.float32(TWO_PI - C1 - C2))
INV_FREQ = [float(v) for v in (np.float32(500000.0) ** (-np.arange(0, 16, 2, dtype=np.float32) / np.float32(16)))]
SIN_SCALE = float(np.nextafter(np.float32(TWO_PI), np.float32(0)))

FFN_QUADS = sum(8 * n + 4 * n for n in THIRDS)
Q_FFN1 = 0
Q_WIN = FFN_QUADS
Q_GLU = Q_WIN + 32
Q_OUT = Q_GLU + 4
Q_FFN2 = Q_OUT + 16
FFN_PAIRS = sum(n + 2 for n in THIRDS)
J_FFN1 = 0
J_WIN = FFN_PAIRS
J_GLU = J_WIN + 4
J_OUT = J_GLU + 1
J_FFN2 = J_OUT + 2
T_H1 = 0
T_FFN1 = 8
T_H2 = T_FFN1 + 2 * sum(THIRDS)
T_U = T_H2 + 8
T_QK = T_U + 4
T_A = T_QK + 8
T_AO = T_A + 16
T_YG = T_AO + 4
T_Y2 = T_YG + 4
T_H3 = T_Y2 + 4
T_FFN2 = T_H3 + 8
XA_OUT = 24
XA_FFN2 = XA_OUT + 8
SSM_RD = 2
SSM_NF = 11
SMALL_IN = 16 * 17


def hi_count(bank):
    return bank if bank < T_U else bank - (T_AO - T_U)


def build(nc, x, c, positions, w_ada, b_ada, ffn1_norm, ffn1_w1, ffn1_w3, ffn1_w2,
          mix_norm, w_in, q_norm, k_norm, lambda_q1, lambda_k1, lambda_q2, lambda_k2,
          attn_subln, ssm_a_re, ssm_a_im, ssm_log_dt, ssm_b_re, ssm_b_im, ssm_c_re,
          ssm_c_im, ssm_d, w_glu, b_glu, ssm_out_norm, w_out,
          ffn2_norm, ffn2_w1, ffn2_w3, ffn2_w2, out):
    ctx = ExitStack()
    with ctx:
        def sb(name, shape, dt=F32):
            return ctx.enter_context(nc.sbuf_tensor(name, [P] + shape, dt))

        def overlay(first, *specs):
            with ExitStack() as s:
                if first:
                    s.enter_context(nc.sbuf_tensor(f"skip_{specs[0][0]}", [P, first // 4], F32))
                return [s.enter_context(nc.sbuf_tensor(n, [P] + shape, dt)) for n, shape, dt in specs]

        def sem(name):
            return ctx.enter_context(nc.semaphore(name))

        X = sb("X", [TT, D])
        raw = sb("raw", [4, 4, NB])
        w_hi = sb("w_hi", [2, 4, NB], F32R)
        w_lo = sb("w_lo", [2, 4, NB], F32R)
        bt_re = sb("bt_re", [8, P])
        bt_im = sb("bt_im", [8, P])
        c_re_t = sb("c_re_t", [NT, 32])
        c_im_t = sb("c_im_t", [NT, 32])
        ident = sb("ident", [P])
        ones = sb("ones", [P])
        iota_t = sb("iota_t", [T])
        cols = sb("cols", [328])
        mod = sb("mod", [144])
        ssm_r = sb("ssm_r", [NT])
        psi = sb("psi", [NT])
        psi_hi = sb("psi_hi", [NT])
        psi_lo = sb("psi_lo", [NT])
        cond = sb("cond", [KD])
        h_scale = sb("h_scale", [KD])
        h_shift = sb("h_shift", [KD])
        gate_col = sb("gate_col", [KD])
        half_pi = sb("half_pi", [1])
        ssq = sb("ssq", [TT])
        rstd = sb("rstd", [TT])
        diag = sb("diag", [NB])
        small = sb("small", [64])

        qt, kt = overlay(0, ("qt", [8, T], F32), ("kt", [8, T], F32))
        h_hi = sb("h_hi", [KD, T], F32R)
        h_lo = sb("h_lo", [KD, T], F32R)

        K = 1024
        gt_hi, gt_lo, s1, g, ada, acc, gate = overlay(
            0, ("gt_hi", [16, T], F32R), ("gt_lo", [16, T], F32R), ("s1", [TT, NB], F32),
            ("g", [TT, NB], F32), ("ada", [2, 4, NB], F32), ("acc", [2, 2, NB], F32), ("gate", [D], F32))
        (xs,) = overlay(0, ("xs", [TT, D], F32))
        rows, bnat_re, bnat_im, bpad_re, bpad_im, prod1, prod2, cnat_re, cnat_im, sc = overlay(
            0, ("rows", [4, P], F32), ("bnat_re", [NT, GC], F32), ("bnat_im", [NT, GC], F32),
            ("bpad_re", [NT, 32], F32), ("bpad_im", [NT, 32], F32), ("prod1", [NT, GC], F32),
            ("prod2", [NT, GC], F32), ("cnat_re", [8, P], F32), ("cnat_im", [8, P], F32), ("sc", [16, NT], F32))
        v_tok, ao, u_tok, q_tok, k_tok, ut = overlay(
            0, ("v_tok", [TT, AW], F32), ("ao", [TT, AW], F32), ("u_tok", [TT, SW], F32),
            ("q_tok", [TT, AW], F32), ("k_tok", [TT, AW], F32), ("ut", [8, T], F32))
        (dskip,) = overlay(8 * K, ("dskip", [SW], F32))
        kp, xx, kk_, yy, nf, ab, cs, m1, m2, zz, s_sum = overlay(
            48 * K, ("kp", [T], F32), ("xx", [T], F32), ("kk_", [T], F32), ("yy", [T], F32),
            ("nf", [2, T], F32), ("ab", [T], F32), ("cs", [2, 2, T], F32), ("m1", [2, T], F32),
            ("m2", [2, T], F32), ("zz", [2, T], F32), ("s_sum", [2, 2, T], F32))
        sq, rope_t, qkn, cs_pos, posf, chunk_c, chunk_r, mask, ang = overlay(
            48 * K, ("sq", [AW], F32), ("rope_t", [4, 256], F32), ("qkn", [2, HD], F32), ("cs_pos", [2, TT, 8], F32),
            ("posf", [TT], F32), ("chunk_c", [TT], F32), ("chunk_r", [T], F32), ("mask", [TT, T], F32),
            ("ang", [4, TT, 8], F32))
        sm, pr, aw, at, posi, posr, lamv = overlay(
            61 * K, ("sm", [2, T], F32), ("pr", [2, T], F32), ("aw", [2, T], F32), ("at", [2, T], F32),
            ("posi", [TT], I32), ("posr", [T], I32), ("lamv", [4, HD], F32))
        yt_hi, yt_lo = overlay(24 * K, ("yt_hi", [8, T], F32R), ("yt_lo", [8, T], F32R))
        bglu_b, gsig = overlay(48 * K, ("bglu_b", [SW], F32), ("gsig", [TT, NB], F32))
        (ev_tmp,) = overlay(56 * K, ("ev_tmp", [2, NB], F32))

        def ps(name, n):
            return ctx.enter_context(nc.psum_tensor(name, [P, n, NB], F32))

        acc_a = ps("acc_a", 2)
        acc_b = ps("acc_b", 2)
        tr = ps("tr", 2)
        misc = ps("misc", 2)
        pairs = [acc_a, acc_b]

        raw_landed = [sem(f"raw_landed{i}") for i in range(4)]
        ada_landed = [sem(f"ada_landed{i}") for i in range(2)]
        rounded = sem("rounded")
        split = sem("split")
        quads_used = sem("quads_used")
        job_read = [sem("job_a_read"), sem("job_b_read")]
        ada_fma = sem("ada_fma")
        cols_reduced = sem("cols_reduced")
        mod_saved = sem("mod_saved")
        tr_written = sem("tr_written")
        tr_hi = sem("tr_hi")
        tr_free = sem("tr_free")
        gate_diag = sem("gate_diag")
        gate_bcast = sem("gate_bcast")
        gate_saved = sem("gate_saved")
        x_added = sem("x_added")
        small_in = sem("small_in")
        x_in = sem("x_in")
        out_done = sem("out_done")
        const_ready = sem("const_ready")
        cols_t = sem("cols_t")
        cols_saved = sem("cols_saved")
        c_saved = sem("c_saved")
        b_pad = sem("b_pad")
        dt_spread = sem("dt_spread")
        coef = sem("coef")
        ssum = sem("ssum")
        xs_ready = sem("xs_ready")
        dve_c = sem("dve_chain")
        act_c = sem("act_chain")
        pool_c = sem("pool_chain")
        cond_r = sem("cond_ready")
        gate_cols = sem("gate_cols")
        rms_in = sem("rms_in")
        rms_out = sem("rms_out")
        mix_in = sem("mix_in")
        mix2_in = sem("mix2_in")
        u_scaled = sem("u_scaled")
        nf_ready = sem("nf_ready")
        cs_ready = sem("cs_ready")
        bu_ready = sem("bu_ready")
        bu_read = sem("bu_read")
        prods = sem("prods")
        s_ready = sem("s_ready")
        y_done = sem("y_done")
        qk_ready = sem("qk_ready")
        sc_ready = sem("sc_ready")
        sc_read = sem("sc_read")
        mx_ready = sem("mx_ready")
        p_ready = sem("p_ready")
        a_ready = sem("a_ready")
        at_ready = sem("at_ready")
        o_ready = sem("o_ready")
        o_read = sem("o_read")
        ang_ready = sem("ang_ready")
        trig_ready = sem("trig_ready")
        lam_in = sem("lam_in")
        lam_ex = sem("lam_ex")
        ao_ready = sem("ao_ready")
        yg_ready = sem("yg_ready")
        ysum_ready = sem("ysum_ready")
        sig_ready = sem("sig_ready")
        y2_ready = sem("y2_ready")

        C_ARE, C_AIM, C_LDT = 0, 32, 64
        C_COND, C_N1, C_N2, C_N3, C_OUTN, C_SUBLN = 96, 112, 128, 144, 160, 168
        C_BADA = 176

        def wv(w):
            return w[0].rearrange("(k p) n -> p k n", p=P)

        ada_v, w1a, w3a, w2a = wv(w_ada), wv(ffn1_w1), wv(ffn1_w3), wv(ffn1_w2)
        w1b, w3b, w2b = wv(ffn2_w1), wv(ffn2_w3), wv(ffn2_w2)
        win_v, glu_v, wout_v = wv(w_in), wv(w_glu), wv(w_out)
        WIN_JOBS = [6, 7, 0, 1, 2, 3, 4, 5]
        x_v = x[0].rearrange("(t p) d -> p t d", p=P)
        out_v = out[0].rearrange("(t p) d -> p t d", p=P)

        def cols512(v, k, n):
            return v[:, 4 * k:4 * k + 4, bass.ds(n * NB, NB)]

        def thirds(q0, j0, t0):
            blk = 0
            for n in THIRDS:
                yield blk, n, q0, q0 + 8 * n, j0, t0
                blk, q0, j0, t0 = blk + n, q0 + 12 * n, j0 + n + 2, t0 + 2 * n

        def looped(eng, n, body):
            body(0)
            if n > 1:
                with eng.Fori(1, n) as i:
                    body(i)

        def ada_done_up(layer, t, s, i):
            if layer == 1:
                if s == 4:
                    return [(ADA_UP1[t], 2 * i)]
                if s == 0 and not isinstance(i, int):
                    return [(ADA_UP1[t] - 1, 2 * i)]
            elif t == 0 and s == 4:
                return [(ADA_UP2, i)]
            return []

        def ada_done_down(layer, t, s):
            if layer == 1 and s == 0:
                return [(ADA_UP1[t] + 2 * THIRDS[t] - 1, 0)]
            if layer == 1 and t == 0 and s in (4, 12):
                return [(ADA_DOWN1[s // 12], 0)]
            return []

        ADA_UP1 = [8, 18, 26]
        ADA_DOWN1 = [16, 17]
        ADA_UP2 = 32

        block = ctx.enter_context(nc.Block())

        @block.sync
        def _(sp):
            def load_quad(q, di, src):
                if q >= 4 or not isinstance(di, int):
                    sp.wait_ge(split, q - 3 + di)
                sp.dma_start(raw[:, q % 4], src).then_inc(raw_landed[q % 4], 16)

            def load_ada(b, db, k):
                if 4 * b + k >= 2:
                    sp.wait_ge(ada_fma, 4 * (4 * b + k) - 4 + 16 * db)
                sp.dma_start(ada[:, k % 2], cols512(ada_v, k, b + db)).then_inc(ada_landed[k % 2], 16)

            def col(src, r0, n, tile, width=P):
                sp.dma_start(rows[r0:r0 + n, tile, 0:width], src).then_inc(small_in, 16)

            col(c.rearrange("a (k p) -> (a k) p", p=P), 0, 16, 1)
            col(ssm_a_re[0].rearrange("(r g) p -> r (g p)", g=2), 0, 32, 0)
            col(ssm_a_im[0].rearrange("(r g) p -> r (g p)", g=2), 32, 32, 0)
            sp.dma_start(small[64:96, 24:26], ssm_log_dt[0].rearrange("(r g) -> r g", g=2)).then_inc(small_in, 16)
            col(ffn1_norm.rearrange("a (k p) -> (a k) p", p=P), 16, 16, 1)
            col(mix_norm.rearrange("a (k p) -> (a k) p", p=P), 32, 16, 1)
            col(ffn2_norm.rearrange("a (k p) -> (a k) p", p=P), 48, 16, 1)
            col(ssm_out_norm.rearrange("a (k p) -> (a k) p", p=P), 64, 8, 1)
            col(attn_subln, 72, 1, 1)
            ba = b_ada.rearrange("a (k p) -> (a k) p", p=P)
            col(ba[0:128], 0, 128, 2)
            col(ba[128:144], 0, 16, 3)
            for dst, src in ((bnat_re, ssm_b_re), (bnat_im, ssm_b_im)):
                bv = src[0].rearrange("(r g) p c -> (g p) r c", g=2)
                sp.dma_start(dst[:], bv).then_inc(small_in, 16)
            for dst, src in ((cnat_re, ssm_c_re), (cnat_im, ssm_c_im)):
                cv = src[0].rearrange("(j g) c p -> (g c) j p", g=8)
                for h in range(2):
                    sp.dma_start(dst[:, :, 64 * h:64 * h + 64], cv).then_inc(small_in, 16)
            sp.dma_start(X[:], x_v).then_inc(x_in, 16)
            for b in range(2):
                for k in range(4):
                    load_ada(b, 0, k)
            with sp.Fori(0, 3) as i:
                for b in range(2):
                    for k in range(4):
                        load_ada(2 + b, 2 * i, k)

            def ffn(layer, q0, j0, t0, w1, w3, w2):
                for t, (blk, n, qu, qd, _, _) in enumerate(thirds(q0, j0, t0)):
                    def up(i):
                        for s in range(8):
                            load_quad(qu + s, 8 * i, cols512((w1, w3)[s // 4], s % 4, blk + i))
                            if layer == 1:
                                load_ada(ADA_UP1[t] + s // 4, 2 * i, s % 4)
                            elif t == 0 and s < 4:
                                if s == 0 and isinstance(i, int):
                                    sp.wait_ge(x_added, XA_OUT + 8)
                                load_ada(ADA_UP2, i, s)
                    looped(sp, n, up)
                    for s in range(4 * n):
                        load_quad(qd + s, 0, cols512(w2[:, 4 * blk:4 * (blk + n)], s % n, s // n))
                        if layer == 1 and t == 0 and s // 4 in (0, 2):
                            load_ada(ADA_DOWN1[s // 8], 0, s % 4)

            ffn(1, Q_FFN1, J_FFN1, T_FFN1, w1a, w3a, w2a)
            for s in range(32):
                load_quad(Q_WIN + s, 0, cols512(win_v, s % 4, WIN_JOBS[s // 4]))
                if s == 4:
                    sp.wait_ge(tr_free, T_H2 + 8)
                    sp.dma_start(dskip[:], ssm_d.rearrange("a g c -> a (g c)").to_broadcast([P, SW]))\
                        .then_inc(mix_in, 16)
            sp.wait_ge(ysum_ready, 2)
            sp.dma_start(qkn[:, 0], q_norm.to_broadcast([P, HD])).then_inc(mix2_in, 16)
            sp.dma_start(qkn[:, 1], k_norm.to_broadcast([P, HD])).then_inc(mix2_in, 16)
            for i, v in enumerate((lambda_q1, lambda_k1, lambda_q2, lambda_k2)):
                sp.dma_start(lamv[:, i], v.to_broadcast([P, HD])).then_inc(mix2_in, 16)
            sp.dma_start(posi[:], positions.rearrange("a (t p) -> p (a t)", p=P),
                         allow_slow_non_contiguous=True).then_inc(mix2_in, 16)
            sp.dma_start(posr[:], positions.to_broadcast([P, T])).then_inc(mix2_in, 16)
            for s in range(4):
                load_quad(Q_GLU + s, 0, cols512(glu_v, s % 2, s // 2))
            sp.wait_ge(ao_ready, 1)
            sp.dma_start(bglu_b[:], b_glu.to_broadcast([P, SW])).then_inc(mix2_in, 16)
            for s in range(16):
                load_quad(Q_OUT + s, 0, cols512(wout_v, s % 4, s // 4))
            ffn(2, Q_FFN2, J_FFN2, T_FFN2, w1b, w3b, w2b)
            for n in range(4):
                sp.wait_ge(x_added, XA_FFN2 + 16 + 2 * n + 2)
                sp.dma_start(out_v[:, :, n * NB:(n + 1) * NB], X[:, :, n * NB:(n + 1) * NB]).then_inc(out_done, 16)
            sp.wait_ge(out_done, 64)

        @block.scalar
        def _(act):
            def round_quad(q, di):
                act.wait_ge(raw_landed[q % 4], 16 * (q // 4 + 1) + 4 * di)
                if q >= 2 or not isinstance(di, int):
                    act.wait_ge(quads_used, q - 1 + di)
                nc.scalar.activation(w_hi[:, q % 2], raw[:, q % 4], ACT.Copy).then_inc(rounded, 1)

            def save_mod(b, db):
                act.wait_ge(cols_reduced, b + db + 1)
                nc.scalar.activation(mod[:, bass.ds(4 * b + 4 * db, 4)], misc[:, 0, 0:4], ACT.Copy).then_inc(mod_saved, 1)

            def h_norm(base, x_ready_n):
                if x_ready_n:
                    act.wait_ge(x_added, x_ready_n)
                else:
                    act.wait_ge(x_in, 16)
                for t in range(TT):
                    nc.scalar.activation(xs[:, t], X[:, t], ACT.Square, accum_out=ssq[:, t:t + 1]).then_inc(ssum, 1)

            def hi_scaled(bank, m, hi, k0, scale, bias):
                act.wait_ge(tr_written, bank + 1)
                for kk in range(2):
                    k = 2 * m + kk
                    last = nc.scalar.activation(hi[:, k0 + k], tr[:, bank % 2, kk * T:(kk + 1) * T], ACT.Identity,
                                                bias=bias(k), scale=scale(k))
                last.then_inc(tr_hi, 1)

            def hi_plain(bank, dst):
                act.wait_ge(tr_written, bank + 1)
                nc.scalar.activation(dst, tr[:, bank % 2], ACT.Copy).then_inc(tr_hi, 1)

            def h_make(sub, bank0):
                act.wait_ge(coef, sub + 1)
                for m in range(8):
                    hi_scaled(bank0 + m, m, h_hi, 0, lambda k: h_scale[:, k:k + 1], lambda k: h_shift[:, k:k + 1])

            def hi_gt(bank, dk, b):
                act.wait_ge(tr_written, bank[0] + b + 1 + bank[1])
                nc.scalar.activation(gt_hi[:, bass.ds(4 * dk + 2 * b, 2)].rearrange("p k t -> p (k t)"),
                                     tr[:, b], ACT.Copy).then_inc(tr_hi, 1)

            def save_gate(gg, n):
                act.wait_ge(gate_bcast, gg + 1)
                nc.scalar.activation(gate[:, n * NB:(n + 1) * NB], misc[:, 1], ACT.Copy).then_inc(gate_saved, 1)

            def ffn(layer, q0, j0, t0):
                for t, (blk, n, qu, qd, jp, tb) in enumerate(thirds(q0, j0, t0)):
                    def silu(i):
                        act.wait_ge(quads_used, qu + 4 + 8 * i)
                        if jp or not isinstance(i, int):
                            act.wait_ge(job_read[1], jp + i)
                        nc.scalar.activation(s1[:], acc_a[:], ACT.Silu).then_inc(job_read[0], 1)

                    def up(i):
                        peeled = isinstance(i, int)
                        for s in range(8):
                            round_quad(qu + s, 8 * i)
                            if s == 2 and not peeled:
                                for b in range(2):
                                    hi_gt((tb, 2 * i - 2), i - 1, b)
                            if s == 5:
                                silu(i)
                            for b, db in ada_done_up(layer, t, s - 1, i):
                                save_mod(b, db)
                    looped(act, n, up)
                    for s in range(4 * n):
                        round_quad(qd + s, 0)
                        if s == 2:
                            for b in range(2):
                                hi_gt((tb, 2 * n - 2), n - 1, b)
                        for b, db in ada_done_down(layer, t, s - 1):
                            save_mod(b, db)
                        if t == 0 and s % n == 1:
                            save_gate((0, 8)[layer - 1] + s // n, s // n)

            def save_proj(j):
                act.wait_ge(quads_used, Q_WIN + 4 * j + 4)
                dst = (u_tok, q_tok, k_tok, v_tok)[j // 2][:, :, (j % 2) * NB:(j % 2 + 1) * NB]
                nc.scalar.activation(dst, pairs[j % 2][:], ACT.Copy).then_inc(job_read[j % 2], 1)

            def copy_bank(bank, dst):
                act.wait_ge(tr_written, bank + 1)
                nc.scalar.activation(dst, tr[:, bank % 2], ACT.Copy).then_inc(tr_free, 1)

            for i, (c0, n) in enumerate(((0, 96), (96, 73), (C_BADA, 128), (C_BADA + 128, 16))):
                act.wait_ge(cols_t, i + 1)
                nc.scalar.activation(cols[:, c0:c0 + n], tr[:, i % 2, 0:n], ACT.Copy).then_inc(cols_saved, 1)
                if i == 1:
                    act.wait_ge(cols_saved, 2)
                    nc.scalar.activation(cond[:], cols[:, C_COND:C_COND + 16], ACT.Silu).then_inc(cond_r, 1)
            act.wait_ge(cols_saved, 2)
            nc.scalar.activation(sc[:, 0], cols[:, C_LDT:C_LDT + 32], ACT.Exp).then_inc(act_c, 1)
            save_mod(0, 0)
            act.wait_ge(dve_c, SSM_RD)
            nc.scalar.activation(ssm_r[:], sc[:, 1], ACT.Exp).then_inc(act_c, 1)
            act.wait_ge(dve_c, SSM_NF)
            nc.scalar.activation(sc[:, 5], sc[:, 4], ACT.Abs).then_inc(act_c, 1)
            nc.scalar.activation(sc[:, 6], sc[:, 4], ACT.Sin, scale=-SIN_SCALE).then_inc(act_c, 1)
            act.wait_ge(act_c, 3)
            nc.scalar.activation(sc[:, 7], sc[:, 5], ACT.Sin, scale=-SIN_SCALE, bias=half_pi[:, 0:1])\
                .then_inc(act_c, 1)
            save_mod(1, 0)
            save_mod(2, 0)
            for i in range(8):
                act.wait_ge(cols_t, 4 + i + 1)
                dst = (bt_re, bt_im)[i // 4][:, 2 * (i % 4):2 * (i % 4) + 2].rearrange("p a b -> p (a b)")
                nc.scalar.activation(dst, tr[:, i % 2, 0:256], ACT.Copy).then_inc(cols_saved, 1)
            for b in range(3, 8):
                save_mod(b, 0)
            h_norm(0, 0)
            h_make(0, T_H1)
            ffn(1, Q_FFN1, J_FFN1, T_FFN1)
            h_norm(1, 24)
            h_make(1, T_H2)

            for s in range(32):
                round_quad(Q_WIN + s, 0)
                if s % 4 == 1 and s > 4:
                    save_proj(s // 4 - 1)
            save_proj(7)
            for m in range(4):
                copy_bank(T_U + m, ut[:, 2 * m:2 * m + 2].rearrange("p k t -> p (k t)"))
            for r in range(NT):
                act.wait_ge(nf_ready, r + 1)
                if r:
                    act.wait_ge(cs_ready, r)
                if r >= 2:
                    act.wait_ge(prods, r - 1)
                nc.scalar.activation(ab[:], nf[:, r % 2], ACT.Abs).then_inc(act_c, 1)
                nc.scalar.activation(cs[:, r % 2, 1], nf[:, r % 2], ACT.Sin, scale=-SIN_SCALE).then_inc(act_c, 1)
                act.wait_ge(act_c, 5 + 2 * r + 1)
                nc.scalar.activation(cs[:, r % 2, 0], ab[:], ACT.Sin, scale=-SIN_SCALE, bias=half_pi[:, 0:1])\
                    .then_inc(cs_ready, 1)
            base = 5 + 2 * NT
            act.wait_ge(ang_ready, 1)
            nc.scalar.activation(cs_pos[:, 1], ang[:, 0], ACT.Sin, scale=-SIN_SCALE).then_inc(act_c, 1)
            nc.scalar.activation(ang[:, 1], ang[:, 0], ACT.Abs).then_inc(act_c, 1)
            act.wait_ge(act_c, base + 2)
            nc.scalar.activation(cs_pos[:, 0], ang[:, 1], ACT.Sin, scale=-SIN_SCALE, bias=half_pi[:, 0:1])\
                .then_inc(trig_ready, 1)
            act.wait_ge(lam_in, 1)
            nc.scalar.activation(small[:, 2:4], small[:, 0:2], ACT.Exp).then_inc(lam_ex, 1)
            for m in range(8):
                copy_bank(T_QK + m, (qt, kt)[m // 4][:, 2 * (m % 4):2 * (m % 4) + 2].rearrange("p k t -> p (k t)"))
            for i in range(2 * HEADS):
                act.wait_ge(mx_ready, i + 1)
                for cc in range(2):
                    nc.scalar.activation(pr[:, cc], sm[:, cc], ACT.Exp, bias=small[:, 8 + cc:9 + cc],
                                         accum_out=small[:, 10 + cc:11 + cc]).then_inc(p_ready, 1)
                act.wait_ge(tr_written, T_A + i + 1)
                if i >= 2:
                    act.wait_ge(o_ready, i - 1)
                nc.scalar.activation(at[:, i % 2], tr[:, i % 2, 0:T], ACT.Copy).then_inc(tr_free, 1)
            for m in range(4):
                bank = T_AO + m
                act.wait_ge(tr_written, bank + 1)
                nc.scalar.activation(h_hi[:, 2 * m:2 * m + 2].rearrange("p k t -> p (k t)"), tr[:, bank % 2], ACT.Copy,
                                     scale=small[:, 16:17]).then_inc(tr_hi, 1)
            act.wait_ge(ysum_ready, 2)
            nc.scalar.activation(u_tok[:], u_tok[:], ACT.Gelu_apprx_tanh).then_inc(yg_ready, 1)
            for m in range(4):
                hi_plain(T_YG + m, yt_hi[:, 2 * m:2 * m + 2].rearrange("p k t -> p (k t)"))
            for s in range(4):
                round_quad(Q_GLU + s, 0)
            for j in range(2):
                act.wait_ge(job_read[j], J_GLU + 1)
                nc.scalar.activation(gsig[:], gsig[:], ACT.Sigmoid).then_inc(sig_ready, 1)
            act.wait_ge(y2_ready, 2)
            for t in range(TT):
                nc.scalar.activation(ao[:, t], u_tok[:, t], ACT.Square, accum_out=ssq[:, t:t + 1]).then_inc(ssum, 1)
            for m in range(4):
                hi_scaled(T_Y2 + m, m, h_hi, 8, lambda k: cols[:, C_OUTN + k:C_OUTN + k + 1],
                          lambda k: small[:, 20:21])
            for s in range(16):
                round_quad(Q_OUT + s, 0)
                if s % 4 == 1:
                    save_gate(4 + s // 4, s // 4)
            h_norm(2, XA_OUT + 8)
            h_make(2, T_H3)
            ffn(2, Q_FFN2, J_FFN2, T_FFN2)

        @block.vector
        def _(dve):
            chain = [0]
            rms = [0]
            v = nc.vector

            def link(ins):
                chain[0] += 1
                ins.then_inc(dve_c, 1)
                dve.wait_ge(dve_c, chain[0])

            def split_quad(q, di):
                dve.wait_ge(rounded, q + 1 + di)
                if q >= 2 or not isinstance(di, int):
                    dve.wait_ge(quads_used, q - 1 + di)
                v.tensor_tensor(w_lo[:, q % 2], raw[:, q % 4], w_hi[:, q % 2].bitcast(F32), ALU.subtract)\
                    .then_inc(split, 1)

            def ada_quad(b, db, k, buf, strict=False):
                dve.wait_ge(ada_landed[k % 2], 16 * (2 * b + k // 2 + 1) + 32 * db)
                if k == 0 and b >= 2:
                    dve.wait_ge(cols_reduced, b + db if strict else b - 1 + db)
                for kk in range(4):
                    n = 4 * k + kk
                    dst, w, s = acc[:, buf, n % 2], ada[:, k % 2, kk], cond[:, n:n + 1]
                    if n < 2:
                        ins = v.tensor_scalar(dst, w, s, None, ALU.mult)
                    else:
                        dve.wait_ge(ada_fma, 16 * b + 16 * db + n - 1)
                        ins = v.scalar_tensor_tensor(dst, w, s, dst, ALU.mult, ALU.add)
                    ins.then_inc(ada_fma, 1)

            def coefficients(sub, norm_c):
                dve.wait_ge(mod_saved, 12 * sub + 8)
                s0 = 48 * sub
                v.tensor_tensor(h_shift[:], mod[:, s0:s0 + 16], cols[:, C_BADA + s0:C_BADA + s0 + 16], ALU.add)
                link(v.tensor_tensor(gate_col[:], mod[:, s0 + 16:s0 + 32],
                                     cols[:, C_BADA + s0 + 16:C_BADA + s0 + 32], ALU.add))
                v.scalar_tensor_tensor(h_scale[:], gate_col[:], 1.0, cols[:, norm_c:norm_c + 16], ALU.add, ALU.mult)\
                    .then_inc(coef, 1)
                dve.wait_ge(coef, sub + 1)

            def inv_rms(ins):
                ins.then_inc(rms_in, 1)
                rms[0] += 1
                dve.wait_ge(rms_out, rms[0])

            def h_norm(ss0, dst, src):
                for t in range(TT):
                    rms[0] += 1
                    dve.wait_ge(rms_out, rms[0])
                    v.tensor_scalar(dst[:, t], src[:, t], rstd[:, t:t + 1], None, ALU.mult).then_inc(xs_ready, 1)

            def lo_scaled(bank, m, hi, lo, k0, scale, bias, tmp):
                dve.wait_ge(tr_hi, hi_count(bank) + 1)
                for kk in range(2):
                    k = 2 * m + kk
                    ins = v.tensor_scalar(tmp[:, m % 2, kk * T:(kk + 1) * T], tr[:, bank % 2, kk * T:(kk + 1) * T],
                                          scale(k), bias(k), ALU.mult, ALU.add)
                link(ins)
                v.tensor_tensor(lo[:, k0 + 2 * m:k0 + 2 * m + 2].rearrange("p k t -> p (k t)"), tmp[:, m % 2],
                                hi[:, k0 + 2 * m:k0 + 2 * m + 2].rearrange("p k t -> p (k t)").bitcast(F32),
                                ALU.subtract).then_inc(tr_free, 1)

            def lo_plain(bank, hi, lo):
                dve.wait_ge(tr_hi, hi_count(bank) + 1)
                v.tensor_tensor(lo, tr[:, bank % 2], hi.bitcast(F32), ALU.subtract).then_inc(tr_free, 1)

            def h_make(bank0):
                for m in range(8):
                    lo_scaled(bank0 + m, m, h_hi, h_lo, 0, lambda k: h_scale[:, k:k + 1],
                              lambda k: h_shift[:, k:k + 1], s1)

            def lo_gt(bank, dk, b):
                dve.wait_ge(tr_hi, hi_count(bank[0]) + b + 1 + bank[1])
                dst = bass.ds(4 * dk + 2 * b, 2)
                v.tensor_tensor(gt_lo[:, dst].rearrange("p k t -> p (k t)"), tr[:, b],
                                gt_hi[:, dst].rearrange("p k t -> p (k t)").bitcast(F32), ALU.subtract)\
                    .then_inc(tr_free, 1)

            def add_x(pair, pi, job_quads, n, gsem):
                dve.wait_ge(quads_used, job_quads)
                if gsem is not None:
                    dve.wait_ge(gate_saved, gsem)
                for t in range(TT):
                    ins = v.tensor_tensor(g[:, t], pairs[pair][:, t], gate[:, n * NB:(n + 1) * NB], ALU.mult)
                ins.then_inc(job_read[pair], 1)
                dve.wait_ge(job_read[pair], pi + 1)
                for t in range(TT):
                    xn = X[:, t, n * NB:(n + 1) * NB]
                    v.tensor_tensor(xn, xn, g[:, t], ALU.add).then_inc(x_added, 1)

            def gate_column(sub, factor):
                dve.wait_ge(mod_saved, 12 * sub + 12)
                s0 = 48 * sub + 32
                link(v.tensor_tensor(gate_col[:], mod[:, s0:s0 + 16], cols[:, C_BADA + s0:C_BADA + s0 + 16], ALU.add))
                v.tensor_scalar(gate_col[:], gate_col[:], factor, None, ALU.mult).then_inc(gate_cols, 1)

            def ffn(layer, q0, j0, t0):
                for t, (blk, n, qu, qd, jp, tb) in enumerate(thirds(q0, j0, t0)):
                    def hidden(i, m):
                        dve.wait_ge(quads_used, qu + 8 + 8 * m)
                        dve.wait_ge(job_read[0], jp + m + 1)
                        dve.wait_ge(tr_written, tb + 2 * m)
                        v.tensor_tensor(g[:], s1[:], acc_b[:], ALU.mult).then_inc(job_read[1], 1)

                    def up(i):
                        peeled = isinstance(i, int)
                        for s in range(8):
                            if s == 1 and not peeled:
                                hidden(i, i - 1)
                            split_quad(qu + s, 8 * i)
                            if s == 2 and not peeled:
                                for b in range(2):
                                    lo_gt((tb, 2 * i - 2), i - 1, b)
                            if layer == 1:
                                ada_quad(ADA_UP1[t] + s // 4, 2 * i, s % 4, s // 4)
                            elif t == 0 and s < 4:
                                ada_quad(ADA_UP2, i, s, 0, strict=not peeled)
                    looped(dve, n, up)
                    if t == 0:
                        gate_column(2 * (layer - 1), 0.5)
                    for s in range(4 * n):
                        if s == 1:
                            hidden(None, n - 1)
                        split_quad(qd + s, 0)
                        if s == 2:
                            for b in range(2):
                                lo_gt((tb, 2 * n - 2), n - 1, b)
                        if s % n == 0 and s:
                            j = s // n - 1
                            add_x(j % 2, jp + n + j // 2, qd + n * (j + 1), j,
                                  ((0, 8)[layer - 1] + j + 1) if t == 0 else None)
                        if layer == 1 and t == 0 and s // 4 in (0, 2):
                            ada_quad(ADA_DOWN1[s // 8], 0, s % 4, s // 8)
                    add_x(1, jp + n + 1, qd + 4 * n, 3, ((0, 8)[layer - 1] + 4) if t == 0 else None)

            v.memset(half_pi[:], float(np.pi / 2))
            dve.wait_ge(small_in, SMALL_IN)
            v.tensor_copy(rows[64:96, 0].rearrange("p (g s) -> p g s", g=2),
                          small[64:96, 24:26].unsqueeze(2).to_broadcast([32, 2, ST])).then_inc(dt_spread, 1)
            dve.wait_ge(cond_r, 1)

            def ssm_rates():
                dve.wait_ge(act_c, 1)
                link(v.tensor_scalar(sc[:, 2], cols[:, C_ARE:C_ARE + 32], -1e-4, None, ALU.min))
                link(v.tensor_tensor(sc[:, 1], sc[:, 2], sc[:, 0], ALU.mult))
                assert chain[0] == SSM_RD
                link(v.tensor_tensor(sc[:, 3], cols[:, C_AIM:C_AIM + 32], sc[:, 0], ALU.mult))
                link(v.tensor_scalar(sc[:, 8], sc[:, 3], float(1 / TWO_PI), MAGIC, ALU.mult, ALU.add))
                link(v.tensor_scalar(sc[:, 8], sc[:, 8], MAGIC, None, ALU.subtract))
                for cst in (C1, C2, C3):
                    link(v.scalar_tensor_tensor(sc[:, 3], sc[:, 8], -cst, sc[:, 3], ALU.mult, ALU.add))
                link(v.tensor_scalar(psi[:], sc[:, 3], float(1 / TWO_PI), None, ALU.mult))
                link(v.tensor_scalar(sc[:, 4], psi[:], -1.0, None, ALU.mult))
                link(v.tensor_scalar(sc[:, 4], sc[:, 4], 0.5, -0.5, ALU.min, ALU.max))
                assert chain[0] == SSM_NF
                link(v.tensor_scalar(psi_hi[:], psi[:], MAGIC16, None, ALU.add))
                link(v.tensor_scalar(psi_hi[:], psi_hi[:], MAGIC16, None, ALU.subtract))
                link(v.tensor_tensor(psi_lo[:], psi[:], psi_hi[:], ALU.subtract))

            def ssm_f():
                dve.wait_ge(act_c, 5)
                link(v.tensor_tensor(sc[:, 9], ssm_r[:], sc[:, 7], ALU.mult))
                link(v.tensor_scalar(sc[:, 9], sc[:, 9], 1.0, None, ALU.subtract))
                link(v.tensor_tensor(sc[:, 10], ssm_r[:], sc[:, 6], ALU.mult))
                link(v.tensor_tensor(sc[:, 11], sc[:, 2], sc[:, 2], ALU.mult))
                aim = cols[:, C_AIM:C_AIM + 32]
                link(v.tensor_tensor(sc[:, 12], aim, aim, ALU.mult))
                link(v.tensor_tensor(sc[:, 11], sc[:, 11], sc[:, 12], ALU.add))
                link(v.reciprocal(sc[:, 11], sc[:, 11]))
                link(v.tensor_tensor(sc[:, 12], sc[:, 9], sc[:, 2], ALU.mult))
                link(v.tensor_tensor(sc[:, 13], sc[:, 10], aim, ALU.mult))
                link(v.tensor_tensor(sc[:, 12], sc[:, 12], sc[:, 13], ALU.add))
                link(v.tensor_tensor(sc[:, 14], sc[:, 12], sc[:, 11], ALU.mult))
                link(v.tensor_tensor(sc[:, 12], sc[:, 10], sc[:, 2], ALU.mult))
                link(v.tensor_tensor(sc[:, 13], sc[:, 9], aim, ALU.mult))
                link(v.tensor_tensor(sc[:, 12], sc[:, 12], sc[:, 13], ALU.subtract))
                link(v.tensor_tensor(sc[:, 15], sc[:, 12], sc[:, 11], ALU.mult))

            def ssm_b():
                dve.wait_ge(small_in, SMALL_IN)
                dve.wait_ge(b_pad, 2)
                fr = sc[:, 14].unsqueeze(2).to_broadcast([P, NT, GC])
                fi = sc[:, 15].unsqueeze(2).to_broadcast([P, NT, GC])
                link(v.tensor_tensor(prod1[:], bnat_re[:], fr, ALU.mult))
                link(v.tensor_tensor(prod2[:], bnat_im[:], fi, ALU.mult))
                for h in range(2):
                    hp, hc = slice(64 * h, 64 * h + 64), slice(GC * h, GC * h + GC)
                    link(v.tensor_tensor(bpad_re[hp, :, hc], prod1[hp], prod2[hp], ALU.subtract))
                link(v.tensor_tensor(prod1[:], bnat_im[:], fr, ALU.mult))
                link(v.tensor_tensor(prod2[:], bnat_re[:], fi, ALU.mult))
                for h in range(2):
                    hp, hc = slice(64 * h, 64 * h + 64), slice(GC * h, GC * h + GC)
                    ins = v.tensor_tensor(bpad_im[hp, :, hc], prod1[hp], prod2[hp], ALU.add)
                ins.then_inc(b_pad, 1)

            def ssm_c():
                dve.wait_ge(const_ready, 2)
                for i in range(4):
                    dve.wait_ge(cols_t, 12 + i + 1)
                    dst = (c_re_t, c_im_t)[i // 2]
                    sgn = (1.0, -1.0)[i // 2]
                    src = tr[:, i % 2].rearrange("p (r g c) -> p r g c", g=2, c=GC)
                    for h in range(2):
                        hp, hc = slice(64 * h, 64 * h + 64), slice(GC * h, GC * h + GC)
                        ins = v.tensor_scalar(dst[hp, 16 * (i % 2):16 * (i % 2) + 16, hc], src[hp, :, h], sgn, None, ALU.mult)
                    ins.then_inc(c_saved, 1)


            for b in range(8):
                for k in range(4):
                    ada_quad(b, 0, k, b % 2)
                if b < 4:
                    (ssm_rates, ssm_f, ssm_b, ssm_c)[b]()
            coefficients(0, C_N1)
            h_norm(0, xs, X)
            h_make(T_H1)
            ffn(1, Q_FFN1, J_FFN1, T_FFN1)
            coefficients(1, C_N2)
            h_norm(2, xs, X)
            h_make(T_H2)
            gate_column(1, 1.0)

            for s in range(32):
                split_quad(Q_WIN + s, 0)
            for r in range(NT):
                dve.wait_ge(bu_ready, r + 1)
                dve.wait_ge(cs_ready, r + 1)
                bu = misc[:, r % 2].rearrange("p (a t) -> p a t", a=2)
                csr = cs[:, r % 2]
                if r >= 1:
                    dve.wait_ge(s_ready, 2 * r)
                v.tensor_tensor(m1[:], csr, bu, ALU.mult)
                v.tensor_tensor(m2[:, 0], csr[:, 0], bu[:, 1], ALU.mult)
                v.tensor_tensor(m2[:, 1], csr[:, 1], bu[:, 0], ALU.mult).then_inc(bu_read, 1)
                dve.wait_ge(bu_read, r + 1)
                v.tensor_tensor(m1[:, 0], m1[:, 0], m1[:, 1], ALU.add)
                link(v.tensor_tensor(m2[:, 0], m2[:, 0], m2[:, 1], ALU.subtract))
                rad = ssm_r[:, r:r + 1].to_broadcast([P, T])
                v.tensor_tensor_scan(zz[:, 0], rad, m1[:, 0], 0.0, ALU.mult, ALU.add)
                link(v.tensor_tensor_scan(zz[:, 1], rad, m2[:, 0], 0.0, ALU.mult, ALU.add))
                v.tensor_tensor(m1[:], csr, zz[:], ALU.mult)
                v.tensor_tensor(m2[:, 0], csr[:, 0], zz[:, 1], ALU.mult)
                v.tensor_tensor(m2[:, 1], csr[:, 1], zz[:, 0], ALU.mult).then_inc(prods, 1)
                if r % 16 == 15:
                    hf = r // 16
                    dve.wait_ge(y_done, r + 1)
                    dve.wait_ge(u_scaled, 1)
                    for t in range(TT):
                        dst = u_tok[:, t, hf * NB:(hf + 1) * NB]
                        ins = v.tensor_tensor(dst, tr[:, t], dst, ALU.add)
                    ins.then_inc(ysum_ready, 1)
            dve.wait_ge(mix2_in, 16 * 8)
            link(v.tensor_copy(posf[:], posi[:]))
            for t in range(TT):
                for f in range(8):
                    ins = v.tensor_scalar(ang[:, 2, t, f:f + 1], posf[:, t:t + 1], INV_FREQ[f], None, ALU.mult)
            link(ins)
            link(v.tensor_scalar(ang[:, 3], ang[:, 2], float(1 / TWO_PI), MAGIC, ALU.mult, ALU.add))
            link(v.tensor_scalar(ang[:, 3], ang[:, 3], MAGIC, None, ALU.subtract))
            for cst in (C1, C2, C3):
                link(v.scalar_tensor_tensor(ang[:, 2].rearrange("p a b -> p (a b)"),
                                            ang[:, 3].rearrange("p a b -> p (a b)"), -cst,
                                            ang[:, 2].rearrange("p a b -> p (a b)"), ALU.mult, ALU.add))
            link(v.tensor_scalar(ang[:, 0], ang[:, 2], float(-1 / TWO_PI), None, ALU.mult))
            v.tensor_scalar(ang[:, 0], ang[:, 0], 0.5, -0.5, ALU.min, ALU.max).then_inc(ang_ready, 1)
            link(v.tensor_scalar(posi[:], posi[:], 6, None, ALU.arith_shift_right))
            link(v.tensor_scalar(posr[:], posr[:], 6, None, ALU.arith_shift_right))
            v.tensor_copy(chunk_c[:], posi[:])
            link(v.tensor_copy(chunk_r[:], posr[:]))
            for t in range(TT):
                ins = v.tensor_scalar(mask[:, t], chunk_r[:], chunk_c[:, t:t + 1], NEG, ALU.is_gt, ALU.mult)
            link(ins)
            v.tensor_tensor(lamv[:, 0], lamv[:, 0], lamv[:, 1], ALU.mult)
            link(v.tensor_tensor(lamv[:, 2], lamv[:, 2], lamv[:, 3], ALU.mult))
            v.tensor_reduce(small[:, 0:1], lamv[:, 0], AX.X, ALU.add)
            v.tensor_reduce(small[:, 1:2], lamv[:, 2], AX.X, ALU.add).then_inc(lam_in, 1)
            dve.wait_ge(lam_ex, 1)
            link(v.tensor_tensor(small[:, 4:5], small[:, 3:4], small[:, 2:3], ALU.subtract))
            link(v.tensor_scalar(small[:, 4:5], small[:, 4:5], LAM_INIT, None, ALU.subtract))
            link(v.tensor_scalar(small[:, 16:17], cols[:, C_SUBLN:C_SUBLN + 1], 1.0 - LAM_INIT, None, ALU.mult))
            link(v.memset(small[:, 20:21], 0.0))
            dve.wait_ge(job_read[0], J_WIN + 4)
            dve.wait_ge(job_read[1], J_WIN + 4)
            dve.wait_ge(trig_ready, 1)
            for w, tok in ((0, q_tok), (1, k_tok)):
                for t in range(TT):
                    link(v.tensor_tensor(sq[:], tok[:, t], tok[:, t], ALU.mult))
                    ss = small[:, 32:48]
                    inv_rms(v.tensor_reduce(ss, sq[:].rearrange("p (h d) -> p h d", d=HD), AX.X, ALU.add))
                    tv = tok[:, t].rearrange("p (h d) -> p h d", d=HD)
                    link(v.tensor_tensor(tv, tv, ss.unsqueeze(2).to_broadcast([P, 16, HD]), ALU.mult))
                    link(v.tensor_tensor(tv, tv, qkn[:, w].unsqueeze(1).to_broadcast([P, 16, HD]), ALU.mult))
                    cb = cs_pos[:, 0, t].unsqueeze(1).to_broadcast([P, 16, 8])
                    sb_ = cs_pos[:, 1, t].unsqueeze(1).to_broadcast([P, 16, 8])
                    x1, x2 = tv[:, :, 0:8], tv[:, :, 8:16]
                    rt = [rope_t[:, i, 0:128].rearrange("p (h d) -> p h d", d=8) for i in range(4)]
                    v.tensor_tensor(rt[0], x1, cb, ALU.mult)
                    v.tensor_tensor(rt[1], x2, sb_, ALU.mult)
                    v.tensor_tensor(rt[2], x1, sb_, ALU.mult)
                    link(v.tensor_tensor(rt[3], x2, cb, ALU.mult))
                    v.tensor_tensor(x1, rt[0], rt[1], ALU.subtract)
                    link(v.tensor_tensor(x2, rt[2], rt[3], ALU.add))
                v.memset(small[:, 21:22], 0.0).then_inc(qk_ready, 1)
            def out_head(i):
                dve.wait_ge(o_ready, i + 1)
                v.tensor_copy(ao[:, i % 2, (i // 2) * P:(i // 2 + 1) * P], misc[:, i % 2, 0:P]).then_inc(o_read, 1)

            for i in range(2 * HEADS):
                h, t = i // 2, i % 2
                dve.wait_ge(sc_ready, i + 1)
                if i:
                    dve.wait_ge(p_ready, 2 * i)
                for cc in range(2):
                    ins = v.scalar_tensor_tensor(sm[:, cc], pairs[i % 2][:, cc, 0:T], HD ** -0.5, mask[:, t],
                                                 ALU.mult, ALU.add)
                ins.then_inc(sc_read, 1)
                dve.wait_ge(sc_read, i + 1)
                link(v.tensor_reduce(small[:, 8:10], sm[:], AX.X, ALU.max))
                v.tensor_scalar(small[:, 8:10], small[:, 8:10], -1.0, None, ALU.mult).then_inc(mx_ready, 1)
                if i >= 1:
                    out_head(i - 1)
                dve.wait_ge(p_ready, 2 * i + 2)
                link(v.reciprocal(small[:, 12:14], small[:, 10:12]))
                link(v.tensor_tensor(small[:, 13:14], small[:, 13:14], small[:, 4:5], ALU.mult))
                if i >= 2:
                    dve.wait_ge(tr_written, T_A + i - 1)
                link(v.tensor_scalar(aw[:, i % 2], pr[:, 0], small[:, 12:13], None, ALU.mult))
                v.scalar_tensor_tensor(aw[:, i % 2], pr[:, 1], small[:, 13:14], aw[:, i % 2], ALU.mult, ALU.add)\
                    .then_inc(a_ready, 1)
            out_head(2 * HEADS - 1)
            dve.wait_ge(o_read, 2 * HEADS)
            for t in range(TT):
                link(v.tensor_tensor(sq[:], ao[:, t], ao[:, t], ALU.mult))
                ss = small[:, 32:40]
                inv_rms(v.tensor_reduce(ss, sq[:].rearrange("p (h d) -> p h d", d=P), AX.X, ALU.add))
                av = ao[:, t].rearrange("p (h d) -> p h d", d=P)
                ins = v.tensor_tensor(av, av, ss.unsqueeze(2).to_broadcast([P, 8, P]), ALU.mult)
            ins.then_inc(ao_ready, 1)
            for m in range(4):
                lo_scaled(T_AO + m, m, h_hi, h_lo, 0, lambda k: small[:, 16:17], lambda k: small[:, 20:21], ev_tmp)
            for m in range(4):
                lo_plain(T_YG + m, yt_hi[:, 2 * m:2 * m + 2].rearrange("p k t -> p (k t)"),
                         yt_lo[:, 2 * m:2 * m + 2].rearrange("p k t -> p (k t)"))
            for s in range(4):
                split_quad(Q_GLU + s, 0)
            dve.wait_ge(mix2_in, 16 * 9)
            for j in range(2):
                dve.wait_ge(quads_used, Q_GLU + 2 * j + 2)
                if j:
                    dve.wait_ge(y2_ready, j)
                for t in range(TT):
                    ins = v.tensor_tensor(gsig[:, t], pairs[j][:, t], bglu_b[:, j * NB:(j + 1) * NB], ALU.add)
                ins.then_inc(job_read[j], 1)
                dve.wait_ge(sig_ready, j + 1)
                yv = u_tok[:, :, j * NB:(j + 1) * NB]
                v.tensor_tensor(yv, yv, gsig[:], ALU.mult).then_inc(y2_ready, 1)
            h_norm(4, u_tok, u_tok)
            for m in range(4):
                lo_scaled(T_Y2 + m, m, h_hi, h_lo, 8, lambda k: cols[:, C_OUTN + k:C_OUTN + k + 1],
                          lambda k: small[:, 20:21], ev_tmp)
            for s in range(16):
                split_quad(Q_OUT + s, 0)
                if s % 4 == 0 and s:
                    j = s // 4 - 1
                    add_x(j % 2, J_OUT + j // 2, Q_OUT + 4 * j + 4, j, 4 + j + 1)
            add_x(1, J_OUT + 1, Q_OUT + 16, 3, 8)
            coefficients(2, C_N3)
            h_norm(6, xs, X)
            h_make(T_H3)
            ffn(2, Q_FFN2, J_FFN2, T_FFN2)

        @block.gpsimd
        def _(pool):
            g_ = nc.gpsimd
            chain = [0]
            rms = [0]

            def link(ins):
                chain[0] += 1
                ins.then_inc(pool_c, 1)
                pool.wait_ge(pool_c, chain[0])

            def inv_rms(ready, n, dst, src, width):
                pool.wait_ge(ready, n)
                link(g_.tensor_scalar(dst, src, 1.0 / width, EPS, ALU.mult, ALU.add))
                g_.tensor_tensor(dst, dst, small[:, 48:48 + dst.shape[-1]], ALU.pow).then_inc(rms_out, 1)

            def h_norm(ss0, width):
                for t in range(TT):
                    inv_rms(ssum, ss0 + t + 1, rstd[:, t:t + 1], ssq[:, t:t + 1], width)

            def gate_groups(sub):
                pool.wait_ge(gate_cols, sub + 1)
                for n in range(4):
                    gg = 4 * sub + n
                    if gg:
                        pool.wait_ge(gate_bcast, gg)
                    for j in range(4):
                        k = 4 * n + j
                        ins = g_.tensor_scalar(diag[:, j * P:(j + 1) * P], ident[:], gate_col[:, k:k + 1], None, ALU.mult)
                    ins.then_inc(gate_diag, 1)

            g_.memset(small[:, 48:64], -0.5)
            link(g_.memset(ident[:], 0.0))
            link(g_.affine_select(out=ident[:], in_=ident[:], compare_op=ALU.not_equal, fill=1.0, base=0,
                                  pattern=[[-1, P]], channel_multiplier=1))
            g_.memset(ones[:], 1.0).then_inc(const_ready, 1)
            g_.memset(bpad_re[:], 0.0).then_inc(b_pad, 1)
            g_.memset(bpad_im[:], 0.0).then_inc(b_pad, 1)
            g_.memset(c_re_t[:], 0.0)
            link(g_.memset(c_im_t[:], 0.0))
            g_.iota(iota_t[:], pattern=[[1, T]], base=0, channel_multiplier=0,
                    allow_small_or_imprecise_dtypes=True).then_inc(const_ready, 1)
            h_norm(0, D)
            gate_groups(0)
            h_norm(2, D)
            pool.wait_ge(mix_in, 16)
            pool.wait_ge(tr_written, T_U + 4)
            for t in range(TT):
                ins = g_.tensor_tensor(u_tok[:, t], u_tok[:, t], dskip[:], ALU.mult)
            ins.then_inc(u_scaled, 1)

            def phase(r):
                if r:
                    pool.wait_ge(nf_ready, r)
                if r >= 2:
                    pool.wait_ge(cs_ready, r - 1)
                g_.tensor_scalar(kp[:], iota_t[:], psi[:, r:r + 1], MAGIC, ALU.mult, ALU.add)
                g_.tensor_scalar(xx[:], iota_t[:], psi_hi[:, r:r + 1], None, ALU.mult)
                link(g_.tensor_scalar(yy[:], iota_t[:], psi_lo[:, r:r + 1], None, ALU.mult))
                link(g_.tensor_scalar(kk_[:], kp[:], MAGIC, None, ALU.subtract))
                link(g_.tensor_tensor(nf[:, r % 2], kk_[:], xx[:], ALU.subtract))
                link(g_.tensor_tensor(nf[:, r % 2], nf[:, r % 2], yy[:], ALU.subtract))
                g_.tensor_scalar(nf[:, r % 2], nf[:, r % 2], 0.5, -0.5, ALU.min, ALU.max).then_inc(nf_ready, 1)

            phase(0)
            phase(1)
            for r in range(NT):
                pool.wait_ge(prods, r + 1)
                if r >= 2:
                    pool.wait_ge(y_done, r - 1)
                g_.tensor_tensor(s_sum[:, r % 2, 0], m1[:, 0], m1[:, 1], ALU.subtract).then_inc(s_ready, 1)
                g_.tensor_tensor(s_sum[:, r % 2, 1], m2[:, 0], m2[:, 1], ALU.add).then_inc(s_ready, 1)
                if r + 2 < NT:
                    phase(r + 2)
            for i in range(4):
                inv_rms(rms_in, i + 1, small[:, 32:48], small[:, 32:48], HD)
            for i in range(2):
                inv_rms(rms_in, 5 + i, small[:, 32:40], small[:, 32:40], P)
            h_norm(4, SW)
            gate_groups(1)
            h_norm(6, D)
            gate_groups(2)

        @block.tensor
        def _(pe):
            mm = nc.tensor.matmul

            def quad(q, di, hi, lo, k0, pair, start, stop):
                pe.wait_ge(split, q + 1 + di)
                r = q % 2
                for kk in range(4):
                    for t in range(TT):
                        st, sp_ = start and kk == 0, stop and kk == 3
                        bank = pairs[pair][:, t]
                        lh, ll = hi[:, k0 + kk, t * P:(t + 1) * P], lo[:, k0 + kk, t * P:(t + 1) * P]
                        mm(bank, lh, w_hi[:, r, kk], start=st, stop=False)
                        mm(bank, lh, w_lo[:, r, kk], start=False, stop=False)
                        last = mm(bank, ll, w_hi[:, r, kk], start=False, stop=sp_)
                last.then_inc(quads_used, 1)

            def transposes(bank, dbank, b, src):
                if isinstance(dbank, int) and bank + dbank < 2:
                    pass
                else:
                    pe.wait_ge(tr_free, bank - 1 + dbank)
                for kk in range(2):
                    for t in range(TT):
                        last = nc.tensor.transpose(tr[:, b, kk * T + t * P:kk * T + (t + 1) * P], src(kk, t), ident[:])
                last.then_inc(tr_written, 1)

            def rows_to_cols(bank0, n, tok, xs_n, srcsem):
                pe.wait_ge(srcsem, xs_n)
                for m in range(n):
                    transposes(bank0 + m, 0, (bank0 + m) % 2,
                               lambda kk, t: tok[:, t, (2 * m + kk) * P:(2 * m + kk + 1) * P])

            def reduce_ada(b, db):
                pe.wait_ge(ada_fma, 16 * b + 16 + 16 * db)
                if not (isinstance(db, int) and b + db == 0):
                    pe.wait_ge(mod_saved, b + db)
                buf = b % 2
                for j in range(4):
                    for e in range(2):
                        last = mm(misc[:, 0, j:j + 1], acc[:, buf, e, j * P:(j + 1) * P], ones[:, 0:1],
                                  start=(e == 0), stop=(e == 1))
                last.then_inc(cols_reduced, 1)

            def spread_gate(gg):
                pe.wait_ge(gate_diag, gg + 1)
                if gg:
                    pe.wait_ge(gate_saved, gg)
                mm(misc[:, 1], ones[:], diag[:], start=True, stop=True).then_inc(gate_bcast, 1)

            def ffn(layer, q0, j0, t0):
                for t, (blk, n, qu, qd, jp, tb) in enumerate(thirds(q0, j0, t0)):
                    def hidden_t(m):
                        pe.wait_ge(job_read[1], jp + m + 1)
                        for b in range(2):
                            transposes(tb + b, 2 * m, b, lambda kk, tt: g[:, tt, (2 * b + kk) * P:(2 * b + kk + 1) * P])

                    def up(i):
                        peeled = isinstance(i, int)
                        for s in range(8):
                            if s % 4 == 0 and (jp or not peeled):
                                pe.wait_ge(job_read[s // 4], jp + i)
                            if t == 0 and peeled and s < 4:
                                pe.wait_ge(tr_free, t0 - 8 + 2 * s + 2)
                            quad(qu + s, 8 * i, h_hi, h_lo, 4 * (s % 4), s // 4, s % 4 == 0, s % 4 == 3)
                            if s == 0 and not peeled:
                                hidden_t(i - 1)
                            for b, db in ada_done_up(layer, t, s, i):
                                reduce_ada(b, db)
                    looped(pe, n, up)
                    for s in range(4 * n):
                        j, k = s // n, s % n
                        if k == 0:
                            pe.wait_ge(job_read[j % 2], jp + n + j // 2)
                            if t == 0:
                                spread_gate((0, 8)[layer - 1] + j)
                        if s == n - 1:
                            pe.wait_ge(tr_free, tb + 2 * n)
                        elif s == 0:
                            pe.wait_ge(tr_free, tb + 2 * n - 2)
                        quad(qd + s, 0, gt_hi, gt_lo, 4 * k, j % 2, k == 0, k == n - 1)
                        if s == 0:
                            hidden_t(n - 1)
                        for b, db in ada_done_down(layer, t, s):
                            reduce_ada(b, db)

            pe.wait_ge(const_ready, 1)
            pe.wait_ge(small_in, SMALL_IN)
            pe.wait_ge(dt_spread, 1)
            for i, n in enumerate((96, 73, 128, 16)):
                if i >= 2:
                    pe.wait_ge(cols_saved, i - 1)
                nc.tensor.transpose(tr[:, i % 2, 0:n], rows[0:n, i], ident[0:n, 0:n]).then_inc(cols_t, 1)
            for b in range(8):
                reduce_ada(b, 0)
                if b == 2:
                    pe.wait_ge(b_pad, 3)
                    for i in range(8):
                        pe.wait_ge(cols_saved, 4 + i - 1)
                        src = (bpad_re, bpad_im)[i // 4]
                        for kk in range(2):
                            m = 2 * (i % 4) + kk
                            last = nc.tensor.transpose(tr[:, i % 2, kk * P:(kk + 1) * P],
                                                       src[:, 4 * m:4 * m + 4].rearrange("p a b -> p (a b)"), ident[:])
                        last.then_inc(cols_t, 1)
                if b == 3:
                    for i in range(4):
                        if i < 2:
                            pe.wait_ge(cols_saved, 12)
                        else:
                            pe.wait_ge(c_saved, i - 1)
                        for kk in range(4):
                            last = nc.tensor.transpose(tr[:, i % 2, kk * P:(kk + 1) * P],
                                                       (cnat_re, cnat_im)[i // 2][:, 4 * (i % 2) + kk], ident[:])
                        last.then_inc(cols_t, 1)
            pe.wait_ge(c_saved, 4)
            rows_to_cols(T_H1, 8, xs, 2, xs_ready)
            ffn(1, Q_FFN1, J_FFN1, T_FFN1)
            rows_to_cols(T_H2, 8, xs, 4, xs_ready)
            for s in range(32):
                j, k = s // 4, s % 4
                if k == 0:
                    pe.wait_ge(job_read[j % 2], J_WIN + j // 2)
                if j == 0:
                    pe.wait_ge(tr_free, T_H2 + 2 * k + 2)
                quad(Q_WIN + s, 0, h_hi, h_lo, 4 * k, j % 2, k == 0, k == 3)
            rows_to_cols(T_U, 4, u_tok, J_WIN + 1, job_read[1])

            def drive(r):
                if r >= 2:
                    pe.wait_ge(bu_read, r - 1)
                p0, k = 32 * (r % 4), r // 4
                for e, bt in enumerate((bt_re, bt_im)):
                    last = mm(misc[:, r % 2, e * T:(e + 1) * T], bt[p0:p0 + 32, k], ut[p0:p0 + 32, k],
                              start=True, stop=True, tile_position=(p0, 0))
                last.then_inc(bu_ready, 1)

            pe.wait_ge(tr_free, T_U + 4)
            drive(0)
            for r in range(NT):
                if r + 1 < NT:
                    drive(r + 1)
                if r == 16:
                    pe.wait_ge(ysum_ready, 1)
                pe.wait_ge(s_ready, 2 * r + 2)
                for t in range(TT):
                    for e, ct in enumerate((c_re_t, c_im_t)):
                        last = mm(tr[:, t, 32 * (r % 16):32 * (r % 16) + 32], s_sum[:, r % 2, e, t * P:(t + 1) * P],
                                  ct[:, r], start=(e == 0), stop=(e == 1))
                last.then_inc(y_done, 1)
            pe.wait_ge(ysum_ready, 2)
            rows_to_cols(T_QK, 4, q_tok, 1, qk_ready)
            rows_to_cols(T_QK + 4, 4, k_tok, 2, qk_ready)
            pe.wait_ge(tr_free, T_QK + 8)

            def scores(i):
                h, t = i // 2, i % 2
                if i >= 2:
                    pe.wait_ge(sc_read, i - 1)
                for cc in range(2):
                    c0 = HD * cc
                    last = mm(pairs[i % 2][:, cc, 0:T], qt[c0:c0 + HD, h, t * P:(t + 1) * P], kt[c0:c0 + HD, h],
                              start=True, stop=True, tile_position=(c0, 0))
                last.then_inc(sc_ready, 1)

            scores(0)
            for i in range(2 * HEADS):
                if i + 1 < 2 * HEADS:
                    scores(i + 1)
                h, b = i // 2, (T_A + i) % 2
                pe.wait_ge(a_ready, i + 1)
                pe.wait_ge(tr_free, T_A + i - 1)
                for kk in range(2):
                    last = nc.tensor.transpose(tr[:, b, kk * P:(kk + 1) * P], aw[:, i % 2, kk * P:(kk + 1) * P], ident[:])
                last.then_inc(tr_written, 1)
                pe.wait_ge(tr_free, T_A + i + 1)
                if i >= 2:
                    pe.wait_ge(o_read, i - 1)
                for kk in range(2):
                    last = mm(misc[:, i % 2, 0:P], at[:, i % 2, kk * P:(kk + 1) * P],
                              v_tok[:, kk, h * P:(h + 1) * P], start=(kk == 0), stop=(kk == 1))
                last.then_inc(o_ready, 1)
            rows_to_cols(T_AO, 4, ao, 1, ao_ready)
            rows_to_cols(T_YG, 4, u_tok, 1, yg_ready)
            for s in range(4):
                j, k = s // 2, s % 2
                if k == 0:
                    pe.wait_ge(job_read[j], J_GLU)
                if j == 0:
                    pe.wait_ge(tr_free, T_YG + 2 * k + 2)
                quad(Q_GLU + s, 0, yt_hi, yt_lo, 4 * k, j, k == 0, k == 1)
            rows_to_cols(T_Y2, 4, u_tok, 6, xs_ready)
            for s in range(16):
                j, k = s // 4, s % 4
                if k == 0:
                    pe.wait_ge(job_read[j % 2], J_OUT + j // 2)
                    spread_gate(4 + j)
                if j == 0 and k >= 2:
                    pe.wait_ge(tr_free, T_Y2 + 2 * (k - 2) + 2)
                quad(Q_OUT + s, 0, h_hi, h_lo, 4 * k, j % 2, k == 0, k == 3)
            rows_to_cols(T_H3, 8, xs, 8, xs_ready)
            ffn(2, Q_FFN2, J_FFN2, T_FFN2)


_INS = ["x", "c", "positions", "w_ada", "b_ada", "ffn1_norm", "ffn1_w1", "ffn1_w3", "ffn1_w2", "mix_norm", "w_in",
        "q_norm", "k_norm", "lambda_q1", "lambda_k1", "lambda_q2", "lambda_k2", "attn_subln", "ssm_a_re", "ssm_a_im",
        "ssm_log_dt", "ssm_b_re", "ssm_b_im", "ssm_c_re", "ssm_c_im", "ssm_d", "w_glu", "b_glu", "ssm_out_norm",
        "w_out", "ffn2_norm", "ffn2_w1", "ffn2_w3", "ffn2_w2"]


def kernel(**inputs):
    import numpy as _np
    import concourse.bacc as _bacc
    from concourse import mybir as _mybir
    from concourse.bass_utils import run_bass_kernel_spmd as _run

    nc = _bacc.Bacc("TRN2", target_bir_lowering=False, num_devices=1)
    arrays, args = {}, []
    for name in _INS:
        a = _np.ascontiguousarray(inputs[name])
        arrays[f"in_{name}"] = a
        args.append(nc.dram_tensor(f"in_{name}", a.shape, _mybir.dt.from_np(a.dtype), kind="ExternalInput").ap())
    args.append(nc.dram_tensor("out_x", (1, T, D), _mybir.dt.float32, kind="ExternalOutput").ap())
    build(nc, *args)
    r = _run(nc, [arrays], core_ids=[0])
    return r.results[0]["out_x"]
```

```python
from contextlib import ExitStack

import numpy as np

import concourse.bass as bass
from concourse import mybir

F32 = mybir.dt.float32
F32R = mybir.dt.float32r
I32 = mybir.dt.int32
ACT = mybir.ActivationFunctionType
ALU = mybir.AluOpType
AX = mybir.AxisListType

P = 128
D = 2048
T = 256
TT = T // P
KD = D // P
NB = 512
F = 5632
THIRDS = (4, 4, 3)
AW = 1024
SW = 1024
HEADS = 8
HD = 64
ROT = 16
GROUPS = 64
GC = 16
ST = 64
NT = GROUPS * ST // P
EPS = 1e-6
LAM_INIT = 0.8 - 0.6
NEG = -1e30
MAGIC = 1.5 * 2.0 ** 23
MAGIC16 = 1.5 * 2.0 ** 7
TWO_PI = 2.0 * np.pi
C1 = 6.28125
C2 = float(np.float32(np.floor((TWO_PI - C1) * 2 ** 21) / 2 ** 21))
C3 = float(np.float32(TWO_PI - C1 - C2))
INV_FREQ = [float(v) for v in (np.float32(500000.0) ** (-np.arange(0, 16, 2, dtype=np.float32) / np.float32(16)))]
SIN_SCALE = float(np.nextafter(np.float32(TWO_PI), np.float32(0)))

FFN_QUADS = sum(8 * n + 4 * n for n in THIRDS)
Q_FFN1 = 0
Q_WIN = FFN_QUADS
Q_GLU = Q_WIN + 32
Q_OUT = Q_GLU + 4
Q_FFN2 = Q_OUT + 16
FFN_PAIRS = sum(n + 2 for n in THIRDS)
J_FFN1 = 0
J_WIN = FFN_PAIRS
J_GLU = J_WIN + 4
J_OUT = J_GLU + 1
J_FFN2 = J_OUT + 4
T_H1 = 0
T_FFN1 = 8
T_H2 = T_FFN1 + 2 * sum(THIRDS)
T_U = T_H2 + 8
T_YG = T_U + 4
T_QK = T_YG + 4
T_A = T_QK + 8
A_FIRST = 4
T_Y2 = T_A + A_FIRST
T_A2 = T_Y2 + 4
T_AO = T_A2 + 2 * HEADS - A_FIRST
T_H3 = T_AO + 4
T_FFN2 = T_H3 + 8
FIRST_STEP = 10
XA_OUT = 24
XA_FFN2 = XA_OUT + 16
SSM_RD = 2
SSM_NF = 11
SMALL_IN = 16 * 17


def hi_count(bank):
    plain = ((T_U, 4), (T_QK, 8), (T_A, A_FIRST), (T_A2, 2 * HEADS - A_FIRST))
    return bank - sum(n for start, n in plain if start < bank)


def a_bank(i):
    return T_A + i if i < A_FIRST else T_A2 + i - A_FIRST


def build(nc, x, c, positions, w_ada, b_ada, ffn1_norm, ffn1_w1, ffn1_w3, ffn1_w2,
          mix_norm, w_in, q_norm, k_norm, lambda_q1, lambda_k1, lambda_q2, lambda_k2,
          attn_subln, ssm_a_re, ssm_a_im, ssm_log_dt, ssm_b_re, ssm_b_im, ssm_c_re,
          ssm_c_im, ssm_d, w_glu, b_glu, ssm_out_norm, w_out,
          ffn2_norm, ffn2_w1, ffn2_w3, ffn2_w2, out):
    ctx = ExitStack()
    with ctx:
        def sb(name, shape, dt=F32):
            return ctx.enter_context(nc.sbuf_tensor(name, [P] + shape, dt))

        def overlay(first, *specs):
            with ExitStack() as s:
                if first:
                    s.enter_context(nc.sbuf_tensor(f"skip_{specs[0][0]}", [P, first // 4], F32))
                return [s.enter_context(nc.sbuf_tensor(n, [P] + shape, dt)) for n, shape, dt in specs]

        def sem(name):
            return ctx.enter_context(nc.semaphore(name))

        X = sb("X", [TT, D])
        raw = sb("raw", [4, 4, NB])
        w_hi = sb("w_hi", [2, 4, NB], F32R)
        w_lo = sb("w_lo", [2, 4, NB], F32R)
        bt_re = sb("bt_re", [8, P])
        bt_im = sb("bt_im", [8, P])
        c_re_t = sb("c_re_t", [NT, 32])
        c_im_t = sb("c_im_t", [NT, 32])
        ident = sb("ident", [P])
        ones = sb("ones", [P])
        iota_t = sb("iota_t", [T])
        cols = sb("cols", [328])
        mod = sb("mod", [144])
        ssm_r = sb("ssm_r", [NT])
        psi = sb("psi", [NT])
        psi_hi = sb("psi_hi", [NT])
        psi_lo = sb("psi_lo", [NT])
        cond = sb("cond", [KD])
        h_scale = sb("h_scale", [KD])
        h_shift = sb("h_shift", [KD])
        gate_col = sb("gate_col", [KD])
        half_pi = sb("half_pi", [1])
        magic = sb("magic", [2])
        ssq = sb("ssq", [TT])
        rstd = sb("rstd", [TT])
        diag = sb("diag", [NB])
        small = sb("small", [112])
        rope_g = sb("rope_g", [2, 4, TT, 8])
        gain_col = sb("gain_col", [2])
        cs_pos = sb("cs_pos", [2, TT, 8])
        early_mask = diag[:].rearrange("p (t k) -> p t k", t=TT)

        (qt,) = overlay(0, ("qt", [8, T], F32))
        (qk_ss,) = overlay(8 * 1024, ("qk_ss", [64], F32))
        (kt,) = overlay(16 * 1024, ("kt", [8, T], F32))
        h_hi = sb("h_hi", [KD, T], F32R)
        h_lo = sb("h_lo", [KD, T], F32R)

        K = 1024
        gt_hi, gt_lo, s1, g, ada, acc, gate = overlay(
            0, ("gt_hi", [16, T], F32R), ("gt_lo", [16, T], F32R), ("s1", [TT, NB], F32),
            ("g", [TT, NB], F32), ("ada", [2, 4, NB], F32), ("acc", [2, 2, NB], F32), ("gate", [D], F32))
        (xs,) = overlay(0, ("xs", [TT, D], F32))
        rows, bnat_re, bnat_im, bpad_re, bpad_im, prod1, prod2, cnat_re, cnat_im, sc = overlay(
            0, ("rows", [4, P], F32), ("bnat_re", [NT, GC], F32), ("bnat_im", [NT, GC], F32),
            ("bpad_re", [NT, 32], F32), ("bpad_im", [NT, 32], F32), ("prod1", [NT, GC], F32),
            ("prod2", [NT, GC], F32), ("cnat_re", [8, P], F32), ("cnat_im", [8, P], F32), ("sc", [16, NT], F32))
        v_tok, ao, u_tok, q_tok, k_tok, ut = overlay(
            0, ("v_tok", [TT, AW], F32), ("ao", [TT, AW], F32), ("u_tok", [TT, SW], F32),
            ("q_tok", [TT, AW], F32), ("k_tok", [TT, AW], F32), ("ut", [8, T], F32))
        dskip, p1, p2 = overlay(8 * K, ("dskip", [SW], F32), ("p1", [2, T], F32), ("p2", [2, T], F32))
        late_cs, late_zin = overlay(8 * K, ("late_cs", [2, T], F32), ("late_zin", [2, T], F32))
        kp0, xx0, yy0, nf, ab, cs3, zin0, zz, back = overlay(
            48 * K, ("kp0", [T], F32), ("xx0", [T], F32), ("yy0", [T], F32),
            ("nf", [2, T], F32), ("ab", [T], F32), ("cs3", [3, 2, T], F32), ("zin0", [2, T], F32),
            ("zz", [2, T], F32), ("back", [2, 2, 2, T], F32))
        posi, posr, lamv, posf, chunk_c, chunk_r, ang, qkn = overlay(
            12 * K, ("posi", [TT], I32), ("posr", [T], I32), ("lamv", [4, HD], F32), ("posf", [TT], F32),
            ("chunk_c", [TT], F32), ("chunk_r", [T], F32), ("ang", [4, TT, 8], F32), ("qkn", [2, HD], F32))
        (yy1,) = overlay(2 * K, ("yy1", [T], F32))
        kp1, xx1 = overlay(6 * K, ("kp1", [T], F32), ("xx1", [T], F32))
        parts = [(kp0, xx0, yy0), (kp1, xx1, yy1)]
        cs = [cs3[:, 0], cs3[:, 1], cs3[:, 2], late_cs[:]]
        zin = [zin0[:], late_zin[:]]
        (sq,) = overlay(8 * K, ("sq", [TT, AW], F32))
        (yt_hi,) = overlay(40 * K, ("yt_hi", [8, T], F32R))
        (yt_lo,) = overlay(48 * K, ("yt_lo", [8, T], F32R))
        (y_sq,) = overlay(40 * K, ("y_sq", [TT, SW], F32))
        ev_tmp, gsig0, mask, rope_t, bglu_b = overlay(
            48 * K, ("ev_tmp", [2, NB], F32), ("gsig0", [TT, NB], F32), ("mask", [TT, T], F32),
            ("rope_t", [4, P], F32), ("bglu_b", [SW], F32))
        gsig = [gsig0, g]
        sm, pr, aw, at = overlay(
            24 * K, ("sm", [2, 2, T], F32), ("pr", [2, 2, T], F32), ("aw", [2, T], F32), ("at", [2, T], F32))
        (o_sq,) = overlay(58 * K, ("o_sq", [2, P], F32))

        def ps(name, n):
            return ctx.enter_context(nc.psum_tensor(name, [P, n, NB], F32))

        acc_a = ps("acc_a", 2)
        acc_b = ps("acc_b", 2)
        tr = ps("tr", 2)
        misc = ps("misc", 2)
        pairs = [acc_a, acc_b]

        raw_landed = [sem(f"raw_landed{i}") for i in range(4)]
        ada_landed = [sem(f"ada_landed{i}") for i in range(2)]
        rounded = sem("rounded")
        split = sem("split")
        quads_used = sem("quads_used")
        job_read = [sem("job_a_read"), sem("job_b_read")]
        ada_fma = sem("ada_fma")
        cols_reduced = sem("cols_reduced")
        mod_saved = sem("mod_saved")
        tr_written = sem("tr_written")
        tr_hi = sem("tr_hi")
        tr_free = sem("tr_free")
        gate_diag = sem("gate_diag")
        gate_bcast = sem("gate_bcast")
        gate_saved = sem("gate_saved")
        x_added = sem("x_added")
        small_in = sem("small_in")
        x_in = sem("x_in")
        out_done = sem("out_done")
        const_ready = sem("const_ready")
        cols_t = sem("cols_t")
        cols_saved = sem("cols_saved")
        c_saved = sem("c_saved")
        b_pad = sem("b_pad")
        dt_spread = sem("dt_spread")
        coef = sem("coef")
        ssum = sem("ssum")
        xs_ready = sem("xs_ready")
        dve_c = sem("dve_chain")
        act_c = sem("act_chain")
        pool_c = sem("pool_chain")
        cond_r = sem("cond_ready")
        gate_cols = sem("gate_cols")
        rms_in = sem("rms_in")
        rms_out = sem("rms_out")
        mix_in = sem("mix_in")
        mix2_in = sem("mix2_in")
        u_scaled = sem("u_scaled")
        parts_ready = sem("parts_ready")
        nf_ready = sem("nf_ready")
        cs_ready = sem("cs_ready")
        bu_ready = sem("bu_ready")
        bu_read = sem("bu_read")
        zin_ready = sem("zin_ready")
        scanned = sem("scanned")
        prods = sem("prods")
        s_ready = sem("s_ready")
        y_done = sem("y_done")
        gain_ones = sem("gain_ones")
        mask_moved = sem("mask_moved")
        sq_ready = sem("sq_ready")
        sq_read = sem("sq_read")
        qk_ready = sem("qk_ready")
        sc_half = sem("sc_half")
        sc_ready = sem("sc_ready")
        sc_read = sem("sc_read")
        mx_ready = sem("mx_ready")
        p_ready = sem("p_ready")
        a_ready = sem("a_ready")
        at_ready = sem("at_ready")
        o_ready = sem("o_ready")
        o_read = sem("o_read")
        ang_ready = sem("ang_ready")
        trig_ready = sem("trig_ready")
        lam_in = sem("lam_in")
        lam_ex = sem("lam_ex")
        ao_ready = sem("ao_ready")
        yg_ready = sem("yg_ready")
        ysum_ready = sem("ysum_ready")
        sig_ready = sem("sig_ready")
        y2_ready = sem("y2_ready")

        C_ARE, C_AIM, C_LDT = 0, 32, 64
        C_COND, C_N1, C_N2, C_N3, C_OUTN, C_SUBLN = 96, 112, 128, 144, 160, 168
        C_BADA = 176

        def wv(w):
            return w[0].rearrange("(k p) n -> p k n", p=P)

        ada_v, w1a, w3a, w2a = wv(w_ada), wv(ffn1_w1), wv(ffn1_w3), wv(ffn1_w2)
        w1b, w3b, w2b = wv(ffn2_w1), wv(ffn2_w3), wv(ffn2_w2)
        win_v, glu_v, wout_v = wv(w_in), wv(w_glu), wv(w_out)
        WIN_JOBS = [6, 7, 0, 1, 2, 3, 4, 5]
        x_v = x[0].rearrange("(t p) d -> p t d", p=P)
        out_v = out[0].rearrange("(t p) d -> p t d", p=P)

        def cols512(v, k, n):
            return v[:, 4 * k:4 * k + 4, bass.ds(n * NB, NB)]

        def thirds(q0, j0, t0):
            blk = 0
            for n in THIRDS:
                yield blk, n, q0, q0 + 8 * n, j0, t0
                blk, q0, j0, t0 = blk + n, q0 + 12 * n, j0 + n + 2, t0 + 2 * n

        def looped(eng, n, body):
            body(0)
            if n > 1:
                with eng.Fori(1, n) as i:
                    body(i)

        def ada_done_up(layer, t, s, i):
            if layer == 1:
                if s == 4:
                    return [(ADA_UP1[t], 2 * i)]
                if s == 0 and not isinstance(i, int):
                    return [(ADA_UP1[t] - 1, 2 * i)]
            elif t == 0 and s == 4:
                return [(ADA_UP2, i)]
            return []

        def ada_done_down(layer, t, s):
            if layer == 1 and s == 0:
                return [(ADA_UP1[t] + 2 * THIRDS[t] - 1, 0)]
            if layer == 1 and t == 0 and s in (4, 12):
                return [(ADA_DOWN1[s // 12], 0)]
            return []

        ADA_UP1 = [8, 18, 26]
        ADA_DOWN1 = [16, 17]
        ADA_UP2 = 32

        def attention_steps(s):
            return [A_FIRST + 2 * s, A_FIRST + 2 * s + 1] if A_FIRST + 2 * s < 2 * HEADS else []

        def stat(i):
            return small[:, 96 + 8 * (i % 2):104 + 8 * (i % 2)]

        def tile_steps(s):
            if s < FIRST_STEP:
                return []
            return range((s - FIRST_STEP) * NT // (32 - FIRST_STEP), (s + 1 - FIRST_STEP) * NT // (32 - FIRST_STEP))

        block = ctx.enter_context(nc.Block())

        @block.sync
        def _(sp):
            def load_quad(q, di, src):
                if q >= 4 or not isinstance(di, int):
                    sp.wait_ge(split, q - 3 + di)
                sp.dma_start(raw[:, q % 4], src).then_inc(raw_landed[q % 4], 16)

            def load_ada(b, db, k):
                if 4 * b + k >= 2:
                    sp.wait_ge(ada_fma, 4 * (4 * b + k) - 4 + 16 * db)
                sp.dma_start(ada[:, k % 2], cols512(ada_v, k, b + db)).then_inc(ada_landed[k % 2], 16)

            def col(src, r0, n, tile, width=P):
                sp.dma_start(rows[r0:r0 + n, tile, 0:width], src).then_inc(small_in, 16)

            col(c.rearrange("a (k p) -> (a k) p", p=P), 0, 16, 1)
            col(ssm_a_re[0].rearrange("(r g) p -> r (g p)", g=2), 0, 32, 0)
            col(ssm_a_im[0].rearrange("(r g) p -> r (g p)", g=2), 32, 32, 0)
            sp.dma_start(small[64:96, 24:26], ssm_log_dt[0].rearrange("(r g) -> r g", g=2)).then_inc(small_in, 16)
            col(ffn1_norm.rearrange("a (k p) -> (a k) p", p=P), 16, 16, 1)
            col(mix_norm.rearrange("a (k p) -> (a k) p", p=P), 32, 16, 1)
            col(ffn2_norm.rearrange("a (k p) -> (a k) p", p=P), 48, 16, 1)
            col(ssm_out_norm.rearrange("a (k p) -> (a k) p", p=P), 64, 8, 1)
            col(attn_subln, 72, 1, 1)
            ba = b_ada.rearrange("a (k p) -> (a k) p", p=P)
            col(ba[0:128], 0, 128, 2)
            col(ba[128:144], 0, 16, 3)
            for dst, src in ((bnat_re, ssm_b_re), (bnat_im, ssm_b_im)):
                bv = src[0].rearrange("(r g) p c -> (g p) r c", g=2)
                sp.dma_start(dst[:], bv).then_inc(small_in, 16)
            for dst, src in ((cnat_re, ssm_c_re), (cnat_im, ssm_c_im)):
                cv = src[0].rearrange("(j g) c p -> (g c) j p", g=8)
                for h in range(2):
                    sp.dma_start(dst[:, :, 64 * h:64 * h + 64], cv).then_inc(small_in, 16)
            sp.dma_start(X[:], x_v).then_inc(x_in, 16)
            for b in range(2):
                for k in range(4):
                    load_ada(b, 0, k)
            with sp.Fori(0, 3) as i:
                for b in range(2):
                    for k in range(4):
                        load_ada(2 + b, 2 * i, k)

            def ffn(layer, q0, j0, t0, w1, w3, w2):
                for t, (blk, n, qu, qd, _, _) in enumerate(thirds(q0, j0, t0)):
                    def up(i):
                        for s in range(8):
                            load_quad(qu + s, 8 * i, cols512((w1, w3)[s // 4], s % 4, blk + i))
                            if layer == 1:
                                load_ada(ADA_UP1[t] + s // 4, 2 * i, s % 4)
                            elif t == 0 and s < 4:
                                if s == 0 and isinstance(i, int):
                                    sp.wait_ge(x_added, XA_FFN2)
                                load_ada(ADA_UP2, i, s)
                    looped(sp, n, up)
                    for s in range(4 * n):
                        load_quad(qd + s, 0, cols512(w2[:, 4 * blk:4 * (blk + n)], s % n, s // n))
                        if layer == 1 and t == 0 and s // 4 in (0, 2):
                            load_ada(ADA_DOWN1[s // 8], 0, s % 4)

            ffn(1, Q_FFN1, J_FFN1, T_FFN1, w1a, w3a, w2a)
            for s in range(32):
                load_quad(Q_WIN + s, 0, cols512(win_v, s % 4, WIN_JOBS[s // 4]))
                if s == 4:
                    sp.wait_ge(tr_free, T_H2 + 8)
                    sp.dma_start(dskip[:], ssm_d.rearrange("a g c -> a (g c)").to_broadcast([P, SW]))\
                        .then_inc(mix_in, 16)
                    sp.dma_start(qkn[:, 0], q_norm.to_broadcast([P, HD])).then_inc(mix2_in, 16)
                    sp.dma_start(qkn[:, 1], k_norm.to_broadcast([P, HD])).then_inc(mix2_in, 16)
                    sp.wait_ge(gain_ones, 1)
                    for w, gain in enumerate((q_norm, k_norm)):
                        for p0 in (ROT, HD + ROT):
                            sp.dma_start(gain_col[p0:p0 + HD - ROT, w:w + 1],
                                         gain[:, ROT:HD].rearrange("a d -> d a")).then_inc(mix2_in, 16)
                    for i, v in enumerate((lambda_q1, lambda_k1, lambda_q2, lambda_k2)):
                        sp.dma_start(lamv[:, i], v.to_broadcast([P, HD])).then_inc(mix2_in, 16)
                    sp.dma_start(posi[:], positions.rearrange("a (t p) -> p (a t)", p=P),
                                 allow_slow_non_contiguous=True).then_inc(mix2_in, 16)
                    sp.dma_start(posr[:], positions.to_broadcast([P, T])).then_inc(mix2_in, 16)
            for s in range(4):
                load_quad(Q_GLU + s, 0, cols512(glu_v, s % 2, s // 2))
            sp.wait_ge(ysum_ready, 2)
            sp.dma_start(bglu_b[:], b_glu.to_broadcast([P, SW])).then_inc(mix2_in, 16)
            for s in range(16):
                load_quad(Q_OUT + s, 0, cols512(wout_v, 2 * (1 - s // 8) + s % 2, s // 2 % 4))
            ffn(2, Q_FFN2, J_FFN2, T_FFN2, w1b, w3b, w2b)
            for n in range(4):
                sp.wait_ge(x_added, XA_FFN2 + 16 + 2 * n + 2)
                sp.dma_start(out_v[:, :, n * NB:(n + 1) * NB], X[:, :, n * NB:(n + 1) * NB]).then_inc(out_done, 16)
            sp.wait_ge(out_done, 64)

        @block.scalar
        def _(act):
            def round_quad(q, di):
                act.wait_ge(raw_landed[q % 4], 16 * (q // 4 + 1) + 4 * di)
                if q >= 2 or not isinstance(di, int):
                    act.wait_ge(quads_used, q - 1 + di)
                nc.scalar.activation(w_hi[:, q % 2], raw[:, q % 4], ACT.Copy).then_inc(rounded, 1)

            def save_mod(b, db):
                act.wait_ge(cols_reduced, b + db + 1)
                nc.scalar.activation(mod[:, bass.ds(4 * b + 4 * db, 4)], misc[:, 0, 0:4], ACT.Copy).then_inc(mod_saved, 1)

            def h_norm(base, x_ready_n):
                if x_ready_n:
                    act.wait_ge(x_added, x_ready_n)
                else:
                    act.wait_ge(x_in, 16)
                for t in range(TT):
                    nc.scalar.activation(xs[:, t], X[:, t], ACT.Square, accum_out=ssq[:, t:t + 1]).then_inc(ssum, 1)

            def hi_scaled(bank, m, hi, k0, scale, bias):
                act.wait_ge(tr_written, bank + 1)
                for kk in range(2):
                    k = 2 * m + kk
                    last = nc.scalar.activation(hi[:, k0 + k], tr[:, bank % 2, kk * T:(kk + 1) * T], ACT.Identity,
                                                bias=bias(k), scale=scale(k))
                last.then_inc(tr_hi, 1)

            def hi_plain(bank, dst):
                act.wait_ge(tr_written, bank + 1)
                nc.scalar.activation(dst, tr[:, bank % 2], ACT.Copy).then_inc(tr_hi, 1)

            def h_make(sub, bank0):
                act.wait_ge(coef, sub + 1)
                for m in range(8):
                    hi_scaled(bank0 + m, m, h_hi, 0, lambda k: h_scale[:, k:k + 1], lambda k: h_shift[:, k:k + 1])

            def hi_gt(bank, dk, b):
                act.wait_ge(tr_written, bank[0] + b + 1 + bank[1])
                nc.scalar.activation(gt_hi[:, bass.ds(4 * dk + 2 * b, 2)].rearrange("p k t -> p (k t)"),
                                     tr[:, b], ACT.Copy).then_inc(tr_hi, 1)

            def save_gate(gg, n):
                act.wait_ge(gate_bcast, gg + 1)
                nc.scalar.activation(gate[:, n * NB:(n + 1) * NB], misc[:, 1], ACT.Copy).then_inc(gate_saved, 1)

            def ffn(layer, q0, j0, t0):
                for t, (blk, n, qu, qd, jp, tb) in enumerate(thirds(q0, j0, t0)):
                    def silu(i):
                        act.wait_ge(quads_used, qu + 4 + 8 * i)
                        if jp or not isinstance(i, int):
                            act.wait_ge(job_read[1], jp + i)
                        nc.scalar.activation(s1[:], acc_a[:], ACT.Silu).then_inc(job_read[0], 1)

                    def up(i):
                        peeled = isinstance(i, int)
                        for s in range(8):
                            round_quad(qu + s, 8 * i)
                            if s == 2 and not peeled:
                                for b in range(2):
                                    hi_gt((tb, 2 * i - 2), i - 1, b)
                            if s == 5:
                                silu(i)
                            for b, db in ada_done_up(layer, t, s - 1, i):
                                save_mod(b, db)
                    looped(act, n, up)
                    for s in range(4 * n):
                        round_quad(qd + s, 0)
                        if s == 2:
                            for b in range(2):
                                hi_gt((tb, 2 * n - 2), n - 1, b)
                        for b, db in ada_done_down(layer, t, s - 1):
                            save_mod(b, db)
                        if t == 0 and s % n == 1:
                            save_gate((0, 8)[layer - 1] + s // n, s // n)

            def save_proj(j):
                act.wait_ge(quads_used, Q_WIN + 4 * j + 4)
                dst = (u_tok, q_tok, k_tok, v_tok)[j // 2][:, :, (j % 2) * NB:(j % 2 + 1) * NB]
                nc.scalar.activation(dst, pairs[j % 2][:], ACT.Copy).then_inc(job_read[j % 2], 1)

            def copy_bank(bank, dst):
                act.wait_ge(tr_written, bank + 1)
                nc.scalar.activation(dst, tr[:, bank % 2], ACT.Copy).then_inc(tr_free, 1)

            for i, (c0, n) in enumerate(((0, 96), (96, 73), (C_BADA, 128), (C_BADA + 128, 16))):
                act.wait_ge(cols_t, i + 1)
                nc.scalar.activation(cols[:, c0:c0 + n], tr[:, i % 2, 0:n], ACT.Copy).then_inc(cols_saved, 1)
                if i == 1:
                    act.wait_ge(cols_saved, 2)
                    nc.scalar.activation(cond[:], cols[:, C_COND:C_COND + 16], ACT.Silu).then_inc(cond_r, 1)
            act.wait_ge(cols_saved, 2)
            nc.scalar.activation(sc[:, 0], cols[:, C_LDT:C_LDT + 32], ACT.Exp).then_inc(act_c, 1)
            save_mod(0, 0)
            act.wait_ge(dve_c, SSM_RD)
            nc.scalar.activation(ssm_r[:], sc[:, 1], ACT.Exp).then_inc(act_c, 1)
            act.wait_ge(dve_c, SSM_NF)
            nc.scalar.activation(sc[:, 5], sc[:, 4], ACT.Abs).then_inc(act_c, 1)
            nc.scalar.activation(sc[:, 6], sc[:, 4], ACT.Sin, scale=-SIN_SCALE).then_inc(act_c, 1)
            act.wait_ge(act_c, 3)
            nc.scalar.activation(sc[:, 7], sc[:, 5], ACT.Sin, scale=-SIN_SCALE, bias=half_pi[:, 0:1])\
                .then_inc(act_c, 1)
            save_mod(1, 0)
            save_mod(2, 0)
            for i in range(8):
                act.wait_ge(cols_t, 4 + i + 1)
                dst = (bt_re, bt_im)[i // 4][:, 2 * (i % 4):2 * (i % 4) + 2].rearrange("p a b -> p (a b)")
                nc.scalar.activation(dst, tr[:, i % 2, 0:256], ACT.Copy).then_inc(cols_saved, 1)
            for b in range(3, 8):
                save_mod(b, 0)
            h_norm(0, 0)
            h_make(0, T_H1)
            ffn(1, Q_FFN1, J_FFN1, T_FFN1)
            h_norm(1, 24)
            h_make(1, T_H2)

            steps = [5]

            def step(ins):
                steps[0] += 1
                ins.then_inc(act_c, 1)

            def phase_parts(r):
                kp, xx, yy = parts[r % 2]
                if r >= 2:
                    act.wait_ge(nf_ready, r - 1)
                step(nc.scalar.activation(kp[:], iota_t[:], ACT.Identity, scale=psi[:, r:r + 1], bias=magic[:, 0:1]))
                nc.scalar.activation(xx[:], iota_t[:], ACT.Copy, scale=psi_hi[:, r:r + 1])
                nc.scalar.activation(yy[:], iota_t[:], ACT.Copy, scale=psi_lo[:, r:r + 1])
                act.wait_ge(act_c, steps[0])
                nc.scalar.activation(kp[:], kp[:], ACT.Identity, bias=magic[:, 1:2]).then_inc(parts_ready, 1)

            def angles():
                act.wait_ge(ang_ready, 1)
                nc.scalar.activation(cs_pos[:, 1], ang[:, 0], ACT.Sin, scale=-SIN_SCALE)
                step(nc.scalar.activation(ang[:, 1], ang[:, 0], ACT.Abs))
                act.wait_ge(act_c, steps[0])
                nc.scalar.activation(cs_pos[:, 0], ang[:, 1], ACT.Sin, scale=-SIN_SCALE, bias=half_pi[:, 0:1])\
                    .then_inc(trig_ready, 1)
                act.wait_ge(lam_in, 1)
                nc.scalar.activation(small[:, 2:4], small[:, 0:2], ACT.Exp).then_inc(lam_ex, 1)

            def cos_sin(r):
                act.wait_ge(nf_ready, r + 1)
                if r:
                    act.wait_ge(cs_ready, r)
                if r == 3:
                    act.wait_ge(u_scaled, 1)
                if r >= 4:
                    act.wait_ge(prods, r - 3)
                step(nc.scalar.activation(ab[:], nf[:, r % 2], ACT.Abs))
                nc.scalar.activation(cs[r % 4][:, 1], nf[:, r % 2], ACT.Sin, scale=-SIN_SCALE)
                act.wait_ge(act_c, steps[0])
                nc.scalar.activation(cs[r % 4][:, 0], ab[:], ACT.Sin, scale=-SIN_SCALE, bias=half_pi[:, 0:1])\
                    .then_inc(cs_ready, 1)

            def gelu(hf):
                act.wait_ge(ysum_ready, hf + 1)
                yv = u_tok[:, :, hf * NB:(hf + 1) * NB]
                nc.scalar.activation(yv, yv, ACT.Gelu_apprx_tanh).then_inc(yg_ready, 1)

            for s in range(33):
                round_quad(Q_WIN + s, 0)
                if s % 4 == 1 and s > 4:
                    save_proj(s // 4 - 1)
                if s == 9:
                    for m in range(4):
                        copy_bank(T_U + m, ut[:, 2 * m:2 * m + 2].rearrange("p k t -> p (k t)"))
                if s == 0:
                    phase_parts(0)
                    phase_parts(1)
                if s == 1 or s == 2:
                    cos_sin(s - 1)
                    phase_parts(s + 1)
                if s == 7:
                    angles()
                for r in tile_steps(s - 1):
                    if r + 2 < NT:
                        cos_sin(r + 2)
                    if r + 4 < NT:
                        phase_parts(r + 4)
                    if r == 20:
                        gelu(0)
            round_quad(Q_GLU + 1, 0)

            def squares(w, tok):
                for t in range(TT):
                    if w:
                        act.wait_ge(sq_read, t + 1)
                    nc.scalar.activation(sq[:, t], tok[:, t], ACT.Square).then_inc(sq_ready, 1)

            act.wait_ge(prods, NT)
            squares(0, q_tok)
            gelu(1)
            nc.scalar.activation(mask[:], early_mask, ACT.Copy).then_inc(mask_moved, 1)
            save_proj(7)
            for m in range(4):
                hi_plain(T_YG + m, yt_hi[:, 2 * m:2 * m + 2].rearrange("p k t -> p (k t)"))
            squares(1, k_tok)

            def sigmoid(j):
                act.wait_ge(job_read[j], J_GLU + 1)
                nc.scalar.activation(gsig[j][:], gsig[j][:], ACT.Sigmoid).then_inc(sig_ready, 1)

            round_quad(Q_GLU + 2, 0)
            save_gate(4, 0)
            round_quad(Q_GLU + 3, 0)
            sigmoid(0)
            round_quad(Q_OUT, 0)
            save_gate(5, 1)
            for m in range(8):
                bank, w = T_QK + m, m // 4
                act.wait_ge(tr_written, bank + 1)
                nc.scalar.activation((qt, kt)[w][:, 2 * (m % 4):2 * (m % 4) + 2].rearrange("p k t -> p (k t)"),
                                     tr[:, bank % 2], ACT.Copy, scale=gain_col[:, w:w + 1]).then_inc(tr_free, 1)
                if m % 4 == 3:
                    save_gate(6 + w, 2 + w)
            round_quad(Q_OUT + 1, 0)
            sigmoid(1)

            def exps(i):
                act.wait_ge(mx_ready, i + 1)
                st = stat(i)
                for cc in range(2):
                    last = nc.scalar.activation(pr[:, i % 2, cc], sm[:, i % 2, cc], ACT.Exp, bias=st[:, cc:cc + 1],
                                                accum_out=st[:, 2 + cc:3 + cc])
                last.then_inc(p_ready, 1)

            def output(i):
                h, t = i // 2, i % 2
                act.wait_ge(o_ready, i + 1)
                nc.scalar.activation(o_sq[:, i % 2], tr[:, i % 2, T:T + P], ACT.Square,
                                     accum_out=small[:, 32 + 8 * t + h:33 + 8 * t + h])
                nc.scalar.activation(ao[:, t, h * P:(h + 1) * P], tr[:, i % 2, T:T + P], ACT.Copy).then_inc(tr_free, 1)

            def attend(i):
                if i + 1 < 2 * HEADS:
                    exps(i + 1)
                act.wait_ge(tr_written, a_bank(i) + 1)
                if i >= 2:
                    act.wait_ge(o_ready, i - 1)
                nc.scalar.activation(at[:, i % 2], tr[:, i % 2, 0:T], ACT.Copy).then_inc(at_ready, 1)
                if i not in (0, A_FIRST):
                    output(i - 1)

            exps(0)
            for i in range(A_FIRST):
                attend(i)
                if i == 0:
                    act.wait_ge(y2_ready, 2)
                    for t in range(TT):
                        nc.scalar.activation(y_sq[:, t], u_tok[:, t], ACT.Square, accum_out=ssq[:, t:t + 1])\
                            .then_inc(ssum, 1)
            output(A_FIRST - 1)
            for m in range(4):
                hi_scaled(T_Y2 + m, m, h_hi, 8, lambda k: cols[:, C_OUTN + k:C_OUTN + k + 1],
                          lambda k: small[:, 20:21])
            for s in range(8):
                steps = attention_steps(s)
                if steps:
                    attend(steps[0])
                if s:
                    round_quad(Q_OUT + s + 1, 0)
                if steps:
                    attend(steps[1])
                if attention_steps(s) and attention_steps(s)[-1] == 2 * HEADS - 1:
                    output(2 * HEADS - 1)
            for m in range(4):
                bank = T_AO + m
                act.wait_ge(tr_written, bank + 1)
                nc.scalar.activation(h_hi[:, 2 * m:2 * m + 2].rearrange("p k t -> p (k t)"), tr[:, bank % 2], ACT.Copy,
                                     scale=small[:, 16:17]).then_inc(tr_hi, 1)
            for s in range(9, 16):
                round_quad(Q_OUT + s, 0)
            h_norm(2, XA_FFN2)
            h_make(2, T_H3)
            ffn(2, Q_FFN2, J_FFN2, T_FFN2)

        @block.vector
        def _(dve):
            chain = [0]
            rms = [0]
            added = [0]
            v = nc.vector

            def link(ins):
                chain[0] += 1
                ins.then_inc(dve_c, 1)
                dve.wait_ge(dve_c, chain[0])

            def split_quad(q, di):
                dve.wait_ge(rounded, q + 1 + di)
                if q >= 2 or not isinstance(di, int):
                    dve.wait_ge(quads_used, q - 1 + di)
                v.tensor_tensor(w_lo[:, q % 2], raw[:, q % 4], w_hi[:, q % 2].bitcast(F32), ALU.subtract)\
                    .then_inc(split, 1)

            def ada_quad(b, db, k, buf, strict=False):
                dve.wait_ge(ada_landed[k % 2], 16 * (2 * b + k // 2 + 1) + 32 * db)
                if k == 0 and b >= 2:
                    dve.wait_ge(cols_reduced, b + db if strict else b - 1 + db)
                for kk in range(4):
                    n = 4 * k + kk
                    dst, w, s = acc[:, buf, n % 2], ada[:, k % 2, kk], cond[:, n:n + 1]
                    if n < 2:
                        ins = v.tensor_scalar(dst, w, s, None, ALU.mult)
                    else:
                        dve.wait_ge(ada_fma, 16 * b + 16 * db + n - 1)
                        ins = v.scalar_tensor_tensor(dst, w, s, dst, ALU.mult, ALU.add)
                    ins.then_inc(ada_fma, 1)

            def coefficients(sub, norm_c):
                dve.wait_ge(mod_saved, 12 * sub + 8)
                s0 = 48 * sub
                v.tensor_tensor(h_shift[:], mod[:, s0:s0 + 16], cols[:, C_BADA + s0:C_BADA + s0 + 16], ALU.add)
                link(v.tensor_tensor(gate_col[:], mod[:, s0 + 16:s0 + 32],
                                     cols[:, C_BADA + s0 + 16:C_BADA + s0 + 32], ALU.add))
                v.scalar_tensor_tensor(h_scale[:], gate_col[:], 1.0, cols[:, norm_c:norm_c + 16], ALU.add, ALU.mult)\
                    .then_inc(coef, 1)
                dve.wait_ge(coef, sub + 1)

            def inv_rms(ins):
                ins.then_inc(rms_in, 1)
                rms[0] += 1
                dve.wait_ge(rms_out, rms[0])

            def h_norm(ss0, dst, src):
                for t in range(TT):
                    rms[0] += 1
                    dve.wait_ge(rms_out, rms[0])
                    v.tensor_scalar(dst[:, t], src[:, t], rstd[:, t:t + 1], None, ALU.mult).then_inc(xs_ready, 1)

            def lo_scaled(bank, m, hi, lo, k0, scale, bias, tmp):
                dve.wait_ge(tr_hi, hi_count(bank) + 1)
                for kk in range(2):
                    k = 2 * m + kk
                    ins = v.tensor_scalar(tmp[:, m % 2, kk * T:(kk + 1) * T], tr[:, bank % 2, kk * T:(kk + 1) * T],
                                          scale(k), bias(k), ALU.mult, ALU.add)
                link(ins)
                v.tensor_tensor(lo[:, k0 + 2 * m:k0 + 2 * m + 2].rearrange("p k t -> p (k t)"), tmp[:, m % 2],
                                hi[:, k0 + 2 * m:k0 + 2 * m + 2].rearrange("p k t -> p (k t)").bitcast(F32),
                                ALU.subtract).then_inc(tr_free, 1)

            def lo_plain(bank, hi, lo):
                dve.wait_ge(tr_hi, hi_count(bank) + 1)
                v.tensor_tensor(lo, tr[:, bank % 2], hi.bitcast(F32), ALU.subtract).then_inc(tr_free, 1)

            def h_make(bank0):
                for m in range(8):
                    lo_scaled(bank0 + m, m, h_hi, h_lo, 0, lambda k: h_scale[:, k:k + 1],
                              lambda k: h_shift[:, k:k + 1], s1)

            def lo_gt(bank, dk, b):
                dve.wait_ge(tr_hi, hi_count(bank[0]) + b + 1 + bank[1])
                dst = bass.ds(4 * dk + 2 * b, 2)
                v.tensor_tensor(gt_lo[:, dst].rearrange("p k t -> p (k t)"), tr[:, b],
                                gt_hi[:, dst].rearrange("p k t -> p (k t)").bitcast(F32), ALU.subtract)\
                    .then_inc(tr_free, 1)

            def add_x(pair, pi, job_quads, n, gsem):
                dve.wait_ge(quads_used, job_quads)
                if gsem is not None:
                    dve.wait_ge(gate_saved, gsem)
                if added[0]:
                    dve.wait_ge(x_added, added[0])
                added[0] += TT
                for t in range(TT):
                    ins = v.tensor_tensor(g[:, t], pairs[pair][:, t], gate[:, n * NB:(n + 1) * NB], ALU.mult)
                ins.then_inc(job_read[pair], 1)
                dve.wait_ge(job_read[pair], pi + 1)
                for t in range(TT):
                    xn = X[:, t, n * NB:(n + 1) * NB]
                    v.tensor_tensor(xn, xn, g[:, t], ALU.add).then_inc(x_added, 1)

            def gate_column(sub, factor):
                dve.wait_ge(mod_saved, 12 * sub + 12)
                s0 = 48 * sub + 32
                link(v.tensor_tensor(gate_col[:], mod[:, s0:s0 + 16], cols[:, C_BADA + s0:C_BADA + s0 + 16], ALU.add))
                v.tensor_scalar(gate_col[:], gate_col[:], factor, None, ALU.mult).then_inc(gate_cols, 1)

            def ffn(layer, q0, j0, t0):
                for t, (blk, n, qu, qd, jp, tb) in enumerate(thirds(q0, j0, t0)):
                    def hidden(i, m):
                        dve.wait_ge(quads_used, qu + 8 + 8 * m)
                        dve.wait_ge(job_read[0], jp + m + 1)
                        dve.wait_ge(tr_written, tb + 2 * m)
                        v.tensor_tensor(g[:], s1[:], acc_b[:], ALU.mult).then_inc(job_read[1], 1)

                    def up(i):
                        peeled = isinstance(i, int)
                        for s in range(8):
                            if s == 1 and not peeled:
                                hidden(i, i - 1)
                            split_quad(qu + s, 8 * i)
                            if s == 2 and not peeled:
                                for b in range(2):
                                    lo_gt((tb, 2 * i - 2), i - 1, b)
                            if layer == 1:
                                ada_quad(ADA_UP1[t] + s // 4, 2 * i, s % 4, s // 4)
                            elif t == 0 and s < 4:
                                ada_quad(ADA_UP2, i, s, 0, strict=not peeled)
                    looped(dve, n, up)
                    if t == 0:
                        gate_column(2 * (layer - 1), 0.5)
                    for s in range(4 * n):
                        if s == 1:
                            hidden(None, n - 1)
                        split_quad(qd + s, 0)
                        if s == 2:
                            for b in range(2):
                                lo_gt((tb, 2 * n - 2), n - 1, b)
                        if s % n == 0 and s:
                            j = s // n - 1
                            add_x(j % 2, jp + n + j // 2, qd + n * (j + 1), j,
                                  ((0, 8)[layer - 1] + j + 1) if t == 0 else None)
                        if layer == 1 and t == 0 and s // 4 in (0, 2):
                            ada_quad(ADA_DOWN1[s // 8], 0, s % 4, s // 8)
                    add_x(1, jp + n + 1, qd + 4 * n, 3, ((0, 8)[layer - 1] + 4) if t == 0 else None)

            v.memset(half_pi[:], float(np.pi / 2))
            v.memset(magic[:, 0:1], MAGIC)
            v.memset(gain_col[:], 1.0).then_inc(gain_ones, 1)
            v.memset(magic[:, 1:2], -MAGIC)
            dve.wait_ge(small_in, SMALL_IN)
            v.tensor_copy(rows[64:96, 0].rearrange("p (g s) -> p g s", g=2),
                          small[64:96, 24:26].unsqueeze(2).to_broadcast([32, 2, ST])).then_inc(dt_spread, 1)
            dve.wait_ge(cond_r, 1)

            def ssm_rates():
                dve.wait_ge(act_c, 1)
                link(v.tensor_scalar(sc[:, 2], cols[:, C_ARE:C_ARE + 32], -1e-4, None, ALU.min))
                link(v.tensor_tensor(sc[:, 1], sc[:, 2], sc[:, 0], ALU.mult))
                assert chain[0] == SSM_RD
                link(v.tensor_tensor(sc[:, 3], cols[:, C_AIM:C_AIM + 32], sc[:, 0], ALU.mult))
                link(v.tensor_scalar(sc[:, 8], sc[:, 3], float(1 / TWO_PI), MAGIC, ALU.mult, ALU.add))
                link(v.tensor_scalar(sc[:, 8], sc[:, 8], MAGIC, None, ALU.subtract))
                for cst in (C1, C2, C3):
                    link(v.scalar_tensor_tensor(sc[:, 3], sc[:, 8], -cst, sc[:, 3], ALU.mult, ALU.add))
                link(v.tensor_scalar(psi[:], sc[:, 3], float(1 / TWO_PI), None, ALU.mult))
                link(v.tensor_scalar(sc[:, 4], psi[:], -1.0, None, ALU.mult))
                link(v.tensor_scalar(sc[:, 4], sc[:, 4], 0.5, -0.5, ALU.min, ALU.max))
                assert chain[0] == SSM_NF
                link(v.tensor_scalar(psi_hi[:], psi[:], MAGIC16, None, ALU.add))
                link(v.tensor_scalar(psi_hi[:], psi_hi[:], MAGIC16, None, ALU.subtract))
                link(v.tensor_tensor(psi_lo[:], psi[:], psi_hi[:], ALU.subtract))

            def ssm_f():
                dve.wait_ge(act_c, 5)
                link(v.tensor_tensor(sc[:, 9], ssm_r[:], sc[:, 7], ALU.mult))
                link(v.tensor_scalar(sc[:, 9], sc[:, 9], 1.0, None, ALU.subtract))
                link(v.tensor_tensor(sc[:, 10], ssm_r[:], sc[:, 6], ALU.mult))
                link(v.tensor_tensor(sc[:, 11], sc[:, 2], sc[:, 2], ALU.mult))
                aim = cols[:, C_AIM:C_AIM + 32]
                link(v.tensor_tensor(sc[:, 12], aim, aim, ALU.mult))
                link(v.tensor_tensor(sc[:, 11], sc[:, 11], sc[:, 12], ALU.add))
                link(v.reciprocal(sc[:, 11], sc[:, 11]))
                link(v.tensor_tensor(sc[:, 12], sc[:, 9], sc[:, 2], ALU.mult))
                link(v.tensor_tensor(sc[:, 13], sc[:, 10], aim, ALU.mult))
                link(v.tensor_tensor(sc[:, 12], sc[:, 12], sc[:, 13], ALU.add))
                link(v.tensor_tensor(sc[:, 14], sc[:, 12], sc[:, 11], ALU.mult))
                link(v.tensor_tensor(sc[:, 12], sc[:, 10], sc[:, 2], ALU.mult))
                link(v.tensor_tensor(sc[:, 13], sc[:, 9], aim, ALU.mult))
                link(v.tensor_tensor(sc[:, 12], sc[:, 12], sc[:, 13], ALU.subtract))
                link(v.tensor_tensor(sc[:, 15], sc[:, 12], sc[:, 11], ALU.mult))

            def ssm_b():
                dve.wait_ge(small_in, SMALL_IN)
                dve.wait_ge(b_pad, 2)
                fr = sc[:, 14].unsqueeze(2).to_broadcast([P, NT, GC])
                fi = sc[:, 15].unsqueeze(2).to_broadcast([P, NT, GC])
                link(v.tensor_tensor(prod1[:], bnat_re[:], fr, ALU.mult))
                link(v.tensor_tensor(prod2[:], bnat_im[:], fi, ALU.mult))
                for h in range(2):
                    hp, hc = slice(64 * h, 64 * h + 64), slice(GC * h, GC * h + GC)
                    link(v.tensor_tensor(bpad_re[hp, :, hc], prod1[hp], prod2[hp], ALU.subtract))
                link(v.tensor_tensor(prod1[:], bnat_im[:], fr, ALU.mult))
                link(v.tensor_tensor(prod2[:], bnat_re[:], fi, ALU.mult))
                for h in range(2):
                    hp, hc = slice(64 * h, 64 * h + 64), slice(GC * h, GC * h + GC)
                    ins = v.tensor_tensor(bpad_im[hp, :, hc], prod1[hp], prod2[hp], ALU.add)
                ins.then_inc(b_pad, 1)

            def ssm_c():
                dve.wait_ge(const_ready, 2)
                for i in range(4):
                    dve.wait_ge(cols_t, 12 + i + 1)
                    dst = (c_re_t, c_im_t)[i // 2]
                    sgn = (1.0, -1.0)[i // 2]
                    src = tr[:, i % 2].rearrange("p (r g c) -> p r g c", g=2, c=GC)
                    for h in range(2):
                        hp, hc = slice(64 * h, 64 * h + 64), slice(GC * h, GC * h + GC)
                        ins = v.tensor_scalar(dst[hp, 16 * (i % 2):16 * (i % 2) + 16, hc], src[hp, :, h], sgn, None, ALU.mult)
                    ins.then_inc(c_saved, 1)


            for b in range(8):
                for k in range(4):
                    ada_quad(b, 0, k, b % 2)
                if b < 4:
                    (ssm_rates, ssm_f, ssm_b, ssm_c)[b]()
            coefficients(0, C_N1)
            h_norm(0, xs, X)
            h_make(T_H1)
            ffn(1, Q_FFN1, J_FFN1, T_FFN1)
            coefficients(1, C_N2)
            h_norm(2, xs, X)
            h_make(T_H2)
            gate_column(1, 1.0)

            def turn(r):
                dve.wait_ge(bu_ready, r + 1)
                dve.wait_ge(cs_ready, r + 1)
                bu = misc[:, r % 2].rearrange("p (a t) -> p a t", a=2)
                csr = cs[r % 4]
                if r:
                    dve.wait_ge(zin_ready, r)
                v.tensor_tensor(p1[:], csr, bu, ALU.mult)
                v.tensor_tensor(p2[:, 0], csr[:, 0], bu[:, 1], ALU.mult)
                v.tensor_tensor(p2[:, 1], csr[:, 1], bu[:, 0], ALU.mult).then_inc(bu_read, 1)

            def scan_input(r):
                dve.wait_ge(bu_read, r + 1)
                if r == 1:
                    dve.wait_ge(u_scaled, 1)
                if r >= 2:
                    dve.wait_ge(scanned, r - 1)
                zi = zin[r % 2]
                v.tensor_tensor(zi[:, 0], p1[:, 0], p1[:, 1], ALU.add)
                v.tensor_tensor(zi[:, 1], p2[:, 0], p2[:, 1], ALU.subtract).then_inc(zin_ready, 1)

            def scan(r):
                dve.wait_ge(zin_ready, r + 1)
                if r:
                    dve.wait_ge(prods, r)
                rad = ssm_r[:, r:r + 1].to_broadcast([P, T])
                v.tensor_tensor_scan(zz[:, 0], rad, zin[r % 2][:, 0], 0.0, ALU.mult, ALU.add)
                v.tensor_tensor_scan(zz[:, 1], rad, zin[r % 2][:, 1], 0.0, ALU.mult, ALU.add).then_inc(scanned, 1)

            def turn_back(r):
                dve.wait_ge(scanned, r + 1)
                if r >= 2:
                    dve.wait_ge(y_done, r - 1)
                csr, bk = cs[r % 4], back[:, r % 2]
                v.tensor_tensor(bk[:, 0], csr, zz[:], ALU.mult)
                v.tensor_tensor(bk[:, 1, 0], csr[:, 0], zz[:, 1], ALU.mult)
                v.tensor_tensor(bk[:, 1, 1], csr[:, 1], zz[:, 0], ALU.mult).then_inc(prods, 1)

            def add_du(hf):
                dve.wait_ge(y_done, 16 * hf + 16)
                dve.wait_ge(u_scaled, 1)
                for t in range(TT):
                    dst = u_tok[:, t, hf * NB:(hf + 1) * NB]
                    ins = v.tensor_tensor(dst, tr[:, t], dst, ALU.add)
                ins.then_inc(ysum_ready, 1)

            def prepare_attention():
                dve.wait_ge(mix2_in, 16 * 12)
                link(v.tensor_copy(posf[:], posi[:]))
                for t in range(TT):
                    for f in range(8):
                        ins = v.tensor_scalar(ang[:, 2, t, f:f + 1], posf[:, t:t + 1], INV_FREQ[f], None, ALU.mult)
                link(ins)
                link(v.tensor_scalar(ang[:, 3], ang[:, 2], float(1 / TWO_PI), MAGIC, ALU.mult, ALU.add))
                link(v.tensor_scalar(ang[:, 3], ang[:, 3], MAGIC, None, ALU.subtract))
                for cst in (C1, C2, C3):
                    link(v.scalar_tensor_tensor(ang[:, 2].rearrange("p a b -> p (a b)"),
                                                ang[:, 3].rearrange("p a b -> p (a b)"), -cst,
                                                ang[:, 2].rearrange("p a b -> p (a b)"), ALU.mult, ALU.add))
                link(v.tensor_scalar(ang[:, 0], ang[:, 2], float(-1 / TWO_PI), None, ALU.mult))
                v.tensor_scalar(ang[:, 0], ang[:, 0], 0.5, -0.5, ALU.min, ALU.max).then_inc(ang_ready, 1)
                link(v.tensor_scalar(posi[:], posi[:], 6, None, ALU.arith_shift_right))
                link(v.tensor_scalar(posr[:], posr[:], 6, None, ALU.arith_shift_right))
                v.tensor_copy(chunk_c[:], posi[:])
                link(v.tensor_copy(chunk_r[:], posr[:]))
                for t in range(TT):
                    ins = v.tensor_scalar(early_mask[:, t], chunk_r[:], chunk_c[:, t:t + 1], NEG, ALU.is_gt, ALU.mult)
                link(ins)
                v.tensor_tensor(lamv[:, 0], lamv[:, 0], lamv[:, 1], ALU.mult)
                link(v.tensor_tensor(lamv[:, 2], lamv[:, 2], lamv[:, 3], ALU.mult))
                v.tensor_reduce(small[:, 0:1], lamv[:, 0], AX.X, ALU.add)
                v.tensor_reduce(small[:, 1:2], lamv[:, 2], AX.X, ALU.add).then_inc(lam_in, 1)
                dve.wait_ge(lam_ex, 1)
                link(v.tensor_tensor(small[:, 4:5], small[:, 3:4], small[:, 2:3], ALU.subtract))
                link(v.tensor_scalar(small[:, 4:5], small[:, 4:5], LAM_INIT, None, ALU.subtract))
                link(v.tensor_scalar(small[:, 16:17], cols[:, C_SUBLN:C_SUBLN + 1], 1.0 - LAM_INIT, None, ALU.mult))
                link(v.memset(small[:, 20:21], 0.0))

            for s in range(33):
                split_quad(Q_WIN + s, 0)
                if s == 6:
                    prepare_attention()
                if s == FIRST_STEP:
                    dve.wait_ge(trig_ready, 1)
                    for w in range(2):
                        for e, (fn, half) in enumerate(((0, 0), (1, 1), (1, 0), (0, 1))):
                            ins = v.tensor_tensor(rope_g[:, w, e], cs_pos[:, fn],
                                                  qkn[:, w, 8 * half:8 * half + 8].unsqueeze(1).to_broadcast([P, TT, 8]),
                                                  ALU.mult)
                    link(ins)
                    turn(0)
                    scan_input(0)
                for r in tile_steps(s - 1):
                    if r + 1 < NT:
                        turn(r + 1)
                    scan(r)
                    if r + 1 < NT:
                        scan_input(r + 1)
                    turn_back(r)
                    if r == 17:
                        add_du(0)
            split_quad(Q_GLU + 1, 0)
            add_du(1)

            ss = qk_ss[:].rearrange("p (w t h) -> p w t h", w=2, t=TT)

            def sum_squares(w):
                for t in range(TT):
                    dve.wait_ge(sq_ready, 2 * w + t + 1)
                    v.tensor_reduce(ss[:, w, t], sq[:, t].rearrange("p (h d) -> p h d", d=HD), AX.X, ALU.add)\
                        .then_inc(sq_read, 1)

            def rotate(w, tok):
                for t in range(TT):
                    rms[0] += 1
                    dve.wait_ge(rms_out, rms[0])
                    tv = tok[:, t].rearrange("p (h d) -> p h d", d=HD)
                    link(v.tensor_tensor(tv, tv, ss[:, w, t].unsqueeze(2).to_broadcast([P, 16, HD]), ALU.mult))
                    x1, x2 = tv[:, :, 0:8], tv[:, :, 8:16]
                    rt = [rope_t[:, i].rearrange("p (h d) -> p h d", d=8) for i in range(4)]
                    for e, xe in enumerate((x1, x2, x1, x2)):
                        tab = rope_g[:, w, e, t].unsqueeze(1).to_broadcast([P, 16, 8])
                        ins = v.tensor_tensor(rt[e], xe, tab, ALU.mult)
                    link(ins)
                    v.tensor_tensor(x1, rt[0], rt[1], ALU.subtract)
                    ins = v.tensor_tensor(x2, rt[2], rt[3], ALU.add)
                    if t == 0:
                        link(ins)
                ins.then_inc(qk_ready, 1)

            sum_squares(0)
            for m in range(4):
                lo_plain(T_YG + m, yt_hi[:, 2 * m:2 * m + 2].rearrange("p k t -> p (k t)"),
                         yt_lo[:, 2 * m:2 * m + 2].rearrange("p k t -> p (k t)"))
            split_quad(Q_GLU + 2, 0)
            rotate(0, q_tok)
            sum_squares(1)
            split_quad(Q_GLU + 3, 0)
            dve.wait_ge(job_read[1], J_WIN + 4)
            rotate(1, k_tok)

            def glu_sum(j):
                dve.wait_ge(quads_used, Q_GLU + 4)
                if j:
                    dve.wait_ge(tr_written, T_QK + 8)
                for t in range(TT):
                    ins = v.tensor_tensor(gsig[j][:, t], pairs[j][:, t], bglu_b[:, j * NB:(j + 1) * NB], ALU.add)
                ins.then_inc(job_read[j], 1)

            def glu_gate(j):
                dve.wait_ge(sig_ready, j + 1)
                yv = u_tok[:, :, j * NB:(j + 1) * NB]
                v.tensor_tensor(yv, yv, gsig[j][:], ALU.mult).then_inc(y2_ready, 1)

            dve.wait_ge(mix2_in, 16 * 13)
            glu_sum(0)
            glu_sum(1)
            split_quad(Q_OUT, 0)
            split_quad(Q_OUT + 1, 0)
            glu_gate(0)

            def maxima(i):
                st = stat(i)
                dve.wait_ge(sc_ready, i + 1)
                if i >= 2:
                    dve.wait_ge(p_ready, i - 1)
                for cc in range(2):
                    ins = v.scalar_tensor_tensor(sm[:, i % 2, cc], misc[:, i % 2, cc * T:(cc + 1) * T], HD ** -0.5,
                                                 mask[:, i % 2], ALU.mult, ALU.add)
                ins.then_inc(sc_read, 1)
                dve.wait_ge(sc_read, i + 1)
                link(v.tensor_reduce(st[:, 6:8], sm[:, i % 2], AX.X, ALU.max))
                v.tensor_scalar(st[:, 0:2], st[:, 6:8], -1.0, None, ALU.mult).then_inc(mx_ready, 1)

            def attend(i):
                if i + 1 < 2 * HEADS:
                    maxima(i + 1)
                st = stat(i)
                dve.wait_ge(p_ready, i + 1)
                link(v.reciprocal(st[:, 4:6], st[:, 2:4]))
                if i >= 2:
                    dve.wait_ge(tr_written, a_bank(i - 2) + 1)
                link(v.tensor_tensor(st[:, 5:6], st[:, 5:6], small[:, 4:5], ALU.mult))
                link(v.tensor_scalar(aw[:, i % 2], pr[:, i % 2, 0], st[:, 4:5], None, ALU.mult))
                v.scalar_tensor_tensor(aw[:, i % 2], pr[:, i % 2, 1], st[:, 5:6], aw[:, i % 2], ALU.mult, ALU.add)\
                    .then_inc(a_ready, 1)

            dve.wait_ge(mask_moved, 1)
            maxima(0)
            glu_gate(1)
            for i in range(A_FIRST):
                attend(i)
                if i == 1:
                    h_norm(4, u_tok, u_tok)
            for m in range(4):
                lo_scaled(T_Y2 + m, m, h_hi, h_lo, 8, lambda k: cols[:, C_OUTN + k:C_OUTN + k + 1],
                          lambda k: small[:, 20:21], ev_tmp)

            def out_sum(hj):
                add_x(hj % 2, J_OUT + hj // 2, Q_OUT + 2 * hj + 2, hj % 4, 8 if hj < 4 else None)

            for s in range(8):
                steps = attention_steps(s)
                if steps:
                    attend(steps[0])
                if s:
                    split_quad(Q_OUT + s + 1, 0)
                if steps:
                    attend(steps[1])
                if s % 2 == 0 and s:
                    out_sum(s // 2 - 1)
            rms[0] += 1
            dve.wait_ge(rms_out, rms[0])
            for t in range(TT):
                av = ao[:, t].rearrange("p (h d) -> p h d", d=P)
                ins = v.tensor_tensor(av, av, small[:, 32 + 8 * t:40 + 8 * t].unsqueeze(2).to_broadcast([P, 8, P]),
                                      ALU.mult)
            ins.then_inc(ao_ready, 1)
            out_sum(3)
            for m in range(4):
                lo_scaled(T_AO + m, m, h_hi, h_lo, 0, lambda k: small[:, 16:17], lambda k: small[:, 20:21], ev_tmp)
            for s in range(9, 16):
                split_quad(Q_OUT + s, 0)
                if s % 2 == 0:
                    out_sum(s // 2 - 1)
            out_sum(7)
            coefficients(2, C_N3)
            h_norm(6, xs, X)
            h_make(T_H3)
            ffn(2, Q_FFN2, J_FFN2, T_FFN2)

        @block.gpsimd
        def _(pool):
            g_ = nc.gpsimd
            chain = [0]
            rms = [0]

            def link(ins):
                chain[0] += 1
                ins.then_inc(pool_c, 1)
                pool.wait_ge(pool_c, chain[0])

            def inv_rms(ready, n, dst, src, width):
                pool.wait_ge(ready, n)
                link(g_.tensor_scalar(dst, src, 1.0 / width, EPS, ALU.mult, ALU.add))
                g_.tensor_tensor(dst, dst, small[:, 64:64 + dst.shape[-1]], ALU.pow).then_inc(rms_out, 1)

            def h_norm(ss0, width):
                for t in range(TT):
                    inv_rms(ssum, ss0 + t + 1, rstd[:, t:t + 1], ssq[:, t:t + 1], width)

            def gate_groups(sub, first=0, end=4):
                pool.wait_ge(gate_cols, sub + 1)
                for n in range(first, end):
                    gg = 4 * sub + n
                    if gg:
                        pool.wait_ge(gate_bcast, gg)
                    for j in range(4):
                        k = 4 * n + j
                        ins = g_.tensor_scalar(diag[:, j * P:(j + 1) * P], ident[:], gate_col[:, k:k + 1], None, ALU.mult)
                    ins.then_inc(gate_diag, 1)

            g_.memset(small[:, 64:96], -0.5)
            link(g_.memset(ident[:], 0.0))
            link(g_.affine_select(out=ident[:], in_=ident[:], compare_op=ALU.not_equal, fill=1.0, base=0,
                                  pattern=[[-1, P]], channel_multiplier=1))
            g_.memset(ones[:], 1.0).then_inc(const_ready, 1)
            g_.memset(bpad_re[:], 0.0).then_inc(b_pad, 1)
            g_.memset(bpad_im[:], 0.0).then_inc(b_pad, 1)
            g_.memset(c_re_t[:], 0.0)
            link(g_.memset(c_im_t[:], 0.0))
            g_.iota(iota_t[:], pattern=[[1, T]], base=0, channel_multiplier=0,
                    allow_small_or_imprecise_dtypes=True).then_inc(const_ready, 1)
            h_norm(0, D)
            gate_groups(0)
            h_norm(2, D)
            def phase(r):
                kp, xx, yy = parts[r % 2]
                if r >= 2:
                    pool.wait_ge(cs_ready, r - 1)
                pool.wait_ge(parts_ready, r + 1)
                link(g_.tensor_tensor(nf[:, r % 2], kp[:], xx[:], ALU.subtract))
                link(g_.tensor_tensor(nf[:, r % 2], nf[:, r % 2], yy[:], ALU.subtract))
                g_.tensor_scalar(nf[:, r % 2], nf[:, r % 2], 0.5, -0.5, ALU.min, ALU.max).then_inc(nf_ready, 1)

            phase(0)
            phase(1)
            pool.wait_ge(mix_in, 16)
            pool.wait_ge(tr_written, T_U + 4)
            for t in range(TT):
                ins = g_.tensor_tensor(u_tok[:, t], u_tok[:, t], dskip[:], ALU.mult)
            ins.then_inc(u_scaled, 1)
            phase(2)
            for r in range(NT):
                if r + 3 < NT:
                    phase(r + 3)
                bk = back[:, r % 2]
                pool.wait_ge(prods, r + 1)
                g_.tensor_tensor(bk[:, 0, 0], bk[:, 0, 0], bk[:, 0, 1], ALU.subtract)
                g_.tensor_tensor(bk[:, 1, 0], bk[:, 1, 0], bk[:, 1, 1], ALU.add).then_inc(s_ready, 1)
            pool.wait_ge(mask_moved, 1)
            gate_groups(1, 0, 1)
            for i in range(2 * TT):
                inv_rms(sq_read, i + 1, qk_ss[:, 16 * i:16 * i + 16], qk_ss[:, 16 * i:16 * i + 16], HD)
            gate_groups(1, 1, 4)
            h_norm(4, SW)
            inv_rms(tr_free, T_AO, small[:, 32:48], small[:, 32:48], P)
            h_norm(6, D)
            gate_groups(2)

        @block.tensor
        def _(pe):
            mm = nc.tensor.matmul

            def quad(q, di, hi, lo, k0, pair, start, stop, middle=None):
                pe.wait_ge(split, q + 1 + di)
                r = q % 2
                for kk in range(4):
                    if kk == 2 and middle:
                        middle()
                    for t in range(TT):
                        st, sp_ = start and kk == 0, stop and kk == 3
                        bank = pairs[pair][:, t]
                        lh, ll = hi[:, k0 + kk, t * P:(t + 1) * P], lo[:, k0 + kk, t * P:(t + 1) * P]
                        mm(bank, lh, w_hi[:, r, kk], start=st, stop=False)
                        mm(bank, lh, w_lo[:, r, kk], start=False, stop=False)
                        last = mm(bank, ll, w_hi[:, r, kk], start=False, stop=sp_)
                last.then_inc(quads_used, 1)

            def transposes(bank, dbank, b, src):
                if isinstance(dbank, int) and bank + dbank < 2:
                    pass
                else:
                    pe.wait_ge(tr_free, bank - 1 + dbank)
                for kk in range(2):
                    for t in range(TT):
                        last = nc.tensor.transpose(tr[:, b, kk * T + t * P:kk * T + (t + 1) * P], src(kk, t), ident[:])
                last.then_inc(tr_written, 1)

            def rows_to_cols(bank0, n, tok, xs_n, srcsem):
                pe.wait_ge(srcsem, xs_n)
                for m in range(n):
                    transposes(bank0 + m, 0, (bank0 + m) % 2,
                               lambda kk, t: tok[:, t, (2 * m + kk) * P:(2 * m + kk + 1) * P])

            def reduce_ada(b, db):
                pe.wait_ge(ada_fma, 16 * b + 16 + 16 * db)
                if not (isinstance(db, int) and b + db == 0):
                    pe.wait_ge(mod_saved, b + db)
                buf = b % 2
                for j in range(4):
                    for e in range(2):
                        last = mm(misc[:, 0, j:j + 1], acc[:, buf, e, j * P:(j + 1) * P], ones[:, 0:1],
                                  start=(e == 0), stop=(e == 1))
                last.then_inc(cols_reduced, 1)

            def spread_gate(gg):
                pe.wait_ge(gate_diag, gg + 1)
                if gg:
                    pe.wait_ge(gate_saved, gg)
                mm(misc[:, 1], ones[:], diag[:], start=True, stop=True).then_inc(gate_bcast, 1)

            def ffn(layer, q0, j0, t0):
                for t, (blk, n, qu, qd, jp, tb) in enumerate(thirds(q0, j0, t0)):
                    def hidden_t(m):
                        pe.wait_ge(job_read[1], jp + m + 1)
                        for b in range(2):
                            transposes(tb + b, 2 * m, b, lambda kk, tt: g[:, tt, (2 * b + kk) * P:(2 * b + kk + 1) * P])

                    def up(i):
                        peeled = isinstance(i, int)
                        for s in range(8):
                            if s % 4 == 0 and (jp or not peeled):
                                pe.wait_ge(job_read[s // 4], jp + i)
                            if t == 0 and peeled and s < 4:
                                pe.wait_ge(tr_free, t0 - 8 + 2 * s + 2)
                            quad(qu + s, 8 * i, h_hi, h_lo, 4 * (s % 4), s // 4, s % 4 == 0, s % 4 == 3)
                            if s == 0 and not peeled:
                                hidden_t(i - 1)
                            for b, db in ada_done_up(layer, t, s, i):
                                reduce_ada(b, db)
                    looped(pe, n, up)
                    for s in range(4 * n):
                        j, k = s // n, s % n
                        if k == 0:
                            pe.wait_ge(job_read[j % 2], jp + n + j // 2)
                            if t == 0:
                                spread_gate((0, 8)[layer - 1] + j)
                        if s == n - 1:
                            pe.wait_ge(tr_free, tb + 2 * n)
                        elif s == 0:
                            pe.wait_ge(tr_free, tb + 2 * n - 2)
                        quad(qd + s, 0, gt_hi, gt_lo, 4 * k, j % 2, k == 0, k == n - 1)
                        if s == 0:
                            hidden_t(n - 1)
                        for b, db in ada_done_down(layer, t, s):
                            reduce_ada(b, db)

            pe.wait_ge(const_ready, 1)
            pe.wait_ge(small_in, SMALL_IN)
            pe.wait_ge(dt_spread, 1)
            for i, n in enumerate((96, 73, 128, 16)):
                if i >= 2:
                    pe.wait_ge(cols_saved, i - 1)
                nc.tensor.transpose(tr[:, i % 2, 0:n], rows[0:n, i], ident[0:n, 0:n]).then_inc(cols_t, 1)
            for b in range(8):
                reduce_ada(b, 0)
                if b == 2:
                    pe.wait_ge(b_pad, 3)
                    for i in range(8):
                        pe.wait_ge(cols_saved, 4 + i - 1)
                        src = (bpad_re, bpad_im)[i // 4]
                        for kk in range(2):
                            m = 2 * (i % 4) + kk
                            last = nc.tensor.transpose(tr[:, i % 2, kk * P:(kk + 1) * P],
                                                       src[:, 4 * m:4 * m + 4].rearrange("p a b -> p (a b)"), ident[:])
                        last.then_inc(cols_t, 1)
                if b == 3:
                    for i in range(4):
                        if i < 2:
                            pe.wait_ge(cols_saved, 12)
                        else:
                            pe.wait_ge(c_saved, i - 1)
                        for kk in range(4):
                            last = nc.tensor.transpose(tr[:, i % 2, kk * P:(kk + 1) * P],
                                                       (cnat_re, cnat_im)[i // 2][:, 4 * (i % 2) + kk], ident[:])
                        last.then_inc(cols_t, 1)
            pe.wait_ge(c_saved, 4)
            rows_to_cols(T_H1, 8, xs, 2, xs_ready)
            ffn(1, Q_FFN1, J_FFN1, T_FFN1)
            rows_to_cols(T_H2, 8, xs, 4, xs_ready)
            def drive(r):
                if r >= 2:
                    pe.wait_ge(bu_read, r - 1)
                p0, k = 32 * (r % 4), r // 4
                for e, bt in enumerate((bt_re, bt_im)):
                    last = mm(misc[:, r % 2, e * T:(e + 1) * T], bt[p0:p0 + 32, k], ut[p0:p0 + 32, k],
                              start=True, stop=True, tile_position=(p0, 0))
                last.then_inc(bu_ready, 1)

            def read_out(r):
                if r == 16:
                    pe.wait_ge(ysum_ready, 1)
                pe.wait_ge(s_ready, r + 1)
                for t in range(TT):
                    for e, ct in enumerate((c_re_t, c_im_t)):
                        last = mm(tr[:, t, 32 * (r % 16):32 * (r % 16) + 32], back[:, r % 2, e, 0, t * P:(t + 1) * P],
                                  ct[:, r], start=(e == 0), stop=(e == 1))
                last.then_inc(y_done, 1)

            for s in range(32):
                j, k = s // 4, s % 4
                if k == 0:
                    pe.wait_ge(job_read[j % 2], J_WIN + j // 2)
                if j == 0:
                    pe.wait_ge(tr_free, T_H2 + 2 * k + 2)
                steps = list(tile_steps(s))

                def middle():
                    if steps:
                        if steps[0]:
                            read_out(steps[0] - 1)
                        if len(steps) > 1 and steps[1] + 2 < NT:
                            drive(steps[1] + 2)

                if steps and steps[0] + 2 < NT:
                    drive(steps[0] + 2)
                quad(Q_WIN + s, 0, h_hi, h_lo, 4 * k, j % 2, k == 0, k == 3, middle)
                if s == 8:
                    rows_to_cols(T_U, 4, u_tok, J_WIN + 1, job_read[1])
                    pe.wait_ge(tr_free, T_U + 4)
                    drive(0)
                    drive(1)
                if len(steps) > 1:
                    read_out(steps[0])
            read_out(NT - 1)
            rows_to_cols(T_YG, 4, u_tok, 2, yg_ready)
            for s in range(4):
                j, k = s // 2, s % 2
                if k == 0:
                    pe.wait_ge(job_read[j], J_GLU)
                if j == 0:
                    pe.wait_ge(tr_free, T_YG + 2 * k + 2)
                quad(Q_GLU + s, 0, yt_hi, yt_lo, 4 * k, j, k == 0, k == 1)
                if s == 0:
                    spread_gate(4)
            spread_gate(5)
            rows_to_cols(T_QK, 4, q_tok, 1, qk_ready)
            spread_gate(6)
            rows_to_cols(T_QK + 4, 4, k_tok, 2, qk_ready)
            spread_gate(7)
            pe.wait_ge(tr_free, T_QK + 8)
            pe.wait_ge(gate_saved, 8)

            def scores(i):
                h, t = i // 2, i % 2
                if i >= 2:
                    pe.wait_ge(sc_read, i - 1)
                for cc in range(2):
                    c0 = HD * cc
                    if cc:
                        pe.wait_ge(sc_half, i + 1)
                    mm(misc[:, i % 2, cc * T:(cc + 1) * T], qt[c0:c0 + HD, h, t * P:(t + 1) * P],
                       kt[c0:c0 + HD, h], start=True, stop=True, tile_position=(c0, 0))\
                        .then_inc((sc_half, sc_ready)[cc], 1)

            def heads_out(i):
                pe.wait_ge(at_ready, i + 1)
                for kk in range(2):
                    last = mm(tr[:, i % 2, T:T + P], at[:, i % 2, kk * P:(kk + 1) * P],
                              v_tok[:, kk, (i // 2) * P:(i // 2 + 1) * P], start=(kk == 0), stop=(kk == 1))
                last.then_inc(o_ready, 1)

            def attend(i):
                if i + 2 < 2 * HEADS:
                    scores(i + 2)
                pe.wait_ge(a_ready, i + 1)
                pe.wait_ge(tr_free, a_bank(i) if i == A_FIRST else a_bank(i) - 1)
                for kk in range(2):
                    last = nc.tensor.transpose(tr[:, i % 2, kk * P:(kk + 1) * P], aw[:, i % 2, kk * P:(kk + 1) * P],
                                               ident[:])
                last.then_inc(tr_written, 1)
                if i not in (0, A_FIRST):
                    heads_out(i - 1)

            scores(0)
            scores(1)
            for i in range(A_FIRST):
                attend(i)
            heads_out(A_FIRST - 1)
            pe.wait_ge(tr_free, T_Y2)
            rows_to_cols(T_Y2, 4, u_tok, 6, xs_ready)
            for s in range(16):
                hj, k = s // 2, 2 * (1 - s // 8) + s % 2
                if s % 2 == 0:
                    pe.wait_ge(job_read[hj % 2], J_OUT + hj // 2)
                if hj == 0:
                    pe.wait_ge(tr_free, T_Y2 + 2 * s + 2)
                if hj == 4:
                    pe.wait_ge(tr_free, T_AO + 2 * (s - 8) + 2)
                steps = attention_steps(s)
                quad(Q_OUT + s, 0, h_hi, h_lo, 4 * k, hj % 2, s % 2 == 0, s % 2 == 1,
                     (lambda: attend(steps[0])) if steps else None)
                if steps:
                    attend(steps[1])
                    if steps[1] == 2 * HEADS - 1:
                        heads_out(steps[1])
                if s == 7:
                    pe.wait_ge(tr_free, T_AO)
                    rows_to_cols(T_AO, 4, ao, 1, ao_ready)
            rows_to_cols(T_H3, 8, xs, 8, xs_ready)
            ffn(2, Q_FFN2, J_FFN2, T_FFN2)


_INS = ["x", "c", "positions", "w_ada", "b_ada", "ffn1_norm", "ffn1_w1", "ffn1_w3", "ffn1_w2", "mix_norm", "w_in",
        "q_norm", "k_norm", "lambda_q1", "lambda_k1", "lambda_q2", "lambda_k2", "attn_subln", "ssm_a_re", "ssm_a_im",
        "ssm_log_dt", "ssm_b_re", "ssm_b_im", "ssm_c_re", "ssm_c_im", "ssm_d", "w_glu", "b_glu", "ssm_out_norm",
        "w_out", "ffn2_norm", "ffn2_w1", "ffn2_w3", "ffn2_w2"]


def kernel(**inputs):
    import numpy as _np
    import concourse.bacc as _bacc
    from concourse import mybir as _mybir
    from concourse.bass_utils import run_bass_kernel_spmd as _run

    nc = _bacc.Bacc("TRN2", target_bir_lowering=False, num_devices=1)
    arrays, args = {}, []
    for name in _INS:
        a = _np.ascontiguousarray(inputs[name])
        arrays[f"in_{name}"] = a
        args.append(nc.dram_tensor(f"in_{name}", a.shape, _mybir.dt.from_np(a.dtype), kind="ExternalInput").ap())
    args.append(nc.dram_tensor("out_x", (1, T, D), _mybir.dt.float32, kind="ExternalOutput").ap())
    build(nc, *args)
    r = _run(nc, [arrays], core_ids=[0])
    return r.results[0]["out_x"]
```

```python
from contextlib import ExitStack

import numpy as np

import concourse.bass as bass
from concourse import mybir

F32 = mybir.dt.float32
F32R = mybir.dt.float32r
I32 = mybir.dt.int32
ACT = mybir.ActivationFunctionType
ALU = mybir.AluOpType
AX = mybir.AxisListType

P = 128
D = 2048
T = 256
TT = T // P
KD = D // P
NB = 512
THIRDS = (4, 4, 3)
AW = 1024
SW = 1024
HEADS = 8
HD = 64
ROT = 16
GROUPS = 64
GC = 16
ST = 64
NT = GROUPS * ST // P
EPS = 1e-6
LAM_INIT = 0.8 - 0.6
ADA_FIRST = 8
ADA_PE_FMA = 4 * ADA_FIRST
NEG = -1e30
MAGIC = 1.5 * 2.0 ** 23
MAGIC16 = 1.5 * 2.0 ** 7
TWO_PI = 2.0 * np.pi
C1 = 6.28125
C2 = float(np.float32(np.floor((TWO_PI - C1) * 2 ** 21) / 2 ** 21))
C3 = float(np.float32(TWO_PI - C1 - C2))
INV_FREQ = [float(v) for v in (np.float32(500000.0) ** (-np.arange(0, 16, 2, dtype=np.float32) / np.float32(16)))]
SIN_SCALE = float(np.nextafter(np.float32(TWO_PI), np.float32(0)))

FFN_QUADS = sum(8 * n + 4 * n for n in THIRDS)
Q_FFN1 = 0
Q_WIN = FFN_QUADS
Q_GLU = Q_WIN + 32
Q_OUT = Q_GLU + 4
Q_FFN2 = Q_OUT + 16
FFN_PAIRS = sum(n + 2 for n in THIRDS)
J_FFN1 = 0
J_WIN = FFN_PAIRS
J_GLU = J_WIN + 4
J_OUT = J_GLU + 1
J_FFN2 = J_OUT + 4
T_H1 = 0
T_FFN1 = 8
T_H2 = T_FFN1 + 2 * sum(THIRDS)
T_U = T_H2 + 8
T_YG = T_U + 4
T_QK = T_YG + 4
T_Y2 = T_QK + 8
T_AO = T_Y2 + 4
A_FIRST = 2
OUT_QUADS = ((0, 2), (1, 2), (0, 3), (1, 3), (2, 2), (2, 3), (3, 2), (3, 3),
             (0, 0), (0, 1), (1, 0), (1, 1), (2, 0), (2, 1), (3, 0), (3, 1))
T_H3 = T_AO + 4
T_FFN2 = T_H3 + 8
FIRST_STEP = 10
XA_OUT = 8 * len(THIRDS)
XA_FFN2 = XA_OUT + 16
SSM_RD = 2
SSM_NF = 11
SMALL_IN = 16 * 17


def hi_count(bank):
    plain = ((T_U, 4), (T_QK, 8))
    return bank - sum(n for start, n in plain if start < bank)


def build(nc, x, c, positions, w_ada, b_ada, ffn1_norm, ffn1_w1, ffn1_w3, ffn1_w2,
          mix_norm, w_in, q_norm, k_norm, lambda_q1, lambda_k1, lambda_q2, lambda_k2,
          attn_subln, ssm_a_re, ssm_a_im, ssm_log_dt, ssm_b_re, ssm_b_im, ssm_c_re,
          ssm_c_im, ssm_d, w_glu, b_glu, ssm_out_norm, w_out,
          ffn2_norm, ffn2_w1, ffn2_w3, ffn2_w2, out):
    ctx = ExitStack()
    with ctx:
        def sb(name, shape, dt=F32):
            return ctx.enter_context(nc.sbuf_tensor(name, [P] + shape, dt))

        def overlay(first, *specs):
            with ExitStack() as s:
                if first:
                    s.enter_context(nc.sbuf_tensor(f"skip_{specs[0][0]}", [P, first // 4], F32))
                return [s.enter_context(nc.sbuf_tensor(n, [P] + shape, dt)) for n, shape, dt in specs]

        def sem(name):
            return ctx.enter_context(nc.semaphore(name))

        X = sb("X", [TT, D])
        raw = sb("raw", [4, 4, NB])
        w_hi = sb("w_hi", [2, 4, NB], F32R)
        w_lo = sb("w_lo", [2, 4, NB], F32R)
        bt_re = sb("bt_re", [8, P])
        bt_im = sb("bt_im", [8, P])
        c_re_t = sb("c_re_t", [NT, 32])
        c_im_t = sb("c_im_t", [NT, 32])
        ident = sb("ident", [P])
        ones = sb("ones", [P])
        iota_t = sb("iota_t", [T])
        cols = sb("cols", [328])
        mod = sb("mod", [144])
        ssm_r = sb("ssm_r", [NT])
        psi = sb("psi", [NT])
        psi_hi = sb("psi_hi", [NT])
        psi_lo = sb("psi_lo", [NT])
        cond = sb("cond", [KD])
        h_scale = sb("h_scale", [KD])
        h_shift = sb("h_shift", [KD])
        gate_col = sb("gate_col", [KD])
        half_pi = sb("half_pi", [1])
        magic = sb("magic", [2])
        ssq = sb("ssq", [TT])
        ssq4 = sb("ssq4", [4, TT])
        rstd = sb("rstd", [TT])
        diag = sb("diag", [NB])
        small = sb("small", [112])
        rope_g = sb("rope_g", [2, 4, TT, 8])
        gain_col = sb("gain_col", [2])
        cs_pos = sb("cs_pos", [2, TT, 8])
        early_mask = diag[:].rearrange("p (t k) -> p t k", t=TT)

        (qt,) = overlay(0, ("qt", [8, T], F32))
        (qk_ss,) = overlay(8 * 1024, ("qk_ss", [64], F32))
        (kt,) = overlay(16 * 1024, ("kt", [8, T], F32))
        h_hi = sb("h_hi", [KD, T], F32R)
        h_lo = sb("h_lo", [KD, T], F32R)

        K = 1024
        gt_hi, gt_lo, s1, g, ada, acc, gate = overlay(
            0, ("gt_hi", [16, T], F32R), ("gt_lo", [16, T], F32R), ("s1", [TT, NB], F32),
            ("g", [TT, NB], F32), ("ada", [2, 4, NB], F32), ("acc", [2, 2, NB], F32), ("gate", [D], F32))
        (xs,) = overlay(0, ("xs", [TT, D], F32))
        rows, bnat_re, bnat_im, bpad_re, bpad_im, prod1, prod2, cnat_re, cnat_im, sc = overlay(
            0, ("rows", [4, P], F32), ("bnat_re", [NT, GC], F32), ("bnat_im", [NT, GC], F32),
            ("bpad_re", [NT, 32], F32), ("bpad_im", [NT, 32], F32), ("prod1", [NT, GC], F32),
            ("prod2", [NT, GC], F32), ("cnat_re", [8, P], F32), ("cnat_im", [8, P], F32), ("sc", [16, NT], F32))
        v_tok, ao, u_tok, q_tok, k_tok, ut = overlay(
            0, ("v_tok", [TT, AW], F32), ("ao", [TT, AW], F32), ("u_tok", [TT, SW], F32),
            ("q_tok", [TT, AW], F32), ("k_tok", [TT, AW], F32), ("ut", [8, T], F32))
        dskip, p1, p2 = overlay(8 * K, ("dskip", [SW], F32), ("p1", [2, T], F32), ("p2", [2, T], F32))
        late_cs, late_zin = overlay(8 * K, ("late_cs", [2, T], F32), ("late_zin", [2, T], F32))
        kp0, xx0, yy0, nf, ab, cs3, zin0, zz, back = overlay(
            48 * K, ("kp0", [T], F32), ("xx0", [T], F32), ("yy0", [T], F32),
            ("nf", [2, T], F32), ("ab", [T], F32), ("cs3", [3, 2, T], F32), ("zin0", [2, T], F32),
            ("zz", [2, T], F32), ("back", [2, 2, 2, T], F32))
        posi, posr, lamv, posf, chunk_c, chunk_r, ang, qkn = overlay(
            12 * K, ("posi", [TT], I32), ("posr", [T], I32), ("lamv", [4, HD], F32), ("posf", [TT], F32),
            ("chunk_c", [TT], F32), ("chunk_r", [T], F32), ("ang", [4, TT, 8], F32), ("qkn", [2, HD], F32))
        (yy1,) = overlay(2 * K, ("yy1", [T], F32))
        kp1, xx1 = overlay(6 * K, ("kp1", [T], F32), ("xx1", [T], F32))
        parts = [(kp0, xx0, yy0), (kp1, xx1, yy1)]
        cs = [cs3[:, 0], cs3[:, 1], cs3[:, 2], late_cs[:]]
        zin = [zin0[:], late_zin[:]]
        (sq,) = overlay(8 * K, ("sq", [TT, AW], F32))
        (yt_hi,) = overlay(40 * K, ("yt_hi", [8, T], F32R))
        (yt_lo,) = overlay(48 * K, ("yt_lo", [8, T], F32R))
        (y_sq,) = overlay(40 * K, ("y_sq", [TT, SW], F32))
        ev_tmp, gsig0, mask, rope_t, bglu_b = overlay(
            48 * K, ("ev_tmp", [2, NB], F32), ("gsig0", [TT, NB], F32), ("mask", [TT, T], F32),
            ("rope_t", [4, P], F32), ("bglu_b", [SW], F32))
        (gsig1,) = overlay(40 * K, ("gsig1", [TT, NB], F32))
        gsig = [gsig0, gsig1]
        sm, pr, aw, at = overlay(
            24 * K, ("sm", [2, 2, T], F32), ("pr", [2, 2, T], F32), ("aw", [2, T], F32), ("at", [2, T], F32))
        (o_sq,) = overlay(58 * K, ("o_sq", [2, P], F32))

        def ps(name, n):
            return ctx.enter_context(nc.psum_tensor(name, [P, n, NB], F32))

        acc_a = ps("acc_a", 2)
        acc_b = ps("acc_b", 2)
        tr = ps("tr", 2)
        misc = ps("misc", 2)
        pairs = [acc_a, acc_b]

        raw_landed = [sem(f"raw_landed{i}") for i in range(4)]
        ada_landed = [sem(f"ada_landed{i}") for i in range(2)]
        rounded = sem("rounded")
        split = sem("split")
        rounded_a = sem("rounded_a")
        split_a = sem("split_a")
        half_used = sem("half_used")
        quads_used = sem("quads_used")
        job_read = [sem("job_a_read"), sem("job_b_read")]
        ada_sum = sem("ada_sum")
        ada_pe = sem("ada_pe")
        ada_fma = sem("ada_fma")
        cols_reduced = sem("cols_reduced")
        mod_saved = sem("mod_saved")
        tr_written = sem("tr_written")
        tr_hi = sem("tr_hi")
        tr_free = sem("tr_free")
        gate_diag = sem("gate_diag")
        gate_bcast = sem("gate_bcast")
        gate_saved = sem("gate_saved")
        x_added = sem("x_added")
        small_in = sem("small_in")
        x_in = sem("x_in")
        out_done = sem("out_done")
        const_ready = sem("const_ready")
        cols_t = sem("cols_t")
        cols_saved = sem("cols_saved")
        c_saved = sem("c_saved")
        b_pad = sem("b_pad")
        dt_spread = sem("dt_spread")
        coef = sem("coef")
        sq_added = sem("sq_added")
        ssum = sem("ssum")
        xs_ready = sem("xs_ready")
        dve_c = sem("dve_chain")
        act_c = sem("act_chain")
        pool_c = sem("pool_chain")
        cond_r = sem("cond_ready")
        gate_cols = sem("gate_cols")
        rms_out = sem("rms_out")
        mix_in = sem("mix_in")
        mix2_in = sem("mix2_in")
        u_scaled = sem("u_scaled")
        parts_ready = sem("parts_ready")
        nf_ready = sem("nf_ready")
        cs_ready = sem("cs_ready")
        bu_ready = sem("bu_ready")
        bu_read = sem("bu_read")
        zin_ready = sem("zin_ready")
        scanned = sem("scanned")
        prods = sem("prods")
        s_ready = sem("s_ready")
        y_done = sem("y_done")
        gain_ones = sem("gain_ones")
        mask_moved = sem("mask_moved")
        sq_ready = sem("sq_ready")
        sq_read = sem("sq_read")
        qk_ready = sem("qk_ready")
        sc_half = sem("sc_half")
        sc_ready = sem("sc_ready")
        sc_read = sem("sc_read")
        mx_ready = sem("mx_ready")
        p_ready = sem("p_ready")
        a_ready = sem("a_ready")
        wt_ready = sem("wt_ready")
        o_done = sem("o_done")
        at_ready = sem("at_ready")
        o_ready = sem("o_ready")
        ang_ready = sem("ang_ready")
        trig_ready = sem("trig_ready")
        lam_in = sem("lam_in")
        lam_ex = sem("lam_ex")
        ao_ready = sem("ao_ready")
        yg_ready = sem("yg_ready")
        ysum_ready = sem("ysum_ready")
        sig_ready = sem("sig_ready")
        y2_ready = sem("y2_ready")

        C_ARE, C_AIM, C_LDT = 0, 32, 64
        C_COND, C_N1, C_N2, C_N3, C_OUTN, C_SUBLN = 96, 112, 128, 144, 160, 168
        C_BADA = 176

        def wv(w):
            return w[0].rearrange("(k p) n -> p k n", p=P)

        ada_v, w1a, w3a, w2a = wv(w_ada), wv(ffn1_w1), wv(ffn1_w3), wv(ffn1_w2)
        w1b, w3b, w2b = wv(ffn2_w1), wv(ffn2_w3), wv(ffn2_w2)
        win_v, glu_v, wout_v = wv(w_in), wv(w_glu), wv(w_out)
        WIN_JOBS = [6, 7, 0, 1, 2, 3, 4, 5]
        x_v = x[0].rearrange("(t p) d -> p t d", p=P)
        out_v = out[0].rearrange("(t p) d -> p t d", p=P)

        def cols512(v, k, n):
            return v[:, 4 * k:4 * k + 4, bass.ds(n * NB, NB)]

        def thirds(q0, j0, t0):
            blk = 0
            for n in THIRDS:
                yield blk, n, q0, q0 + 8 * n, j0, t0
                blk, q0, j0, t0 = blk + n, q0 + 12 * n, j0 + n + 2, t0 + 2 * n

        def in_halves(q):
            return Q_WIN <= q < Q_FFN2

        def looped(eng, n, body):
            body(0)
            if n > 1:
                with eng.Fori(1, n) as i:
                    body(i)

        ADA_DOWN1 = [15, 23, 30]

        def ada_up(layer, t, s, i):
            first = isinstance(i, int)
            if layer == 2:
                slots = [s] if not first else ([2 * s - 8, 2 * s - 7] if s >= 4 else [])
                return [(32, i, x, 0, not first) for x in slots if x < 4] if t == 0 else []
            if t == 0:
                if first:
                    return [(8, 0, s - 4, 0, False)] if s >= 4 else []
                return [(7 + s // 4, 2 * i, s % 4, 1 - s // 4, False)]
            b = (18, 26)[t - 1]
            if first:
                return {3: [(b, 0, 3, 0, False), (b + 1, 0, 0, 1, False)], 7: []}.get(
                    s, [(b, 0, s, 0, False)] if s < 3 else [(b + 1, 0, s - 3, 1, False)])
            return [(b + 1, i, s, 0, True)] if s < 4 else []

        def ada_down(layer, t, s):
            n = THIRDS[t]
            slots = [x for x in range(4 * n - 1) if x == 0 or x % n]
            if layer == 2 or s not in slots:
                return []
            m = slots.index(s)
            b = ADA_DOWN1[t] + m // 4
            return [(b, 0, m % 4, down_buf(t, b), False)]

        def down_buf(t, b):
            return (b + (t == 2)) % 2

        def ada_done_up(layer, t, s, i):
            first = isinstance(i, int)
            if layer == 2:
                return [(32, i, 0)] if t == 0 and s == (6 if first else 4) else []
            if t == 0:
                if first:
                    return []
                return {0: [(6, 2 * i, 0)], 4: [(7, 2 * i, 1)]}.get(s, [])
            b = (18, 26)[t - 1]
            if first:
                return {4: [(b, 0, 0)], 6: [(b + 1, 0, 1)]}.get(s, [])
            return [(b + 1, i, 0)] if s == 4 else []

        def ada_done_down(layer, t, s):
            if layer == 1 and t == 0 and s == 0:
                return [(8 + 2 * THIRDS[0] - 2, 0, 0)]
            ends = (5, 11, 15) if THIRDS[t] == 4 else (5, 11)
            if layer == 1 and s in ends:
                b = ADA_DOWN1[t] + ends.index(s)
                return [(b, 0, down_buf(t, b))]
            return []

        QUADS_IN_H = [{2: 0, 4: 1, 6: 2}, {6: 2}, {6: 2}]

        def attention_steps(s):
            i = A_FIRST + 2 * s
            return [i, i + 1] if A_FIRST <= i < 2 * HEADS else []

        def stat(i):
            return small[:, 96 + 8 * (i % 2):104 + 8 * (i % 2)]

        def tile_steps(s):
            if s < FIRST_STEP:
                return []
            return range((s - FIRST_STEP) * NT // (32 - FIRST_STEP), (s + 1 - FIRST_STEP) * NT // (32 - FIRST_STEP))

        block = ctx.enter_context(nc.Block())

        @block.sync
        def _(sp):
            def load_quad(q, di, src):
                if q >= 4 or not isinstance(di, int):
                    sp.wait_ge(split, q - 3 + di)
                elif q == 0:
                    sp.wait_ge(ada_pe, ADA_FIRST)
                else:
                    sp.wait_ge(ada_fma, 12 * ADA_FIRST - 12 + 4 * q)
                sp.dma_start(raw[:, q % 4], src).then_inc(raw_landed[q % 4], 16)

            def load_ada(b, db, k):
                if 4 * b + k >= 4 * ADA_FIRST + 2 or not isinstance(db, int):
                    sp.wait_ge(ada_fma, 4 * (4 * b + k) - 4 - ADA_PE_FMA + 16 * db)
                sp.dma_start(ada[:, k % 2], cols512(ada_v, k, b + db)).then_inc(ada_landed[k % 2], 16)

            def load_first_ada(b):
                for k in range(4):
                    if not isinstance(b, int):
                        if k == 0:
                            sp.wait_ge(ada_pe, b + 0)
                        else:
                            sp.wait_ge(ada_fma, 12 * b + 4 * k - 12)
                    sp.dma_start(raw[:, k], cols512(ada_v, k, b)).then_inc(raw_landed[k], 16)

            def col(src, r0, n, tile, width=P):
                sp.dma_start(rows[r0:r0 + n, tile, 0:width], src).then_inc(small_in, 16)

            col(c.rearrange("a (k p) -> (a k) p", p=P), 0, 16, 1)
            col(ssm_a_re[0].rearrange("(r g) p -> r (g p)", g=2), 0, 32, 0)
            col(ssm_a_im[0].rearrange("(r g) p -> r (g p)", g=2), 32, 32, 0)
            sp.dma_start(small[64:96, 24:26], ssm_log_dt[0].rearrange("(r g) -> r g", g=2)).then_inc(small_in, 16)
            col(ffn1_norm.rearrange("a (k p) -> (a k) p", p=P), 16, 16, 1)
            col(mix_norm.rearrange("a (k p) -> (a k) p", p=P), 32, 16, 1)
            col(ffn2_norm.rearrange("a (k p) -> (a k) p", p=P), 48, 16, 1)
            col(ssm_out_norm.rearrange("a (k p) -> (a k) p", p=P), 64, 8, 1)
            col(attn_subln, 72, 1, 1)
            ba = b_ada.rearrange("a (k p) -> (a k) p", p=P)
            col(ba[0:128], 0, 128, 2)
            col(ba[128:144], 0, 16, 3)
            for dst, src in ((bnat_re, ssm_b_re), (bnat_im, ssm_b_im)):
                bv = src[0].rearrange("(r g) p c -> (g p) r c", g=2)
                sp.dma_start(dst[:], bv).then_inc(small_in, 16)
            for dst, src in ((cnat_re, ssm_c_re), (cnat_im, ssm_c_im)):
                cv = src[0].rearrange("(j g) c p -> (g c) j p", g=8)
                for h in range(2):
                    sp.dma_start(dst[:, :, 64 * h:64 * h + 64], cv).then_inc(small_in, 16)
            sp.dma_start(X[:], x_v).then_inc(x_in, 16)
            looped(sp, ADA_FIRST, load_first_ada)

            def ffn(layer, q0, j0, t0, w1, w3, w2):
                for t, (blk, n, qu, qd, _, _) in enumerate(thirds(q0, j0, t0)):
                    def up(i):
                        def quads(ss):
                            for s in ss:
                                load_quad(qu + s, 8 * i, cols512((w1, w3)[s // 4], s % 4, blk + i))

                        adas = [a[:3] for s in range(8) for a in ada_up(layer, t, s, i)]
                        if t == 0 and isinstance(i, int):
                            quads(range(4))
                            if layer == 2:
                                sp.wait_ge(x_added, XA_FFN2)
                            for a in adas[:2]:
                                load_ada(*a)
                            quads(range(4, 8))
                            for a in adas[2:]:
                                load_ada(*a)
                        else:
                            for s in range(8):
                                quads([s])
                                if s < len(adas):
                                    load_ada(*adas[s])
                    looped(sp, n, up)
                    for s in range(4 * n):
                        load_quad(qd + s, 0, cols512(w2[:, 4 * blk:4 * (blk + n)], s % n, s // n))
                        for a in ada_down(layer, t, s):
                            load_ada(*a[:3])

            ffn(1, Q_FFN1, J_FFN1, T_FFN1, w1a, w3a, w2a)
            for s in range(32):
                load_quad(Q_WIN + s, 0, cols512(win_v, s % 4, WIN_JOBS[s // 4]))
                if s == 7:
                    sp.wait_ge(tr_free, T_H2 + 8)
                    sp.dma_start(dskip[:], ssm_d.rearrange("a g c -> a (g c)").to_broadcast([P, SW]))\
                        .then_inc(mix_in, 16)
                    sp.dma_start(qkn[:, 0], q_norm.to_broadcast([P, HD])).then_inc(mix2_in, 16)
                    sp.dma_start(qkn[:, 1], k_norm.to_broadcast([P, HD])).then_inc(mix2_in, 16)
                    sp.wait_ge(gain_ones, 1)
                    for w, gain in enumerate((q_norm, k_norm)):
                        for p0 in (ROT, HD + ROT):
                            sp.dma_start(gain_col[p0:p0 + HD - ROT, w:w + 1],
                                         gain[:, ROT:HD].rearrange("a d -> d a")).then_inc(mix2_in, 16)
                    for i, v in enumerate((lambda_q1, lambda_k1, lambda_q2, lambda_k2)):
                        sp.dma_start(lamv[:, i], v.to_broadcast([P, HD])).then_inc(mix2_in, 16)
                    sp.dma_start(posi[:], positions.rearrange("a (t p) -> p (a t)", p=P),
                                 allow_slow_non_contiguous=True).then_inc(mix2_in, 16)
                    sp.dma_start(posr[:], positions.to_broadcast([P, T])).then_inc(mix2_in, 16)
            for s in range(4):
                load_quad(Q_GLU + s, 0, cols512(glu_v, s % 2, s // 2))
            sp.wait_ge(ysum_ready, 2)
            sp.dma_start(bglu_b[:], b_glu.to_broadcast([P, SW])).then_inc(mix2_in, 16)
            for s in range(16):
                load_quad(Q_OUT + s, 0, cols512(wout_v, OUT_QUADS[s][1], OUT_QUADS[s][0]))
            ffn(2, Q_FFN2, J_FFN2, T_FFN2, w1b, w3b, w2b)
            for n in range(4):
                sp.wait_ge(x_added, XA_FFN2 + 16 + 2 * n + 2)
                sp.dma_start(out_v[:, :, n * NB:(n + 1) * NB], X[:, :, n * NB:(n + 1) * NB]).then_inc(out_done, 16)
            sp.wait_ge(out_done, 64)

        @block.scalar
        def _(act):
            def round_quad(q, di):
                act.wait_ge(raw_landed[q % 4], 16 * (ADA_FIRST + q // 4 + 1) + 4 * di)
                if in_halves(q):
                    for hf, done in enumerate((rounded_a, rounded)):
                        if hf == 0 and in_halves(q - 2):
                            act.wait_ge(half_used, q - 2 - Q_WIN + 1)
                        else:
                            act.wait_ge(quads_used, q - 1)
                        ks = slice(2 * hf, 2 * hf + 2)
                        nc.scalar.activation(w_hi[:, q % 2, ks], raw[:, q % 4, ks], ACT.Copy).then_inc(done, 1)
                    return
                if q >= 2 or not isinstance(di, int):
                    act.wait_ge(quads_used, q - 1 + di)
                nc.scalar.activation(w_hi[:, q % 2], raw[:, q % 4], ACT.Copy).then_inc(rounded, 1)

            def save_mod(b, db):
                act.wait_ge(cols_reduced, b + db + 1)
                bank = b % 2 if isinstance(db, int) and b < ADA_FIRST else 0
                nc.scalar.activation(mod[:, bass.ds(4 * b + 4 * db, 4)], misc[:, bank, 0:4], ACT.Copy)\
                    .then_inc(mod_saved, 1)

            sums = [0]

            def square(dst, src, total):
                sums[0] += 1
                nc.scalar.activation(dst, src, ACT.Square, accum_out=total).then_inc(ssum, 1)

            def h_norm(added, blocks):
                for n in blocks:
                    if added:
                        act.wait_ge(x_added, added - 2 * (3 - n))
                    else:
                        act.wait_ge(x_in, 16)
                    for t in range(TT):
                        if n:
                            act.wait_ge(ssum, sums[0] - 1)
                        square(s1[:, t], X[:, t, n * NB:(n + 1) * NB], ssq4[:, n, t:t + 1])

            def hi_scaled(bank, m, hi, k0, scale, bias):
                act.wait_ge(tr_written, bank + 1)
                for kk in range(2):
                    k = 2 * m + kk
                    last = nc.scalar.activation(hi[:, k0 + k], tr[:, bank % 2, kk * T:(kk + 1) * T], ACT.Identity,
                                                bias=bias(k), scale=scale(k))
                last.then_inc(tr_hi, 1)

            def hi_plain(bank, dst):
                act.wait_ge(tr_written, bank + 1)
                nc.scalar.activation(dst, tr[:, bank % 2], ACT.Copy).then_inc(tr_hi, 1)

            def h_make(sub, bank0, q0):
                act.wait_ge(coef, sub + 1)
                for m in range(8):
                    if m in QUADS_IN_H[sub]:
                        round_quad(q0 + QUADS_IN_H[sub][m], 0)
                    hi_scaled(bank0 + m, m, h_hi, 0, lambda k: h_scale[:, k:k + 1], lambda k: h_shift[:, k:k + 1])
                round_quad(q0 + 3, 0)

            def hi_gt(bank, dk, b):
                act.wait_ge(tr_written, bank[0] + b + 1 + bank[1])
                nc.scalar.activation(gt_hi[:, bass.ds(4 * dk + 2 * b, 2)].rearrange("p k t -> p (k t)"),
                                     tr[:, b], ACT.Copy).then_inc(tr_hi, 1)

            def save_gate(gg, n):
                act.wait_ge(gate_bcast, gg + 1)
                nc.scalar.activation(gate[:, n * NB:(n + 1) * NB], misc[:, 1], ACT.Copy).then_inc(gate_saved, 1)

            def ffn(layer, q0, j0, t0):
                for t, (blk, n, qu, qd, jp, tb) in enumerate(thirds(q0, j0, t0)):
                    def silu(i):
                        act.wait_ge(quads_used, qu + 4 + 8 * i)
                        if jp or not isinstance(i, int):
                            act.wait_ge(job_read[1], jp + i)
                        nc.scalar.activation(s1[:], acc_a[:], ACT.Silu).then_inc(job_read[0], 1)

                    def up(i):
                        peeled = isinstance(i, int)
                        for s in range(8):
                            if not (t == 0 and peeled and s < 4):
                                round_quad(qu + s, 8 * i)
                            if s == 1 and peeled and t:
                                for b, db, _ in ada_done_down(layer, t - 1, 4 * THIRDS[t - 1] - 1):
                                    save_mod(b, db)
                            if s == 2 and not peeled:
                                for b in range(2):
                                    hi_gt((tb, 2 * i - 2), i - 1, b)
                            if s == 5:
                                silu(i)
                            for b, db, _ in ada_done_up(layer, t, s - 1, i):
                                save_mod(b, db)
                    looped(act, n, up)
                    for s in range(4 * n):
                        round_quad(qd + s, 0)
                        if s == 2:
                            for b in range(2):
                                hi_gt((tb, 2 * n - 2), n - 1, b)
                        for b, db, _ in ada_done_down(layer, t, s - 1):
                            save_mod(b, db)
                        if t == 0 and s % n == 1:
                            save_gate((0, 8)[layer - 1] + s // n, s // n)
                    if layer == 1 and t == 2:
                        h_norm(XA_OUT, range(3))

            def save_proj(j):
                act.wait_ge(quads_used, Q_WIN + 4 * j + 4)
                dst = (u_tok, q_tok, k_tok, v_tok)[j // 2][:, :, (j % 2) * NB:(j % 2 + 1) * NB]
                nc.scalar.activation(dst, pairs[j % 2][:], ACT.Copy).then_inc(job_read[j % 2], 1)

            def copy_bank(bank, dst):
                act.wait_ge(tr_written, bank + 1)
                nc.scalar.activation(dst, tr[:, bank % 2], ACT.Copy).then_inc(tr_free, 1)

            for i, (c0, n) in enumerate(((0, 96), (96, 73), (C_BADA, 128), (C_BADA + 128, 16))):
                act.wait_ge(cols_t, i + 1)
                nc.scalar.activation(cols[:, c0:c0 + n], tr[:, i % 2, 0:n], ACT.Copy).then_inc(cols_saved, 1)
                if i == 1:
                    act.wait_ge(cols_saved, 2)
                    nc.scalar.activation(cond[:], cols[:, C_COND:C_COND + 16], ACT.Silu).then_inc(cond_r, 1)
            act.wait_ge(cols_saved, 2)
            nc.scalar.activation(sc[:, 0], cols[:, C_LDT:C_LDT + 32], ACT.Exp).then_inc(act_c, 1)
            save_mod(0, 0)
            act.wait_ge(dve_c, SSM_RD)
            nc.scalar.activation(ssm_r[:], sc[:, 1], ACT.Exp).then_inc(act_c, 1)
            act.wait_ge(dve_c, SSM_NF)
            nc.scalar.activation(sc[:, 5], sc[:, 4], ACT.Abs).then_inc(act_c, 1)
            nc.scalar.activation(sc[:, 6], sc[:, 4], ACT.Sin, scale=-SIN_SCALE).then_inc(act_c, 1)
            act.wait_ge(act_c, 3)
            nc.scalar.activation(sc[:, 7], sc[:, 5], ACT.Sin, scale=-SIN_SCALE, bias=half_pi[:, 0:1])\
                .then_inc(act_c, 1)
            save_mod(1, 0)
            save_mod(2, 0)
            for i in range(8):
                act.wait_ge(cols_t, 4 + i + 1)
                dst = (bt_re, bt_im)[i // 4][:, 2 * (i % 4):2 * (i % 4) + 2].rearrange("p a b -> p (a b)")
                nc.scalar.activation(dst, tr[:, i % 2, 0:256], ACT.Copy).then_inc(cols_saved, 1)
            h_norm(0, range(4))
            for b in range(3, ADA_FIRST):
                save_mod(b, 0)
            h_make(0, T_H1, Q_FFN1)
            ffn(1, Q_FFN1, J_FFN1, T_FFN1)
            round_quad(Q_WIN, 0)
            for b, db, _ in ada_done_down(1, 2, 4 * THIRDS[2] - 1):
                save_mod(b, db)
            h_norm(XA_OUT, [3])
            round_quad(Q_WIN + 1, 0)
            h_make(1, T_H2, Q_WIN)

            steps = [5]

            def step(ins):
                steps[0] += 1
                ins.then_inc(act_c, 1)

            def phase_parts(r):
                kp, xx, yy = parts[r % 2]
                if r >= 2:
                    act.wait_ge(nf_ready, r - 1)
                step(nc.scalar.activation(kp[:], iota_t[:], ACT.Identity, scale=psi[:, r:r + 1], bias=magic[:, 0:1]))
                nc.scalar.activation(xx[:], iota_t[:], ACT.Copy, scale=psi_hi[:, r:r + 1])
                nc.scalar.activation(yy[:], iota_t[:], ACT.Copy, scale=psi_lo[:, r:r + 1])
                act.wait_ge(act_c, steps[0])
                nc.scalar.activation(kp[:], kp[:], ACT.Identity, bias=magic[:, 1:2]).then_inc(parts_ready, 1)

            def angles():
                act.wait_ge(ang_ready, 1)
                nc.scalar.activation(cs_pos[:, 1], ang[:, 0], ACT.Sin, scale=-SIN_SCALE)
                step(nc.scalar.activation(ang[:, 1], ang[:, 0], ACT.Abs))
                act.wait_ge(act_c, steps[0])
                nc.scalar.activation(cs_pos[:, 0], ang[:, 1], ACT.Sin, scale=-SIN_SCALE, bias=half_pi[:, 0:1])\
                    .then_inc(trig_ready, 1)
                act.wait_ge(lam_in, 1)
                nc.scalar.activation(small[:, 2:4], small[:, 0:2], ACT.Exp).then_inc(lam_ex, 1)

            def cos_sin(r):
                act.wait_ge(nf_ready, r + 1)
                if r:
                    act.wait_ge(cs_ready, r)
                if r == 3:
                    act.wait_ge(u_scaled, 1)
                if r >= 4:
                    act.wait_ge(prods, r - 3)
                step(nc.scalar.activation(ab[:], nf[:, r % 2], ACT.Abs))
                nc.scalar.activation(cs[r % 4][:, 1], nf[:, r % 2], ACT.Sin, scale=-SIN_SCALE)
                act.wait_ge(act_c, steps[0])
                nc.scalar.activation(cs[r % 4][:, 0], ab[:], ACT.Sin, scale=-SIN_SCALE, bias=half_pi[:, 0:1])\
                    .then_inc(cs_ready, 1)

            def gelu(hf):
                act.wait_ge(ysum_ready, hf + 1)
                yv = u_tok[:, :, hf * NB:(hf + 1) * NB]
                nc.scalar.activation(yv, yv, ACT.Gelu_apprx_tanh).then_inc(yg_ready, 1)

            for s in range(33):
                if s == 9:
                    save_proj(1)
                if s >= 4:
                    round_quad(Q_WIN + s, 0)
                if s % 4 == 1 and s > 4 and s != 9:
                    save_proj(s // 4 - 1)
                if s == 9:
                    for m in range(4):
                        copy_bank(T_U + m, ut[:, 2 * m:2 * m + 2].rearrange("p k t -> p (k t)"))
                if s == 4:
                    phase_parts(0)
                    phase_parts(1)
                if s in (5, 6):
                    cos_sin(s - 5)
                    phase_parts(s - 3)
                if s == 8:
                    angles()
                for r in tile_steps(s - 1):
                    if r + 2 < NT:
                        cos_sin(r + 2)
                    if r + 4 < NT:
                        phase_parts(r + 4)
                    if r == 20:
                        gelu(0)
            round_quad(Q_GLU + 1, 0)

            def squares(w, tok):
                for t in range(TT):
                    if w:
                        act.wait_ge(sq_read, t + 1)
                    nc.scalar.activation(sq[:, t], tok[:, t], ACT.Square).then_inc(sq_ready, 1)

            act.wait_ge(prods, NT)
            squares(0, q_tok)
            gelu(1)
            nc.scalar.activation(mask[:], early_mask, ACT.Copy).then_inc(mask_moved, 1)
            save_proj(7)
            for m in range(4):
                hi_plain(T_YG + m, yt_hi[:, 2 * m:2 * m + 2].rearrange("p k t -> p (k t)"))
            squares(1, k_tok)

            def sigmoid(j):
                act.wait_ge(job_read[j], J_GLU + 1)
                nc.scalar.activation(gsig[j][:], gsig[j][:], ACT.Sigmoid).then_inc(sig_ready, 1)

            round_quad(Q_GLU + 2, 0)
            save_gate(4, 0)
            round_quad(Q_GLU + 3, 0)
            save_gate(5, 1)

            def copy_qk(w):
                for m in range(4):
                    bank = T_QK + 4 * w + m
                    act.wait_ge(tr_written, bank + 1)
                    nc.scalar.activation((qt, kt)[w][:, 2 * m:2 * m + 2].rearrange("p k t -> p (k t)"),
                                         tr[:, bank % 2], ACT.Copy, scale=gain_col[:, w:w + 1]).then_inc(tr_free, 1)

            copy_qk(0)
            sigmoid(0)
            sigmoid(1)
            save_gate(6, 2)
            copy_qk(1)
            save_gate(7, 3)

            def exps(i):
                act.wait_ge(mx_ready, i + 1)
                st = stat(i)
                for cc in range(2):
                    last = nc.scalar.activation(pr[:, i % 2, cc], sm[:, i % 2, cc], ACT.Exp, bias=st[:, cc:cc + 1],
                                                accum_out=st[:, 2 + cc:3 + cc])
                last.then_inc(p_ready, 1)

            def output(i):
                h, t = i // 2, i % 2
                act.wait_ge(o_ready, i + 1)
                nc.scalar.activation(o_sq[:, i % 2], tr[:, i % 2, T:T + P], ACT.Square,
                                     accum_out=small[:, 32 + 8 * t + h:33 + 8 * t + h])
                nc.scalar.activation(ao[:, t, h * P:(h + 1) * P], tr[:, i % 2, T:T + P], ACT.Copy).then_inc(o_done, 1)

            def attend(i, before=None):
                if before:
                    before()
                if i + 1 < 2 * HEADS:
                    exps(i + 1)
                act.wait_ge(wt_ready, i + 1)
                if i >= 2:
                    act.wait_ge(o_ready, i - 1)
                nc.scalar.activation(at[:, i % 2], tr[:, i % 2, 0:T], ACT.Copy).then_inc(at_ready, 1)
                if i not in (0, 2, 4):
                    output(i - 1)
                if i in (1, 3, 2 * HEADS - 1):
                    output(i)

            def y_hi(m):
                hi_scaled(T_Y2 + m, m, h_hi, 8, lambda k: cols[:, C_OUTN + k:C_OUTN + k + 1],
                          lambda k: small[:, 20:21])

            act.wait_ge(y2_ready, 2)
            for t in range(TT):
                square(y_sq[:, t], u_tok[:, t], ssq[:, t:t + 1])
            exps(0)
            y_hi(0)
            y_hi(1)
            attend(0, lambda: round_quad(Q_OUT, 0))
            attend(1)
            for s in range(8):
                steps = attention_steps(s)
                if steps:
                    attend(steps[0], lambda: round_quad(Q_OUT + s + 1, 0))
                    attend(steps[1])
                else:
                    round_quad(Q_OUT + s + 1, 0)
                if s == 0:
                    y_hi(2)
                    y_hi(3)
            for m in range(4):
                bank = T_AO + m
                act.wait_ge(tr_written, bank + 1)
                nc.scalar.activation(h_hi[:, 2 * m:2 * m + 2].rearrange("p k t -> p (k t)"), tr[:, bank % 2], ACT.Copy,
                                     scale=small[:, 16:17]).then_inc(tr_hi, 1)
            for s in range(9, 16):
                round_quad(Q_OUT + s, 0)
            h_norm(XA_FFN2, range(3))
            round_quad(Q_FFN2, 0)
            h_norm(XA_FFN2, [3])
            round_quad(Q_FFN2 + 1, 0)
            h_make(2, T_H3, Q_FFN2)
            ffn(2, Q_FFN2, J_FFN2, T_FFN2)

        @block.vector
        def _(dve):
            chain = [0]
            rms = [0]
            added = [0]
            v = nc.vector

            def link(ins):
                chain[0] += 1
                ins.then_inc(dve_c, 1)
                dve.wait_ge(dve_c, chain[0])

            def split_quad(q, di):
                if in_halves(q):
                    for hf, (ready, done) in enumerate(((rounded_a, split_a), (rounded, split))):
                        dve.wait_ge(ready, q + 1 if hf else q - Q_WIN + 1)
                        if hf == 0 and in_halves(q - 2):
                            dve.wait_ge(half_used, q - 2 - Q_WIN + 1)
                        else:
                            dve.wait_ge(quads_used, q - 1)
                        ks = slice(2 * hf, 2 * hf + 2)
                        v.tensor_tensor(w_lo[:, q % 2, ks], raw[:, q % 4, ks], w_hi[:, q % 2, ks].bitcast(F32),
                                        ALU.subtract).then_inc(done, 1)
                    return
                dve.wait_ge(rounded, q + 1 + di)
                if q >= 2 or not isinstance(di, int):
                    dve.wait_ge(quads_used, q - 1 + di)
                v.tensor_tensor(w_lo[:, q % 2], raw[:, q % 4], w_hi[:, q % 2].bitcast(F32), ALU.subtract)\
                    .then_inc(split, 1)

            def ada_quad(b, db, k, buf, strict=False):
                early = isinstance(db, int) and b < ADA_FIRST
                if early:
                    src = raw[:, k]
                    dve.wait_ge(raw_landed[k], 16 * (b + 1))
                else:
                    src = ada[:, k % 2]
                    dve.wait_ge(ada_landed[k % 2], 16 * (2 * (b - ADA_FIRST) + k // 2 + 1) + 32 * db)
                if k == (1 if early else 0) and b >= 2:
                    dve.wait_ge(cols_reduced, b + db if strict else b - 1 + db)
                first = 4 if early else 0
                before = 12 * b - first if early else 16 * b - ADA_PE_FMA
                for kk in range(4):
                    n = 4 * k + kk
                    dst, w, s = acc[:, buf, n % 2], src[:, kk], cond[:, n:n + 1]
                    if n < first + 2:
                        ins = v.tensor_scalar(dst, w, s, None, ALU.mult)
                    else:
                        dve.wait_ge(ada_fma, before + 16 * db + n - 1)
                        ins = v.scalar_tensor_tensor(dst, w, s, dst, ALU.mult, ALU.add)
                    ins.then_inc(ada_fma, 1)
                if k == 3:
                    dve.wait_ge(ada_fma, before + 16 * db + 16)
                    v.tensor_tensor(acc[:, buf, 0], acc[:, buf, 0], acc[:, buf, 1], ALU.add).then_inc(ada_sum, 1)

            def coefficients(sub, norm_c):
                dve.wait_ge(mod_saved, 12 * sub + 8)
                s0 = 48 * sub
                v.tensor_tensor(h_shift[:], mod[:, s0:s0 + 16], cols[:, C_BADA + s0:C_BADA + s0 + 16], ALU.add)
                link(v.tensor_tensor(gate_col[:], mod[:, s0 + 16:s0 + 32],
                                     cols[:, C_BADA + s0 + 16:C_BADA + s0 + 32], ALU.add))
                v.scalar_tensor_tensor(h_scale[:], gate_col[:], 1.0, cols[:, norm_c:norm_c + 16], ALU.add, ALU.mult)\
                    .then_inc(coef, 1)
                dve.wait_ge(coef, sub + 1)

            def h_norm():
                rms[0] += 1
                dve.wait_ge(rms_out, rms[0])
                for c in range(0, D, D // 2):
                    for t in range(TT):
                        v.tensor_scalar(xs[:, t, c:c + D // 2], X[:, t, c:c + D // 2], rstd[:, t:t + 1], None,
                                        ALU.mult).then_inc(xs_ready, 1)

            def y_norm():
                for t in range(TT):
                    rms[0] += 1
                    dve.wait_ge(rms_out, rms[0])
                    v.tensor_scalar(u_tok[:, t], u_tok[:, t], rstd[:, t:t + 1], None, ALU.mult).then_inc(xs_ready, 1)

            def lo_scaled(bank, m, hi, lo, k0, scale, bias, tmp):
                dve.wait_ge(tr_hi, hi_count(bank) + 1)
                for kk in range(2):
                    k = 2 * m + kk
                    ins = v.tensor_scalar(tmp[:, m % 2, kk * T:(kk + 1) * T], tr[:, bank % 2, kk * T:(kk + 1) * T],
                                          scale(k), bias(k), ALU.mult, ALU.add)
                link(ins)
                v.tensor_tensor(lo[:, k0 + 2 * m:k0 + 2 * m + 2].rearrange("p k t -> p (k t)"), tmp[:, m % 2],
                                hi[:, k0 + 2 * m:k0 + 2 * m + 2].rearrange("p k t -> p (k t)").bitcast(F32),
                                ALU.subtract).then_inc(tr_free, 1)

            def lo_plain(bank, hi, lo):
                dve.wait_ge(tr_hi, hi_count(bank) + 1)
                v.tensor_tensor(lo, tr[:, bank % 2], hi.bitcast(F32), ALU.subtract).then_inc(tr_free, 1)

            def h_make(sub, bank0, q0):
                for m in range(8):
                    if m in QUADS_IN_H[sub]:
                        split_quad(q0 + QUADS_IN_H[sub][m], 0)
                    lo_scaled(bank0 + m, m, h_hi, h_lo, 0, lambda k: h_scale[:, k:k + 1],
                              lambda k: h_shift[:, k:k + 1], s1)
                split_quad(q0 + 3, 0)

            def lo_gt(bank, dk, b):
                dve.wait_ge(tr_hi, hi_count(bank[0]) + b + 1 + bank[1])
                dst = bass.ds(4 * dk + 2 * b, 2)
                v.tensor_tensor(gt_lo[:, dst].rearrange("p k t -> p (k t)"), tr[:, b],
                                gt_hi[:, dst].rearrange("p k t -> p (k t)").bitcast(F32), ALU.subtract)\
                    .then_inc(tr_free, 1)

            def add_x(pair, pi, job_quads, n, gsem):
                dve.wait_ge(quads_used, job_quads)
                if gsem is not None:
                    dve.wait_ge(gate_saved, gsem)
                if added[0]:
                    dve.wait_ge(x_added, added[0])
                added[0] += TT
                for t in range(TT):
                    ins = v.tensor_tensor(g[:, t], pairs[pair][:, t], gate[:, n * NB:(n + 1) * NB], ALU.mult)
                ins.then_inc(job_read[pair], 1)
                dve.wait_ge(job_read[pair], pi + 1)
                for t in range(TT):
                    xn = X[:, t, n * NB:(n + 1) * NB]
                    v.tensor_tensor(xn, xn, g[:, t], ALU.add).then_inc(x_added, 1)

            def gate_column(sub, factor):
                dve.wait_ge(mod_saved, 12 * sub + 12)
                s0 = 48 * sub + 32
                link(v.tensor_tensor(gate_col[:], mod[:, s0:s0 + 16], cols[:, C_BADA + s0:C_BADA + s0 + 16], ALU.add))
                v.tensor_scalar(gate_col[:], gate_col[:], factor, None, ALU.mult).then_inc(gate_cols, 1)

            def ffn(layer, q0, j0, t0):
                for t, (blk, n, qu, qd, jp, tb) in enumerate(thirds(q0, j0, t0)):
                    def hidden(i, m):
                        dve.wait_ge(quads_used, qu + 8 + 8 * m)
                        dve.wait_ge(job_read[0], jp + m + 1)
                        dve.wait_ge(tr_written, tb + 2 * m)
                        v.tensor_tensor(g[:], s1[:], acc_b[:], ALU.mult).then_inc(job_read[1], 1)

                    def up(i):
                        peeled = isinstance(i, int)
                        for s in range(8):
                            if s == 1 and not peeled:
                                hidden(i, i - 1)
                            if not (t == 0 and peeled and s < 4):
                                split_quad(qu + s, 8 * i)
                            if s == 2 and not peeled:
                                for b in range(2):
                                    lo_gt((tb, 2 * i - 2), i - 1, b)
                            if s == 0 and peeled and t:
                                add_x(*last_add)
                            for a in ada_up(layer, t, s, i):
                                ada_quad(*a)
                    looped(dve, n, up)
                    if t == 0:
                        gate_column(2 * (layer - 1), 0.5)
                    for s in range(4 * n):
                        if s == 1:
                            hidden(None, n - 1)
                        split_quad(qd + s, 0)
                        if s == 2:
                            for b in range(2):
                                lo_gt((tb, 2 * n - 2), n - 1, b)
                        if s % n == 0 and s:
                            j = s // n - 1
                            add_x(j % 2, jp + n + j // 2, qd + n * (j + 1), j,
                                  ((0, 8)[layer - 1] + j + 1) if t == 0 else None)
                        for a in ada_down(layer, t, s):
                            ada_quad(*a)
                    last_add = (1, jp + n + 1, qd + 4 * n, 3, ((0, 8)[layer - 1] + 4) if t == 0 else None)
                    if t == 2:
                        add_x(*last_add)

            v.memset(half_pi[:], float(np.pi / 2))
            v.memset(magic[:, 0:1], MAGIC)
            v.memset(gain_col[:], 1.0).then_inc(gain_ones, 1)
            v.memset(magic[:, 1:2], -MAGIC)
            dve.wait_ge(small_in, SMALL_IN)
            v.tensor_copy(rows[64:96, 0].rearrange("p (g s) -> p g s", g=2),
                          small[64:96, 24:26].unsqueeze(2).to_broadcast([32, 2, ST])).then_inc(dt_spread, 1)
            dve.wait_ge(cond_r, 1)

            def ssm_rates():
                dve.wait_ge(act_c, 1)
                link(v.tensor_scalar(sc[:, 2], cols[:, C_ARE:C_ARE + 32], -1e-4, None, ALU.min))
                link(v.tensor_tensor(sc[:, 1], sc[:, 2], sc[:, 0], ALU.mult))
                assert chain[0] == SSM_RD
                link(v.tensor_tensor(sc[:, 3], cols[:, C_AIM:C_AIM + 32], sc[:, 0], ALU.mult))
                link(v.tensor_scalar(sc[:, 8], sc[:, 3], float(1 / TWO_PI), MAGIC, ALU.mult, ALU.add))
                link(v.tensor_scalar(sc[:, 8], sc[:, 8], MAGIC, None, ALU.subtract))
                for cst in (C1, C2, C3):
                    link(v.scalar_tensor_tensor(sc[:, 3], sc[:, 8], -cst, sc[:, 3], ALU.mult, ALU.add))
                link(v.tensor_scalar(psi[:], sc[:, 3], float(1 / TWO_PI), None, ALU.mult))
                link(v.tensor_scalar(sc[:, 4], psi[:], -1.0, None, ALU.mult))
                link(v.tensor_scalar(sc[:, 4], sc[:, 4], 0.5, -0.5, ALU.min, ALU.max))
                assert chain[0] == SSM_NF
                link(v.tensor_scalar(psi_hi[:], psi[:], MAGIC16, None, ALU.add))
                link(v.tensor_scalar(psi_hi[:], psi_hi[:], MAGIC16, None, ALU.subtract))
                link(v.tensor_tensor(psi_lo[:], psi[:], psi_hi[:], ALU.subtract))

            def ssm_f():
                dve.wait_ge(act_c, 5)
                link(v.tensor_tensor(sc[:, 9], ssm_r[:], sc[:, 7], ALU.mult))
                link(v.tensor_scalar(sc[:, 9], sc[:, 9], 1.0, None, ALU.subtract))
                link(v.tensor_tensor(sc[:, 10], ssm_r[:], sc[:, 6], ALU.mult))
                link(v.tensor_tensor(sc[:, 11], sc[:, 2], sc[:, 2], ALU.mult))
                aim = cols[:, C_AIM:C_AIM + 32]
                link(v.tensor_tensor(sc[:, 12], aim, aim, ALU.mult))
                link(v.tensor_tensor(sc[:, 11], sc[:, 11], sc[:, 12], ALU.add))
                link(v.reciprocal(sc[:, 11], sc[:, 11]))
                link(v.tensor_tensor(sc[:, 12], sc[:, 9], sc[:, 2], ALU.mult))
                link(v.tensor_tensor(sc[:, 13], sc[:, 10], aim, ALU.mult))
                link(v.tensor_tensor(sc[:, 12], sc[:, 12], sc[:, 13], ALU.add))
                link(v.tensor_tensor(sc[:, 14], sc[:, 12], sc[:, 11], ALU.mult))
                link(v.tensor_tensor(sc[:, 12], sc[:, 10], sc[:, 2], ALU.mult))
                link(v.tensor_tensor(sc[:, 13], sc[:, 9], aim, ALU.mult))
                link(v.tensor_tensor(sc[:, 12], sc[:, 12], sc[:, 13], ALU.subtract))
                link(v.tensor_tensor(sc[:, 15], sc[:, 12], sc[:, 11], ALU.mult))

            def ssm_b():
                dve.wait_ge(small_in, SMALL_IN)
                dve.wait_ge(b_pad, 2)
                fr = sc[:, 14].unsqueeze(2).to_broadcast([P, NT, GC])
                fi = sc[:, 15].unsqueeze(2).to_broadcast([P, NT, GC])
                link(v.tensor_tensor(prod1[:], bnat_re[:], fr, ALU.mult))
                link(v.tensor_tensor(prod2[:], bnat_im[:], fi, ALU.mult))
                for h in range(2):
                    hp, hc = slice(64 * h, 64 * h + 64), slice(GC * h, GC * h + GC)
                    link(v.tensor_tensor(bpad_re[hp, :, hc], prod1[hp], prod2[hp], ALU.subtract))
                link(v.tensor_tensor(prod1[:], bnat_im[:], fr, ALU.mult))
                link(v.tensor_tensor(prod2[:], bnat_re[:], fi, ALU.mult))
                for h in range(2):
                    hp, hc = slice(64 * h, 64 * h + 64), slice(GC * h, GC * h + GC)
                    ins = v.tensor_tensor(bpad_im[hp, :, hc], prod1[hp], prod2[hp], ALU.add)
                ins.then_inc(b_pad, 1)

            def ssm_c(i0):
                dve.wait_ge(const_ready, 2)
                for i in (i0, i0 + 1):
                    dve.wait_ge(cols_t, 12 + i + 1)
                    dst = (c_re_t, c_im_t)[i // 2]
                    sgn = (1.0, -1.0)[i // 2]
                    src = tr[:, i % 2].rearrange("p (r g c) -> p r g c", g=2, c=GC)
                    for h in range(2):
                        hp, hc = slice(64 * h, 64 * h + 64), slice(GC * h, GC * h + GC)
                        ins = v.tensor_scalar(dst[hp, 16 * (i % 2):16 * (i % 2) + 16, hc], src[hp, :, h], sgn, None, ALU.mult)
                    ins.then_inc(c_saved, 1)


            for b in range(ADA_FIRST):
                for k in range(1, 4):
                    ada_quad(b, 0, k, b % 2)
                if b < 3:
                    (ssm_rates, ssm_f, ssm_b)[b]()
                if b in (4, 5):
                    ssm_c(2 * (b - 4))
                if b == 6:
                    h_norm()
            coefficients(0, C_N1)
            h_make(0, T_H1, Q_FFN1)
            ffn(1, Q_FFN1, J_FFN1, T_FFN1)
            coefficients(1, C_N2)
            split_quad(Q_WIN, 0)
            h_norm()
            split_quad(Q_WIN + 1, 0)
            h_make(1, T_H2, Q_WIN)
            gate_column(1, 1.0)

            def turn(r):
                dve.wait_ge(bu_ready, r + 1)
                dve.wait_ge(cs_ready, r + 1)
                bu = misc[:, r % 2].rearrange("p (a t) -> p a t", a=2)
                csr = cs[r % 4]
                if r:
                    dve.wait_ge(zin_ready, r)
                v.tensor_tensor(p1[:], csr, bu, ALU.mult)
                v.tensor_tensor(p2[:, 0], csr[:, 0], bu[:, 1], ALU.mult)
                v.tensor_tensor(p2[:, 1], csr[:, 1], bu[:, 0], ALU.mult).then_inc(bu_read, 1)

            def scan_input(r):
                dve.wait_ge(bu_read, r + 1)
                if r == 1:
                    dve.wait_ge(u_scaled, 1)
                if r >= 2:
                    dve.wait_ge(scanned, r - 1)
                zi = zin[r % 2]
                v.tensor_tensor(zi[:, 0], p1[:, 0], p1[:, 1], ALU.add)
                v.tensor_tensor(zi[:, 1], p2[:, 0], p2[:, 1], ALU.subtract).then_inc(zin_ready, 1)

            def scan(r):
                dve.wait_ge(zin_ready, r + 1)
                if r:
                    dve.wait_ge(prods, r)
                rad = ssm_r[:, r:r + 1].to_broadcast([P, T])
                v.tensor_tensor_scan(zz[:, 0], rad, zin[r % 2][:, 0], 0.0, ALU.mult, ALU.add)
                v.tensor_tensor_scan(zz[:, 1], rad, zin[r % 2][:, 1], 0.0, ALU.mult, ALU.add).then_inc(scanned, 1)

            def turn_back(r):
                dve.wait_ge(scanned, r + 1)
                if r >= 2:
                    dve.wait_ge(y_done, r - 1)
                csr, bk = cs[r % 4], back[:, r % 2]
                v.tensor_tensor(bk[:, 0], csr, zz[:], ALU.mult)
                v.tensor_tensor(bk[:, 1, 0], csr[:, 0], zz[:, 1], ALU.mult)
                v.tensor_tensor(bk[:, 1, 1], csr[:, 1], zz[:, 0], ALU.mult).then_inc(prods, 1)

            def add_du(hf):
                dve.wait_ge(y_done, 16 * hf + 16)
                dve.wait_ge(u_scaled, 1)
                for t in range(TT):
                    dst = u_tok[:, t, hf * NB:(hf + 1) * NB]
                    ins = v.tensor_tensor(dst, tr[:, t], dst, ALU.add)
                ins.then_inc(ysum_ready, 1)

            def prepare_attention():
                dve.wait_ge(mix2_in, 16 * 12)
                link(v.tensor_copy(posf[:], posi[:]))
                for t in range(TT):
                    for f in range(8):
                        ins = v.tensor_scalar(ang[:, 2, t, f:f + 1], posf[:, t:t + 1], INV_FREQ[f], None, ALU.mult)
                link(ins)
                link(v.tensor_scalar(ang[:, 3], ang[:, 2], float(1 / TWO_PI), MAGIC, ALU.mult, ALU.add))
                link(v.tensor_scalar(ang[:, 3], ang[:, 3], MAGIC, None, ALU.subtract))
                for cst in (C1, C2, C3):
                    link(v.scalar_tensor_tensor(ang[:, 2].rearrange("p a b -> p (a b)"),
                                                ang[:, 3].rearrange("p a b -> p (a b)"), -cst,
                                                ang[:, 2].rearrange("p a b -> p (a b)"), ALU.mult, ALU.add))
                link(v.tensor_scalar(ang[:, 0], ang[:, 2], float(-1 / TWO_PI), None, ALU.mult))
                v.tensor_scalar(ang[:, 0], ang[:, 0], 0.5, -0.5, ALU.min, ALU.max).then_inc(ang_ready, 1)
                link(v.tensor_scalar(posi[:], posi[:], 6, None, ALU.arith_shift_right))
                link(v.tensor_scalar(posr[:], posr[:], 6, None, ALU.arith_shift_right))
                v.tensor_copy(chunk_c[:], posi[:])
                link(v.tensor_copy(chunk_r[:], posr[:]))
                for t in range(TT):
                    ins = v.tensor_scalar(early_mask[:, t], chunk_r[:], chunk_c[:, t:t + 1], NEG, ALU.is_gt, ALU.mult)
                link(ins)
                v.tensor_tensor(lamv[:, 0], lamv[:, 0], lamv[:, 1], ALU.mult)
                link(v.tensor_tensor(lamv[:, 2], lamv[:, 2], lamv[:, 3], ALU.mult))
                v.tensor_reduce(small[:, 0:1], lamv[:, 0], AX.X, ALU.add)
                v.tensor_reduce(small[:, 1:2], lamv[:, 2], AX.X, ALU.add).then_inc(lam_in, 1)
                dve.wait_ge(lam_ex, 1)
                link(v.tensor_tensor(small[:, 4:5], small[:, 3:4], small[:, 2:3], ALU.subtract))
                link(v.tensor_scalar(small[:, 4:5], small[:, 4:5], LAM_INIT, None, ALU.subtract))
                link(v.tensor_scalar(small[:, 16:17], cols[:, C_SUBLN:C_SUBLN + 1], 1.0 - LAM_INIT, None, ALU.mult))
                link(v.memset(small[:, 20:21], 0.0))

            for s in range(33):
                if s >= 4:
                    split_quad(Q_WIN + s, 0)
                if s == 8:
                    prepare_attention()
                if s == FIRST_STEP:
                    dve.wait_ge(trig_ready, 1)
                    for w in range(2):
                        for e, (fn, half) in enumerate(((0, 0), (1, 1), (1, 0), (0, 1))):
                            ins = v.tensor_tensor(rope_g[:, w, e], cs_pos[:, fn],
                                                  qkn[:, w, 8 * half:8 * half + 8].unsqueeze(1).to_broadcast([P, TT, 8]),
                                                  ALU.mult)
                    link(ins)
                    turn(0)
                    scan_input(0)
                for r in tile_steps(s - 1):
                    if r + 1 < NT:
                        turn(r + 1)
                    scan(r)
                    if r + 1 < NT:
                        scan_input(r + 1)
                    turn_back(r)
                    if r == 16:
                        add_du(0)
            add_du(1)
            split_quad(Q_GLU + 1, 0)

            ss = qk_ss[:].rearrange("p (w t h) -> p w t h", w=2, t=TT)

            def sum_squares(w):
                for t in range(TT):
                    dve.wait_ge(sq_ready, 2 * w + t + 1)
                    v.tensor_reduce(ss[:, w, t], sq[:, t].rearrange("p (h d) -> p h d", d=HD), AX.X, ALU.add)\
                        .then_inc(sq_read, 1)

            def rotate(w, tok):
                for t in range(TT):
                    rms[0] += 1
                    dve.wait_ge(rms_out, rms[0])
                    tv = tok[:, t].rearrange("p (h d) -> p h d", d=HD)
                    link(v.tensor_tensor(tv, tv, ss[:, w, t].unsqueeze(2).to_broadcast([P, 16, HD]), ALU.mult))
                    x1, x2 = tv[:, :, 0:8], tv[:, :, 8:16]
                    rt = [rope_t[:, i].rearrange("p (h d) -> p h d", d=8) for i in range(4)]
                    for e, xe in enumerate((x1, x2, x1, x2)):
                        tab = rope_g[:, w, e, t].unsqueeze(1).to_broadcast([P, 16, 8])
                        ins = v.tensor_tensor(rt[e], xe, tab, ALU.mult)
                    link(ins)
                    v.tensor_tensor(x1, rt[0], rt[1], ALU.subtract)
                    ins = v.tensor_tensor(x2, rt[2], rt[3], ALU.add)
                    if t == 0:
                        link(ins)
                ins.then_inc(qk_ready, 1)

            sum_squares(0)
            for m in range(4):
                lo_plain(T_YG + m, yt_hi[:, 2 * m:2 * m + 2].rearrange("p k t -> p (k t)"),
                         yt_lo[:, 2 * m:2 * m + 2].rearrange("p k t -> p (k t)"))
            sum_squares(1)
            split_quad(Q_GLU + 2, 0)
            rotate(0, q_tok)
            split_quad(Q_GLU + 3, 0)
            dve.wait_ge(job_read[1], J_WIN + 4)
            rotate(1, k_tok)

            def glu_sum(j):
                dve.wait_ge(quads_used, Q_GLU + 4)
                for t in range(TT):
                    ins = v.tensor_tensor(gsig[j][:, t], pairs[j][:, t], bglu_b[:, j * NB:(j + 1) * NB], ALU.add)
                ins.then_inc(job_read[j], 1)

            def glu_gate(j):
                dve.wait_ge(sig_ready, j + 1)
                yv = u_tok[:, :, j * NB:(j + 1) * NB]
                v.tensor_tensor(yv, yv, gsig[j][:], ALU.mult).then_inc(y2_ready, 1)

            dve.wait_ge(mix2_in, 16 * 13)
            glu_sum(0)
            glu_sum(1)
            glu_gate(0)

            def maxima(i):
                st = stat(i)
                dve.wait_ge(sc_ready, i + 1)
                if i >= 2:
                    dve.wait_ge(p_ready, i - 1)
                for cc in range(2):
                    ins = v.scalar_tensor_tensor(sm[:, i % 2, cc], misc[:, i % 2, cc * T:(cc + 1) * T], HD ** -0.5,
                                                 mask[:, i % 2], ALU.mult, ALU.add)
                ins.then_inc(sc_read, 1)
                dve.wait_ge(sc_read, i + 1)
                link(v.tensor_reduce(st[:, 6:8], sm[:, i % 2], AX.X, ALU.max))
                v.tensor_scalar(st[:, 0:2], st[:, 6:8], -1.0, None, ALU.mult).then_inc(mx_ready, 1)

            def weights(i):
                st = stat(i)
                dve.wait_ge(p_ready, i + 1)
                link(v.reciprocal(st[:, 4:6], st[:, 2:4]))
                if i >= 2:
                    dve.wait_ge(wt_ready, i - 1)
                link(v.tensor_tensor(st[:, 5:6], st[:, 5:6], small[:, 4:5], ALU.mult))
                link(v.tensor_scalar(aw[:, i % 2], pr[:, i % 2, 0], st[:, 4:5], None, ALU.mult))
                v.scalar_tensor_tensor(aw[:, i % 2], pr[:, i % 2, 1], st[:, 5:6], aw[:, i % 2], ALU.mult, ALU.add)\
                    .then_inc(a_ready, 1)

            def y_lo(m):
                lo_scaled(T_Y2 + m, m, h_hi, h_lo, 8, lambda k: cols[:, C_OUTN + k:C_OUTN + k + 1],
                          lambda k: small[:, 20:21], ev_tmp)

            glu_gate(1)
            dve.wait_ge(mask_moved, 1)
            maxima(0)
            y_norm()
            maxima(1)
            y_lo(0)
            y_lo(1)
            weights(0)
            maxima(2)
            split_quad(Q_OUT, 0)
            weights(1)

            def out_sum(n, used):
                first = used <= 8
                add_x(n % 2, J_OUT + n // 2 + (0 if first else 2), Q_OUT + used, n, 8 if first else None)

            for s in range(8):
                steps = attention_steps(s)
                if steps:
                    weights(steps[0])
                    maxima(steps[1])
                split_quad(Q_OUT + s + 1, 0)
                if steps:
                    weights(steps[1])
                    if steps[1] + 1 < 2 * HEADS:
                        maxima(steps[1] + 1)
                if s == 0:
                    y_lo(2)
                    y_lo(3)
                if s in (3, 4, 6):
                    out_sum(*{3: (0, 3), 4: (1, 4), 6: (2, 6)}[s])
            rms[0] += 1
            dve.wait_ge(rms_out, rms[0])
            for t in range(TT):
                av = ao[:, t].rearrange("p (h d) -> p h d", d=P)
                ins = v.tensor_tensor(av, av, small[:, 32 + 8 * t:40 + 8 * t].unsqueeze(2).to_broadcast([P, 8, P]),
                                      ALU.mult)
            ins.then_inc(ao_ready, 1)
            out_sum(3, 8)
            for m in range(4):
                lo_scaled(T_AO + m, m, h_hi, h_lo, 0, lambda k: small[:, 16:17], lambda k: small[:, 20:21], ev_tmp)
            for s in range(9, 16):
                split_quad(Q_OUT + s, 0)
                if s % 2 == 0:
                    out_sum(s // 2 - 5, s)
            out_sum(3, 16)
            coefficients(2, C_N3)
            split_quad(Q_FFN2, 0)
            h_norm()
            split_quad(Q_FFN2 + 1, 0)
            h_make(2, T_H3, Q_FFN2)
            ffn(2, Q_FFN2, J_FFN2, T_FFN2)

        @block.gpsimd
        def _(pool):
            g_ = nc.gpsimd
            chain = [0]
            h_sums = [0]
            rms = [0]

            def link(ins):
                chain[0] += 1
                ins.then_inc(pool_c, 1)
                pool.wait_ge(pool_c, chain[0])

            def inv_rms(ready, n, dst, src, width):
                pool.wait_ge(ready, n)
                link(g_.tensor_scalar(dst, src, 1.0 / width, EPS, ALU.mult, ALU.add))
                g_.tensor_tensor(dst, dst, small[:, 64:64 + dst.shape[-1]], ALU.pow).then_inc(rms_out, 1)

            def h_norm(n):
                pool.wait_ge(ssum, n)
                link(g_.tensor_tensor(ssq4[:, 0:2], ssq4[:, 0:2], ssq4[:, 2:4], ALU.add))
                g_.tensor_tensor(rstd[:], ssq4[:, 0], ssq4[:, 1], ALU.add).then_inc(sq_added, 1)
                h_sums[0] += 1
                inv_rms(sq_added, h_sums[0], rstd[:], rstd[:], D)

            def gate_groups(sub, first=0, end=4):
                pool.wait_ge(gate_cols, sub + 1)
                for n in range(first, end):
                    gg = 4 * sub + n
                    if gg:
                        pool.wait_ge(gate_bcast, gg)
                    for j in range(4):
                        k = 4 * n + j
                        ins = g_.tensor_scalar(diag[:, j * P:(j + 1) * P], ident[:], gate_col[:, k:k + 1], None, ALU.mult)
                    ins.then_inc(gate_diag, 1)

            g_.memset(small[:, 64:96], -0.5)
            link(g_.memset(ident[:], 0.0))
            link(g_.affine_select(out=ident[:], in_=ident[:], compare_op=ALU.not_equal, fill=1.0, base=0,
                                  pattern=[[-1, P]], channel_multiplier=1))
            g_.memset(ones[:], 1.0).then_inc(const_ready, 1)
            g_.memset(bpad_re[:], 0.0).then_inc(b_pad, 1)
            g_.memset(bpad_im[:], 0.0).then_inc(b_pad, 1)
            g_.memset(c_re_t[:], 0.0)
            link(g_.memset(c_im_t[:], 0.0))
            g_.iota(iota_t[:], pattern=[[1, T]], base=0, channel_multiplier=0,
                    allow_small_or_imprecise_dtypes=True).then_inc(const_ready, 1)
            h_norm(8)
            gate_groups(0)
            h_norm(16)
            def phase(r):
                kp, xx, yy = parts[r % 2]
                if r >= 2:
                    pool.wait_ge(cs_ready, r - 1)
                pool.wait_ge(parts_ready, r + 1)
                link(g_.tensor_tensor(nf[:, r % 2], kp[:], xx[:], ALU.subtract))
                link(g_.tensor_tensor(nf[:, r % 2], nf[:, r % 2], yy[:], ALU.subtract))
                g_.tensor_scalar(nf[:, r % 2], nf[:, r % 2], 0.5, -0.5, ALU.min, ALU.max).then_inc(nf_ready, 1)

            phase(0)
            phase(1)
            pool.wait_ge(mix_in, 16)
            pool.wait_ge(tr_written, T_U + 4)
            for t in range(TT):
                ins = g_.tensor_tensor(u_tok[:, t], u_tok[:, t], dskip[:], ALU.mult)
            ins.then_inc(u_scaled, 1)
            phase(2)
            for r in range(NT):
                if r + 3 < NT:
                    phase(r + 3)
                bk = back[:, r % 2]
                pool.wait_ge(prods, r + 1)
                g_.tensor_tensor(bk[:, 0, 0], bk[:, 0, 0], bk[:, 0, 1], ALU.subtract)
                g_.tensor_tensor(bk[:, 1, 0], bk[:, 1, 0], bk[:, 1, 1], ALU.add).then_inc(s_ready, 1)
            pool.wait_ge(mask_moved, 1)
            gate_groups(1, 0, 1)
            for i in range(2 * TT):
                inv_rms(sq_read, i + 1, qk_ss[:, 16 * i:16 * i + 16], qk_ss[:, 16 * i:16 * i + 16], HD)
            gate_groups(1, 1, 4)
            for t in range(TT):
                inv_rms(ssum, 17 + t, rstd[:, t:t + 1], ssq[:, t:t + 1], SW)
            inv_rms(o_done, 2 * HEADS, small[:, 32:48], small[:, 32:48], P)
            h_norm(26)
            gate_groups(2)

        @block.tensor
        def _(pe):
            mm = nc.tensor.matmul

            def quad(q, di, hi, lo, k0, pair, start, stop, middle=None):
                halves = in_halves(q)
                if halves:
                    pe.wait_ge(split_a, q - Q_WIN + 1)
                else:
                    pe.wait_ge(split, q + 1 + di)
                r = q % 2
                for kk in range(4):
                    if kk == 2:
                        if halves:
                            last.then_inc(half_used, 1)
                        if middle:
                            middle()
                        if halves:
                            pe.wait_ge(split, q + 1)
                    for t in range(TT):
                        st, sp_ = start and kk == 0, stop and kk == 3
                        bank = pairs[pair][:, t]
                        lh, ll = hi[:, k0 + kk, t * P:(t + 1) * P], lo[:, k0 + kk, t * P:(t + 1) * P]
                        mm(bank, lh, w_hi[:, r, kk], start=st, stop=False)
                        mm(bank, lh, w_lo[:, r, kk], start=False, stop=False)
                        last = mm(bank, ll, w_hi[:, r, kk], start=False, stop=sp_)
                last.then_inc(quads_used, 1)

            def transposes(bank, dbank, b, src):
                if isinstance(dbank, int) and bank + dbank < 2:
                    pass
                else:
                    pe.wait_ge(tr_free, bank - 1 + dbank)
                for kk in range(2):
                    for t in range(TT):
                        last = nc.tensor.transpose(tr[:, b, kk * T + t * P:kk * T + (t + 1) * P], src(kk, t), ident[:])
                last.then_inc(tr_written, 1)

            def rows_to_cols(bank0, n, tok, xs_n, srcsem, first=0):
                pe.wait_ge(srcsem, xs_n)
                for m in range(first, n):
                    transposes(bank0 + m, 0, (bank0 + m) % 2,
                               lambda kk, t: tok[:, t, (2 * m + kk) * P:(2 * m + kk + 1) * P])

            def first_quad(b):
                if b >= 2:
                    pe.wait_ge(mod_saved, b - 1)
                pe.wait_ge(raw_landed[0], 16 * (b + 1))
                for kk in range(4):
                    for j in range(4):
                        last = mm(misc[:, b % 2, j:j + 1], raw[:, 0, kk, j * P:(j + 1) * P], cond[:, kk:kk + 1],
                                  start=(kk + j == 0), stop=False)
                last.then_inc(ada_pe, 1)

            def reduce_ada(b, db, buf):
                first = isinstance(db, int) and b < ADA_FIRST
                if not first:
                    pe.wait_ge(mod_saved, b + db)
                pe.wait_ge(ada_sum, b + 1 + db)
                for j in range(4):
                    last = mm(misc[:, b % 2 if first else 0, j:j + 1], acc[:, buf, 0, j * P:(j + 1) * P], ones[:, 0:1],
                              start=not first, stop=(j == 3 or not first))
                last.then_inc(cols_reduced, 1)

            def spread_gate(gg):
                pe.wait_ge(gate_diag, gg + 1)
                if gg:
                    pe.wait_ge(gate_saved, gg)
                mm(misc[:, 1], ones[:], diag[:], start=True, stop=True).then_inc(gate_bcast, 1)

            def ffn(layer, q0, j0, t0, xs_n):
                for t, (blk, n, qu, qd, jp, tb) in enumerate(thirds(q0, j0, t0)):
                    def hidden_t(m):
                        pe.wait_ge(job_read[1], jp + m + 1)
                        for b in range(2):
                            transposes(tb + b, 2 * m, b, lambda kk, tt: g[:, tt, (2 * b + kk) * P:(2 * b + kk + 1) * P])

                    def up(i):
                        peeled = isinstance(i, int)
                        for s in range(8):
                            if s % 4 == 0 and (jp or not peeled):
                                pe.wait_ge(job_read[s // 4], jp + i)
                            if t == 0 and peeled and s < 4:
                                pe.wait_ge(tr_free, t0 - 8 + 2 * s + 2)
                            quad(qu + s, 8 * i, h_hi, h_lo, 4 * (s % 4), s // 4, s % 4 == 0, s % 4 == 3)
                            if s == 0 and not peeled:
                                hidden_t(i - 1)
                            if t == 0 and peeled and s < 2:
                                rows_to_cols(t0 - 8, 6 + 2 * s, xs, xs_n, xs_ready, 4 + 2 * s)
                            for a in ada_done_up(layer, t, s, i):
                                reduce_ada(*a)
                    looped(pe, n, up)
                    for s in range(4 * n):
                        j, k = s // n, s % n
                        if k == 0:
                            pe.wait_ge(job_read[j % 2], jp + n + j // 2)
                            if t == 0:
                                spread_gate((0, 8)[layer - 1] + j)
                        if s == n - 1:
                            pe.wait_ge(tr_free, tb + 2 * n)
                        elif s == 0:
                            pe.wait_ge(tr_free, tb + 2 * n - 2)
                        quad(qd + s, 0, gt_hi, gt_lo, 4 * k, j % 2, k == 0, k == n - 1)
                        if s == 0:
                            hidden_t(n - 1)
                        for a in ada_done_down(layer, t, s):
                            reduce_ada(*a)

            pe.wait_ge(const_ready, 1)
            pe.wait_ge(small_in, SMALL_IN)
            pe.wait_ge(dt_spread, 1)
            for i, n in enumerate((96, 73, 128, 16)):
                if i >= 2:
                    pe.wait_ge(cols_saved, i - 1)
                nc.tensor.transpose(tr[:, i % 2, 0:n], rows[0:n, i], ident[0:n, 0:n]).then_inc(cols_t, 1)
            pe.wait_ge(cond_r, 1)
            first_quad(0)
            for b in range(ADA_FIRST):
                if b + 1 < ADA_FIRST:
                    first_quad(b + 1)
                reduce_ada(b, 0, b % 2)
                if b == 2:
                    pe.wait_ge(b_pad, 3)
                    for i in range(8):
                        pe.wait_ge(cols_saved, 4 + i - 1)
                        src = (bpad_re, bpad_im)[i // 4]
                        for kk in range(2):
                            m = 2 * (i % 4) + kk
                            last = nc.tensor.transpose(tr[:, i % 2, kk * P:(kk + 1) * P],
                                                       src[:, 4 * m:4 * m + 4].rearrange("p a b -> p (a b)"), ident[:])
                        last.then_inc(cols_t, 1)
                if b in (3, 4):
                    for i in (2 * b - 6, 2 * b - 5):
                        if i < 2:
                            pe.wait_ge(cols_saved, 12)
                        else:
                            pe.wait_ge(c_saved, i - 1)
                        for kk in range(4):
                            last = nc.tensor.transpose(tr[:, i % 2, kk * P:(kk + 1) * P],
                                                       (cnat_re, cnat_im)[i // 2][:, 4 * (i % 2) + kk], ident[:])
                        last.then_inc(cols_t, 1)
            pe.wait_ge(c_saved, 4)
            rows_to_cols(T_H1, 4, xs, 2, xs_ready)
            ffn(1, Q_FFN1, J_FFN1, T_FFN1, 4)
            rows_to_cols(T_H2, 4, xs, 6, xs_ready)
            def drive(r):
                if r >= 2:
                    pe.wait_ge(bu_read, r - 1)
                p0, k = 32 * (r % 4), r // 4
                for e, bt in enumerate((bt_re, bt_im)):
                    last = mm(misc[:, r % 2, e * T:(e + 1) * T], bt[p0:p0 + 32, k], ut[p0:p0 + 32, k],
                              start=True, stop=True, tile_position=(p0, 0))
                last.then_inc(bu_ready, 1)

            def read_out(r):
                if r == 16:
                    pe.wait_ge(ysum_ready, 1)
                pe.wait_ge(s_ready, r + 1)
                for t in range(TT):
                    for e, ct in enumerate((c_re_t, c_im_t)):
                        last = mm(tr[:, t, 32 * (r % 16):32 * (r % 16) + 32], back[:, r % 2, e, 0, t * P:(t + 1) * P],
                                  ct[:, r], start=(e == 0), stop=(e == 1))
                last.then_inc(y_done, 1)

            for s in range(32):
                j, k = s // 4, s % 4
                if k == 0:
                    pe.wait_ge(job_read[j % 2], J_WIN + j // 2)
                if j == 0:
                    pe.wait_ge(tr_free, T_H2 + 2 * k + 2)
                steps = list(tile_steps(s))

                def middle():
                    if steps:
                        if steps[0]:
                            read_out(steps[0] - 1)
                        if len(steps) > 1 and steps[1] + 2 < NT:
                            drive(steps[1] + 2)

                if steps and steps[0] + 2 < NT:
                    drive(steps[0] + 2)
                quad(Q_WIN + s, 0, h_hi, h_lo, 4 * k, j % 2, k == 0, k == 3, middle)
                if s < 2:
                    rows_to_cols(T_H2, 6 + 2 * s, xs, 8, xs_ready, 4 + 2 * s)
                if s == 8:
                    rows_to_cols(T_U, 4, u_tok, J_WIN + 1, job_read[1])
                    pe.wait_ge(tr_free, T_U + 4)
                    drive(0)
                    drive(1)
                if len(steps) > 1:
                    read_out(steps[0])
            read_out(NT - 1)
            rows_to_cols(T_YG, 4, u_tok, 2, yg_ready)
            for s in range(4):
                j, k = s // 2, s % 2
                if k == 0:
                    pe.wait_ge(job_read[j], J_GLU)
                if j == 0:
                    pe.wait_ge(tr_free, T_YG + 2 * k + 2)
                quad(Q_GLU + s, 0, yt_hi, yt_lo, 4 * k, j, k == 0, k == 1)
                if s < 3:
                    spread_gate(4 + s) if s < 2 else rows_to_cols(T_QK, 4, q_tok, 1, qk_ready)
            spread_gate(6)
            rows_to_cols(T_QK + 4, 4, k_tok, 2, qk_ready)
            spread_gate(7)
            pe.wait_ge(tr_free, T_QK + 8)

            def scores(i):
                h, t = i // 2, i % 2
                if i >= 2:
                    pe.wait_ge(sc_read, i - 1)
                for cc in range(2):
                    c0 = HD * cc
                    if cc:
                        pe.wait_ge(sc_half, i + 1)
                    mm(misc[:, i % 2, cc * T:(cc + 1) * T], qt[c0:c0 + HD, h, t * P:(t + 1) * P],
                       kt[c0:c0 + HD, h], start=True, stop=True, tile_position=(c0, 0))\
                        .then_inc((sc_half, sc_ready)[cc], 1)

            def heads_out(i):
                pe.wait_ge(at_ready, i + 1)
                for kk in range(2):
                    last = mm(tr[:, i % 2, T:T + P], at[:, i % 2, kk * P:(kk + 1) * P],
                              v_tok[:, kk, (i // 2) * P:(i // 2 + 1) * P], start=(kk == 0), stop=(kk == 1))
                last.then_inc(o_ready, 1)

            def attend(i):
                if i + 2 < 2 * HEADS:
                    scores(i + 2)
                pe.wait_ge(a_ready, i + 1)
                if i >= 2:
                    pe.wait_ge(o_done, i - 1)
                if i in (0, 4):
                    pe.wait_ge(tr_free, T_Y2 + (i or 2))
                for kk in range(2):
                    last = nc.tensor.transpose(tr[:, i % 2, kk * P:(kk + 1) * P], aw[:, i % 2, kk * P:(kk + 1) * P],
                                               ident[:])
                last.then_inc(wt_ready, 1)
                if i not in (0, 2, 4):
                    heads_out(i - 1)
                if i in (1, 3, 2 * HEADS - 1):
                    heads_out(i)

            def y_cols(first):
                if first:
                    pe.wait_ge(o_done, first + 2)
                rows_to_cols(T_Y2, first + 2, u_tok, 10, xs_ready, first)

            scores(0)
            pe.wait_ge(gate_saved, 8)
            scores(1)
            y_cols(0)
            attend(0)
            attend(1)
            for s in range(16):
                n, k = OUT_QUADS[s]
                if s in (0, 1, 4, 6) or s >= 8 and s % 2 == 0:
                    pe.wait_ge(job_read[n % 2], J_OUT + n // 2 + (2 if s >= 8 else 0))
                if s in (0, 2):
                    pe.wait_ge(tr_free, T_Y2 + s + 2)
                if s in (8, 9):
                    pe.wait_ge(tr_free, T_AO + 2 * (s - 8) + 2)
                steps = attention_steps(s)
                quad(Q_OUT + s, 0, h_hi, h_lo, 4 * k, n % 2, k % 2 == 0, k % 2 == 1,
                     (lambda: attend(steps[0])) if steps else None)
                if steps:
                    attend(steps[1])
                if s == 0:
                    y_cols(2)
                if s == 7:
                    pe.wait_ge(o_done, 2 * HEADS)
                    rows_to_cols(T_AO, 4, ao, 1, ao_ready)
            rows_to_cols(T_H3, 4, xs, 12, xs_ready)
            ffn(2, Q_FFN2, J_FFN2, T_FFN2, 14)


_INS = ["x", "c", "positions", "w_ada", "b_ada", "ffn1_norm", "ffn1_w1", "ffn1_w3", "ffn1_w2", "mix_norm", "w_in",
        "q_norm", "k_norm", "lambda_q1", "lambda_k1", "lambda_q2", "lambda_k2", "attn_subln", "ssm_a_re", "ssm_a_im",
        "ssm_log_dt", "ssm_b_re", "ssm_b_im", "ssm_c_re", "ssm_c_im", "ssm_d", "w_glu", "b_glu", "ssm_out_norm",
        "w_out", "ffn2_norm", "ffn2_w1", "ffn2_w3", "ffn2_w2"]


def kernel(**inputs):
    import numpy as _np
    import concourse.bacc as _bacc
    from concourse import mybir as _mybir
    from concourse.bass_utils import run_bass_kernel_spmd as _run

    nc = _bacc.Bacc("TRN2", target_bir_lowering=False, num_devices=1)
    arrays, args = {}, []
    for name in _INS:
        a = _np.ascontiguousarray(inputs[name])
        arrays[f"in_{name}"] = a
        args.append(nc.dram_tensor(f"in_{name}", a.shape, _mybir.dt.from_np(a.dtype), kind="ExternalInput").ap())
    args.append(nc.dram_tensor("out_x", (1, T, D), _mybir.dt.float32, kind="ExternalOutput").ap())
    build(nc, *args)
    r = _run(nc, [arrays], core_ids=[0])
    return r.results[0]["out_x"]
```
